# Optimizing a Trainium2 kernel written in Bass

```python
import jax
import jax.numpy as jnp
from jax import lax
import numpy as np

D_MODEL = 2048
BATCH = 1
SEQ = 256
DEPTH = 2

SB_HEADS = 8
SB_HEAD_DIM = 128
SB_WIDTH = SB_HEADS * SB_HEAD_DIM
GLA_HEADS = 4
GLA_KEY_DIM = 128
GLA_VAL_DIM = 256
GLA_KEY_WIDTH = GLA_HEADS * GLA_KEY_DIM
GLA_VAL_WIDTH = GLA_HEADS * GLA_VAL_DIM
GLA_GATE_RANK = 16
GLA_GATE_NORM = 16.0
GLA_CHUNK = 64
MLA_HEADS = 16
MLA_Q_RANK = 512
MLA_KV_RANK = 512
MLA_NOPE_DIM = 128
MLA_ROPE_DIM = 64
MLA_V_DIM = 128
MLA_WIDTH = MLA_HEADS * MLA_V_DIM
ROPE_THETA = 10000.0
Q_BLOCK = 128
NORM_EPS = 1e-6

EVEN_SIZES = (SB_WIDTH, SB_WIDTH, SB_WIDTH, SB_WIDTH,
              GLA_KEY_WIDTH, GLA_KEY_WIDTH, GLA_VAL_WIDTH, GLA_VAL_WIDTH, GLA_GATE_RANK)
EVEN_IN = sum(EVEN_SIZES)
EVEN_MIX = SB_WIDTH + GLA_VAL_WIDTH
ODD_SIZES = (MLA_Q_RANK, MLA_KV_RANK, MLA_ROPE_DIM, MLA_WIDTH)
ODD_IN = sum(ODD_SIZES)
N_EVEN = (DEPTH + 1) // 2
N_ODD = DEPTH // 2

kernel_name = 'hybrid_stickbreak_gla_mla_trunk'

def _split_points(sizes):
    return [int(v) for v in np.cumsum(sizes)[:-1]]

def rmsnorm(x, g):
    xf = x.astype(jnp.float32)
    y = xf * lax.rsqrt(jnp.mean(xf * xf, axis=-1, keepdims=True) + NORM_EPS)
    return (y * g.astype(jnp.float32)).astype(x.dtype)

def stick_breaking_attention(q, k, v):
    B, S, H, Dh = q.shape
    nb = S // Q_BLOCK
    scale = Dh ** -0.5
    qb = q.reshape(B, nb, Q_BLOCK, H, Dh).transpose(1, 0, 3, 2, 4)
    kh = k.transpose(0, 2, 1, 3)
    vh = v.transpose(0, 2, 1, 3)
    key_pos = jnp.arange(S)

    def block(args):
        q_blk, blk = args
        q_pos = blk * Q_BLOCK + jnp.arange(Q_BLOCK)
        z = jnp.einsum('bhqd,bhkd->bhqk', q_blk, kh).astype(jnp.float32) * scale
        mask = key_pos[None, :] < q_pos[:, None]
        log_stay = jnp.where(mask, jax.nn.log_sigmoid(-z), 0.0)
        later = lax.cumsum(log_stay, axis=3, reverse=True) - log_stay
        w = jnp.where(mask, jnp.exp(jax.nn.log_sigmoid(z) + later), 0.0)
        return jnp.einsum('bhqk,bhkd->bhqd', w.astype(vh.dtype), vh)

    o = lax.map(block, (qb, jnp.arange(nb)))
    return o.transpose(1, 0, 3, 2, 4).reshape(B, S, H * Dh)

def gla_chunked(q, k, v, log_f):
    B, S, H, Dk = q.shape
    Dv = v.shape[-1]
    C = GLA_CHUNK
    nc = S // C

    def to_chunks(t):
        return t.astype(jnp.float32).reshape(B, nc, C, H, t.shape[-1]).transpose(1, 0, 3, 2, 4)

    qc = to_chunks(q) * (Dk ** -0.5)
    kc, vc, gc = to_chunks(k), to_chunks(v), to_chunks(log_f)
    causal = jnp.tril(jnp.ones((C, C), dtype=bool))[None, None, :, :, None]

    def step(state, inp):
        q_c, k_c, v_c, g_c = inp
        b = jnp.cumsum(g_c, axis=2)
        o_inter = jnp.einsum('bhcd,bhde->bhce', q_c * jnp.exp(b), state)
        diff = b[:, :, :, None, :] - b[:, :, None, :, :]
        decay = jnp.where(causal, jnp.exp(jnp.minimum(diff, 0.0)), 0.0)
        att = jnp.einsum('bhijd,bhjd->bhij', q_c[:, :, :, None, :] * decay, k_c)
        o_intra = jnp.einsum('bhij,bhje->bhie', att, v_c)
        b_last = b[:, :, -1:, :]
        new_state = (jnp.exp(b_last[:, :, 0, :])[..., None] * state
                     + jnp.einsum('bhcd,bhce->bhde', k_c * jnp.exp(b_last - b), v_c))
        return new_state, o_inter + o_intra

    state0 = jnp.zeros((B, H, Dk, Dv), jnp.float32)
    _, o = lax.scan(step, state0, (qc, kc, vc, gc))
    return o.transpose(1, 0, 3, 2, 4).reshape(B, S, H, Dv)

def rope_tables(positions, dim):
    half = dim // 2
    inv = ROPE_THETA ** (-jnp.arange(half, dtype=jnp.float32) / half)
    ang = positions.astype(jnp.float32)[..., None] * inv
    return jnp.cos(ang), jnp.sin(ang)

def apply_rope(x, cos, sin):
    half = x.shape[-1] // 2
    x1, x2 = x[..., :half], x[..., half:]
    cos = cos.astype(x.dtype)
    sin = sin.astype(x.dtype)
    return jnp.concatenate([x1 * cos - x2 * sin, x2 * cos + x1 * sin], axis=-1)

def mla_attention(q_nope, q_rope, k_nope, k_rope, v):
    B, S, H, Dn = q_nope.shape
    Dr = q_rope.shape[-1]
    Dv = v.shape[-1]
    nb = S // Q_BLOCK
    scale = (Dn + Dr) ** -0.5
    qn = q_nope.reshape(B, nb, Q_BLOCK, H, Dn).transpose(1, 0, 3, 2, 4)
    qr = q_rope.reshape(B, nb, Q_BLOCK, H, Dr).transpose(1, 0, 3, 2, 4)
    kn = k_nope.transpose(0, 2, 1, 3)
    vh = v.transpose(0, 2, 1, 3)
    key_pos = jnp.arange(S)

    def block(args):
        qn_b, qr_b, blk = args
        q_pos = blk * Q_BLOCK + jnp.arange(Q_BLOCK)
        s = (jnp.einsum('bhqd,bhkd->bhqk', qn_b, kn)
             + jnp.einsum('bhqd,bkd->bhqk', qr_b, k_rope)).astype(jnp.float32) * scale
        s = jnp.where(key_pos[None, :] <= q_pos[:, None], s, -jnp.inf)
        p = jax.nn.softmax(s, axis=-1)
        return jnp.einsum('bhqk,bhkd->bhqd', p.astype(vh.dtype), vh)

    o = lax.map(block, (qn, qr, jnp.arange(nb)))
    return o.transpose(1, 0, 3, 2, 4).reshape(B, S, H * Dv)

def even_layer(x, norm_g, w_in, alpha_up, alpha_bias, gla_norm_g, w_out):
    B, S, _ = x.shape
    h = rmsnorm(x, norm_g)
    z = h @ w_in
    sb_q, sb_k, sb_v, sb_g, gq, gk, gv, gg, ga = jnp.split(z, _split_points(EVEN_SIZES), axis=-1)
    o_a = stick_breaking_attention(sb_q.reshape(B, S, SB_HEADS, SB_HEAD_DIM),
                                   sb_k.reshape(B, S, SB_HEADS, SB_HEAD_DIM),
                                   sb_v.reshape(B, S, SB_HEADS, SB_HEAD_DIM))
    y_a = o_a * jax.nn.silu(sb_g)
    log_f = jax.nn.log_sigmoid((ga @ alpha_up + alpha_bias).astype(jnp.float32)) / GLA_GATE_NORM
    o_b = gla_chunked(gq.reshape(B, S, GLA_HEADS, GLA_KEY_DIM),
                      gk.reshape(B, S, GLA_HEADS, GLA_KEY_DIM),
                      gv.reshape(B, S, GLA_HEADS, GLA_VAL_DIM),
                      log_f.reshape(B, S, GLA_HEADS, GLA_KEY_DIM))
    o_b = rmsnorm(o_b.astype(x.dtype), gla_norm_g).reshape(B, S, GLA_VAL_WIDTH)
    y_b = o_b * jax.nn.silu(gg)
    y = jnp.concatenate([y_a, y_b], axis=-1) @ w_out
    return x + y

def odd_layer(x, positions, norm_g, w_in, q_norm_g, w_q_up, kv_norm_g, w_kv_up, w_out):
    B, S, _ = x.shape
    h = rmsnorm(x, norm_g)
    q_lat, kv_lat, k_rope, gate = jnp.split(h @ w_in, _split_points(ODD_SIZES), axis=-1)
    cos, sin = rope_tables(positions, MLA_ROPE_DIM)
    q = (rmsnorm(q_lat, q_norm_g) @ w_q_up).reshape(B, S, MLA_HEADS, MLA_NOPE_DIM + MLA_ROPE_DIM)
    q_nope = q[..., :MLA_NOPE_DIM]
    q_rope = apply_rope(q[..., MLA_NOPE_DIM:], cos[:, :, None, :], sin[:, :, None, :])
    kv = (rmsnorm(kv_lat, kv_norm_g) @ w_kv_up).reshape(B, S, MLA_HEADS, MLA_NOPE_DIM + MLA_V_DIM)
    k_nope = kv[..., :MLA_NOPE_DIM]
    v = kv[..., MLA_NOPE_DIM:]
    k_rope = apply_rope(k_rope, cos, sin)
    o = mla_attention(q_nope, q_rope, k_nope, k_rope, v)
    y = (o * jax.nn.silu(gate)) @ w_out
    return x + y

def setup_inputs(seed: int = 0) -> dict:
    key = jax.random.key(seed)
    ks = jax.random.split(key, 20)
    f32 = jnp.float32

    def dense(k, shape, fan_in):
        return jax.random.normal(k, shape, f32) * (fan_in ** -0.5)

    def gain(k, shape):
        return 1.0 + 0.02 * jax.random.normal(k, shape, f32)

    x = jax.random.normal(ks[0], (BATCH, SEQ, D_MODEL), f32)
    offset = jax.random.randint(ks[1], (BATCH, 1), 0, 1024, dtype=jnp.int32)
    positions = jnp.arange(SEQ, dtype=jnp.int32)[None, :] + offset
    return {
        'x': x,
        'positions': positions,
        'ln_even': gain(ks[2], (N_EVEN, D_MODEL)),
        'w_in_even': dense(ks[3], (N_EVEN, D_MODEL, EVEN_IN), D_MODEL),
        'gla_alpha_up': dense(ks[4], (N_EVEN, GLA_GATE_RANK, GLA_KEY_WIDTH), GLA_GATE_RANK),
        'gla_alpha_bias': 0.1 * jax.random.normal(ks[5], (N_EVEN, GLA_KEY_WIDTH), f32),
        'gla_norm': gain(ks[6], (N_EVEN, GLA_VAL_DIM)),
        'w_out_even': dense(ks[7], (N_EVEN, EVEN_MIX, D_MODEL), EVEN_MIX),
        'ln_odd': gain(ks[8], (N_ODD, D_MODEL)),
        'w_in_odd': dense(ks[9], (N_ODD, D_MODEL, ODD_IN), D_MODEL),
        'q_norm': gain(ks[10], (N_ODD, MLA_Q_RANK)),
        'w_q_up': dense(ks[11], (N_ODD, MLA_Q_RANK, MLA_HEADS * (MLA_NOPE_DIM + MLA_ROPE_DIM)), MLA_Q_RANK),
        'kv_norm': gain(ks[12], (N_ODD, MLA_KV_RANK)),
        'w_kv_up': dense(ks[13], (N_ODD, MLA_KV_RANK, MLA_HEADS * (MLA_NOPE_DIM + MLA_V_DIM)), MLA_KV_RANK),
        'w_out_odd': dense(ks[14], (N_ODD, MLA_WIDTH, D_MODEL), MLA_WIDTH),
        'final_norm': gain(ks[15], (D_MODEL,)),
    }

def reference(x, positions, ln_even, w_in_even, gla_alpha_up, gla_alpha_bias, gla_norm, w_out_even,
              ln_odd, w_in_odd, q_norm, w_q_up, kv_norm, w_kv_up, w_out_odd, final_norm):
    for layer in range(DEPTH):
        i = layer // 2
        if layer % 2 == 0:
            x = even_layer(x, ln_even[i], w_in_even[i], gla_alpha_up[i], gla_alpha_bias[i],
                           gla_norm[i], w_out_even[i])
        else:
            x = odd_layer(x, positions, ln_odd[i], w_in_odd[i], q_norm[i], w_q_up[i],
                          kv_norm[i], w_kv_up[i], w_out_odd[i])
    return rmsnorm(x, final_norm)


_drawn_inputs = setup_inputs


def setup_inputs(seed=0):
    import zlib

    import numpy as np

    out = dict(_drawn_inputs(seed))
    spreads = {}
    factors = {'ln_even': 3.121,
     'gla_alpha_bias': 3.44,
     'gla_norm': 7.119,
     'ln_odd': 8.0,
     'q_norm': 8.0,
     'kv_norm': 8.0,
     'final_norm': 2.743}
    for name, (base, spread) in spreads.items():
        noise = np.random.default_rng([zlib.crc32(name.encode()), seed]).standard_normal(out[name].shape)
        drawn = base * np.exp(spread * noise) if base else spread * noise
        out[name] = jnp.asarray(drawn.astype(out[name].dtype))
    for name, factor in factors.items():
        out[name] = (out[name] * factor).astype(out[name].dtype)
    return out
```

```python
from contextlib import ExitStack

import numpy as np

import concourse.bass as bass
from concourse import mybir
from concourse.alu_op_type import AluOpType as ALU

ACT = mybir.ActivationFunctionType
F32 = mybir.dt.float32
F32R = mybir.dt.float32r
I32 = mybir.dt.int32

P = 128
D = 2048
T = 2
KT = D // P
CW = 512
PK = 2
NP = KT // PK
RAW = 8
RING = 4
SBH, GH, MH = 8, 4, 16
DH = 128
GV = 256
GR = 16
ROPE = 64
QH = DH + ROPE
LAT = 512
PAIRS = MH // 2
EPS = 1e-6
SB_SCALE = float(DH) ** -0.5
MLA_SCALE = float(QH) ** -0.5
NEG = -1e30
ABS = 0x7FFFFFFF
THETA = 10000.0
TWO_PI = 2 * np.pi
C1 = 6.28125
C2 = float(np.float32(TWO_PI - C1))
C3 = float(np.float32(TWO_PI - C1 - C2))
MAGIC = 12582912.0
INV_FREQ = [float(v) for v in (np.float32(THETA) ** (-np.arange(ROPE // 2, dtype=np.float32) / np.float32(ROPE // 2)))]

SB_Q, SB_V, G_QK, G_V, G_A = 0, 2048, 4096, 5120, 7168
O_KR, O_GATE = 2 * LAT, 2 * LAT + ROPE

B_GQK, B_SBQK, B_SBV, B_SBG, B_GV, B_GG, B_OUT0 = 0, 2, 6, 8, 10, 12, 14
B_LAT, B_GATE, B_MLA, B_OUT1, B_END = 18, 20, 24, 28, 32
C_MLA = 24
C_OUT1 = C_MLA + 2 * PAIRS
U_PREP0, U_QK, U_PREPY, U_PREP1, U_LAT, U_MLA = 0, 4, 10, 14, 18, 20
U_PREPZ = U_MLA + 2 * PAIRS


def freed(u):
    n = 0
    for first, last, each in ((U_PREP0, U_QK, 2), (U_QK, U_PREPY, 1), (U_PREPY, U_MLA, 2), (U_MLA, U_PREPZ, 1), (U_PREPZ, 999, 2)):
        n += each * max(0, min(u, last) - first)
    return n


def pieces_through(c, part="full"):
    if part == "full":
        return c * NP + NP
    if part == "up":
        return c * 2 + (NP * B_MLA - 2 * C_MLA + 2)
    return c * NP + (NP * (B_OUT1 - C_OUT1) + NP)


def build(nc, x, positions, ln_even, w_in_even, gla_alpha_up, gla_alpha_bias, gla_norm, w_out_even,
          ln_odd, w_in_odd, q_norm, w_q_up, kv_norm, w_kv_up, w_out_odd, final_norm, out):
    x_d = x[0].rearrange("(t p) d -> t p d", p=P)
    out_d = out[0].rearrange("(t p) d -> t p d", p=P)

    def by_k(w):
        return w[0].rearrange("(k p) n -> p k n", p=P)

    we_d, wo0_d, wi1_d, wo1_d = by_k(w_in_even), by_k(w_out_even), by_k(w_in_odd), by_k(w_out_odd)
    wq_d, wkv_d = by_k(w_q_up), by_k(w_kv_up)

    with ExitStack() as ctx:
        def sb(name, shape, dt=F32):
            return ctx.enter_context(nc.sbuf_tensor(name, shape, dt))

        def sem(name):
            return ctx.enter_context(nc.semaphore(name))

        ps = ctx.enter_context(nc.psum_tensor("ps", [P, 8, CW], F32))

        raw = sb("raw", [P, RAW, PK * CW])
        w_hi = sb("w_hi", [P, RING, PK * CW], F32R)
        w_lo = sb("w_lo", [P, RING, PK * CW], F32R)
        n_hi = sb("n_hi", [P, KT, ROPE], F32R)
        n_lo = sb("n_lo", [P, KT, ROPE], F32R)
        a_hi = sb("a_hi", [P, KT, T * P], F32R)
        a_lo = sb("a_lo", [P, KT, T * P], F32R)
        xs = sb("xs", [P, T, D])
        ys = sb("ys", [P, T, D])
        even = sb("even", [P, 10240])
        work = sb("work", [P, 2048 + 3584])

        qk_t = even[:, 0:4096].rearrange("p (h q) -> p h q", h=2 * SBH)
        gqk_t = even[:, 4096:6144].rearrange("p (h q) -> p h q", h=2 * GH)
        sb_v = even[:, 6144:8192].rearrange("p (t n) -> p t n", t=T)
        g_v = even[:, 8192:10240].rearrange("p (t n) -> p t n", t=T)
        na_raw = even[:, 8192:8192 + KT * GR].rearrange("p (k n) -> p k n", k=KT)
        lat = even[:, 0:2048].rearrange("p (t n) -> p t n", t=T)
        kr_raw = even[:, 2048:3072].rearrange("p (k n) -> p k n", k=KT)
        fin_g = even[:, 3072:5120]
        q_tok = even[:, 5120:5888].rearrange("p (t n) -> p t n", t=T)
        qn_t = even[:, 5888:6400]
        kn_t = even[:, 6400:6912]
        qr_t = even[:, 6912:7424]
        kv_tok = [even[:, 7424 + 1024 * i:8448 + 1024 * i].rearrange("p (t n) -> p t n", t=T) for i in range(2)]
        p_t = even[:, 9472:10240].rearrange("p (h q) -> p h q", h=2)
        stg = [work[:, 1024 * i:1024 * i + 1024].rearrange("p (t n) -> p t n", t=T) for i in range(2)]
        junk = work[:, 0:2048]
        g_qd, g_kd = work[:, 0:1024], work[:, 1024:2048]
        g_b = work[:, 2048:3072]
        g_u = work[:, 3072:4096]
        att = work[:, 4096:5120]
        att_x = work[:, 5120:5632]
        g_bias = work[:, 4096:4608]
        g_alpha = work[0:GR, 4608:5120]
        g_e2 = g_b
        sa = [work[:, 2048 + 768 * i:2432 + 768 * i] for i in range(2)]
        sp_ = [work[:, 2432 + 768 * i:2816 + 768 * i] for i in range(2)]
        s_m = [work[:, 2048 + 384 * i:2432 + 384 * i] for i in range(2)]
        rope_m1 = work[:, 3072:3328]
        rope_m2 = work[:, 3328:3584]
        kr_t = work[0:ROPE, 3584:3840]
        kr_tok = work[:, 3840:3968].rearrange("p (t n) -> p t n", t=T)

        ident = sb("ident", [P, P])
        tri16 = sb("tri16", [P, P])
        neg_tri = sb("neg_tri", [P, P])
        neg_one = sb("neg_one", [P, P])
        masks = sb("masks", [P, 6, P])
        causal = sb("causal", [P, 2 * P])
        gla_g = sb("gla_g", [P, GV])
        gain_rows = work[0:40, 0:P]
        gain_t = sb("gain_t", [P, 40])
        pos_i = sb("pos_i", [P, T], I32)
        pos_f = sb("pos_f", [P, T])
        ang, red, turn = (work[:, 5120 + 128 * i:5248 + 128 * i].rearrange("p (a t c) -> p a t c", a=2, t=T) for i in range(3))
        inv_f = work[:, 5504:5504 + ROPE // 2]
        cos_ = sb("cos_", [P, T, 2, ROPE // 2])
        sin_ = sb("sin_", [P, T, 2, ROPE // 2])
        half = sb("half", [P, 8])
        ssum = sb("ssum", [P, 24])
        rstd = sb("rstd", [P, 24])
        ga_tok = sb("ga_tok", [P, T, GR])
        ga_t = work[0:GR, 2048:2048 + T * P]
        idle = sb("idle", [P, 2])
        mx = sb("mx", [P, 4])
        nmx = sb("nmx", [P, 4])
        rsum = sb("rsum", [P, 4])
        rinv = sb("rinv", [P, 4])

        x_landed = [sem(f"x_landed{t}") for t in range(T)]
        gains_landed, bias_landed, alpha_landed, gla_g_landed = (sem(n) for n in ("gains_landed", "bias_landed", "alpha_landed", "gla_g_landed"))
        pos_landed, na_landed, kr_landed, fin_landed = (sem(n) for n in ("pos_landed", "na_landed", "kr_landed", "fin_landed"))
        raw_landed = [sem(f"raw_landed{s}") for s in range(RAW)]
        hi_ready, lo_ready, piece_used = sem("hi_ready"), sem("lo_ready"), sem("piece_used")
        n_hi_ready, n_lo_ready = sem("n_hi_ready"), sem("n_lo_ready")
        evac_a, evac_d = sem("evac_a"), sem("evac_d")
        t_done, t_free_a, t_free_d = sem("t_done"), sem("t_free_a"), sem("t_free_d")
        consts, pool_seq = sem("consts"), sem("pool_seq")
        gain_done, gain_ready = sem("gain_done"), sem("gain_ready")
        sq_ready, ms_ready, rstd_ready = sem("sq_ready"), sem("ms_ready"), sem("rstd_ready")
        silu_ready = sem("silu_ready")
        gd_init = sem("gd_init")
        res_added = sem("res_added")
        ga_done, ga_ready, gat_done, gat_ready, u_done, u_ready = (sem(n) for n in ("ga_done", "ga_ready", "gat_done", "gat_ready", "u_done", "u_ready"))
        ua_ready, ue_ready, g_ready, b_done, b_ready = (sem(n) for n in ("ua_ready", "ue_ready", "g_ready", "b_done", "b_ready"))
        gd_ready, ge_ready, gq_ready, lev_done, lev_copied = (sem(n) for n in ("gd_ready", "ge_ready", "gq_ready", "lev_done", "lev_copied"))
        att_ready, go_done, go_sq, gy_ready, gg_ready = (sem(n) for n in ("att_ready", "go_done", "go_sq", "gy_ready", "gg_ready"))
        sz_done, sabs_ready, sexp_ready, slog_ready, ssp_ready, ssel_ready = (sem(n) for n in ("sz_done", "sabs_ready", "sexp_ready", "slog_ready", "ssp_ready", "ssel_ready"))
        sarg_done, sw_ready, swm_ready, sy_done, sy_ready = (sem(n) for n in ("sarg_done", "sw_ready", "swm_ready", "sy_done", "sy_ready"))
        ang_ready, trig_ready, rope_tab = sem("ang_ready"), sem("trig_ready"), sem("rope_tab")
        kr_done, kr_evac, kr_roped, krt_done, krt_ready = (sem(n) for n in ("kr_done", "kr_evac", "kr_roped", "krt_done", "krt_ready"))
        rope_seq, q_roped, qrt_done, qrt_ready = (sem(n) for n in ("rope_seq", "q_roped", "qrt_done", "qrt_ready"))
        sc_done, sc_max, nmx_ready, p_ready, rinv_ready, my_done, my_ready = (
            sem(n) for n in ("sc_done", "sc_max", "nmx_ready", "p_ready", "rinv_ready", "my_done", "my_ready"))
        fin_seq, fin_ready, out_written = sem("fin_seq"), sem("fin_ready"), sem("out_written")

        block = ctx.enter_context(nc.Block())

        @block.sync
        def _(sp):
            def load(dst, src, slot):
                sp.dma_start(dst, src).then_inc(raw_landed[slot], 16)

            def block_of(w, col, b, free=True):
                for j in range(NP):
                    if free:
                        sp.wait_ge(lo_ready, b * 8 + (j + 1 - RAW))
                    dst = raw[:, j, :].rearrange("p (k n) -> p k n", k=PK)
                    load(dst, w[:, PK * j:PK * j + PK, bass.ds(col, CW)], j)

            sp.dma_start(gain_rows[0:16, :], ln_even[0].rearrange("(k p) -> k p", p=P)).then_inc(gains_landed, 16)
            sp.dma_start(gain_rows[16:32, :], ln_odd[0].rearrange("(k p) -> k p", p=P)).then_inc(gains_landed, 16)
            sp.dma_start(gain_rows[32:36, :], q_norm[0].rearrange("(k p) -> k p", p=P)).then_inc(gains_landed, 16)
            sp.dma_start(gain_rows[36:40, :], kv_norm[0].rearrange("(k p) -> k p", p=P)).then_inc(gains_landed, 16)
            block_of(we_d, G_QK, 0, free=False)
            sp.dma_start(na_raw, we_d[:, :, G_A:G_A + GR]).then_inc(na_landed, 16)
            sp.dma_start(g_bias, gla_alpha_bias.to_broadcast([P, GH * DH])).then_inc(bias_landed, 16)
            sp.dma_start(g_alpha, gla_alpha_up[0]).then_inc(alpha_landed, 16)
            sp.dma_start(gla_g[:, :], gla_norm.to_broadcast([P, GV])).then_inc(gla_g_landed, 16)
            for t in range(T):
                sp.dma_start(pos_i[:, t:t + 1], positions[0, P * t:P * t + P].rearrange("(p a) -> p a", a=1)).then_inc(pos_landed, 16)
            block_of(we_d, G_QK + CW, 1)
            with sp.Fori(0, 4) as i:
                block_of(we_d, i * CW + SB_Q, i + B_SBQK)
            with sp.Fori(0, 4) as i:
                block_of(we_d, i * CW + SB_V, i + B_SBV)
            with sp.Fori(0, 4) as i:
                block_of(we_d, i * CW + G_V, i + B_GV)
            with sp.Fori(0, 4) as i:
                block_of(wo0_d, i * CW, i + B_OUT0)
            sp.wait_ge(sy_ready, SBH)
            sp.dma_start(kr_raw, wi1_d[:, :, O_KR:O_KR + ROPE]).then_inc(kr_landed, 16)
            sp.dma_start(fin_g, final_norm.rearrange("(a d) -> a d", a=1).to_broadcast([P, D])).then_inc(fin_landed, 16)
            with sp.Fori(0, 2) as i:
                block_of(wi1_d, i * CW, i + B_LAT)
            with sp.Fori(0, 4) as i:
                block_of(wi1_d, i * CW + O_GATE, i + B_GATE)
            with sp.Fori(0, PAIRS // 2) as i:
                for e in range(2):
                    for j in range(4):
                        slot = 4 * e + j
                        sp.wait_ge(lo_ready, i * 8 + (8 * B_MLA + slot + 1 - RAW))
                        w, n = (wq_d, 2 * QH) if j < 2 else (wkv_d, CW)
                        k = PK * (j % 2)
                        dst = raw[:, slot, 0:PK * n].rearrange("p (k n) -> p k n", k=PK)
                        load(dst, w[:, k:k + PK, bass.ds(i * (2 * n) + e * n, n)], slot)
            with sp.Fori(0, 4) as i:
                block_of(wo1_d, i * CW, i + B_OUT1)
            for t in range(T):
                sp.wait_ge(fin_ready, t + 1)
                sp.dma_start(out_d[t], xs[:, t, :]).then_inc(out_written, 16)
            sp.wait_ge(out_written, 16 * T)

        @block.gpsimd
        def _(pool):
            g = nc.gpsimd
            seq = [0]

            def step(ins):
                seq[0] += 1
                ins.then_inc(pool_seq, 1)
                pool.wait_ge(pool_seq, seq[0])

            g.memset(ident[:, :], 0.0).then_inc(pool_seq, 1)
            g.memset(tri16[:, :], 1.0 / 16.0).then_inc(pool_seq, 1)
            g.memset(neg_tri[:, :], -1.0).then_inc(pool_seq, 1)
            g.memset(neg_one[:, :], -1.0).then_inc(pool_seq, 1)
            g.memset(masks[:, :, :], 1.0).then_inc(pool_seq, 1)
            g.memset(causal[:, :], 0.0).then_inc(pool_seq, 1)
            g.memset(half[:, :], -0.5).then_inc(pool_seq, 1)
            seq[0] = 7
            pool.wait_ge(pool_seq, seq[0])
            g.affine_select(out=ident[:, :], in_=ident[:, :], compare_op=ALU.not_equal, fill=1.0,
                            base=0, pattern=[[-1, P]], channel_multiplier=1).then_inc(consts, 1)
            g.affine_select(out=tri16[:, :], in_=tri16[:, :], compare_op=ALU.is_ge, fill=0.0,
                            base=0, pattern=[[1, P]], channel_multiplier=-1).then_inc(consts, 1)
            g.affine_select(out=neg_tri[:, :], in_=neg_tri[:, :], compare_op=ALU.is_ge, fill=0.0,
                            base=0, pattern=[[-1, P]], channel_multiplier=1).then_inc(consts, 1)
            g.affine_select(out=causal[:, P:2 * P], in_=causal[:, P:2 * P], compare_op=ALU.is_ge, fill=NEG,
                            base=0, pattern=[[-1, P]], channel_multiplier=1).then_inc(consts, 1)
            for m in range(6):
                s = 64 >> m
                v = masks[:, m, :].rearrange("p (b s) -> p b s", s=s)
                step(g.affine_select(out=v, in_=v, compare_op=ALU.is_ge, fill=0.0, base=0,
                                     pattern=[[-s, P // s], [0, s]], channel_multiplier=1))
                g.affine_select(out=v, in_=v, compare_op=ALU.is_ge, fill=0.0, base=s - 1,
                                pattern=[[s, P // s], [0, s]], channel_multiplier=-1).then_inc(consts, 1)
            ms = [0]

            def inverse_root(a, b, width, count):
                pool.wait_ge(sq_ready, count)
                ms[0] += 1
                g.tensor_scalar(ssum[:, a:b], ssum[:, a:b], 1.0 / width, EPS, ALU.mult, ALU.add).then_inc(ms_ready, 1)
                pool.wait_ge(ms_ready, ms[0])
                g.tensor_tensor(rstd[:, a:b], ssum[:, a:b], half[:, 0:b - a], ALU.pow).then_inc(rstd_ready, 1)

            inverse_root(0, 2, D, 2)
            for j, v in enumerate(INV_FREQ):
                ins = g.memset(inv_f[:, j:j + 1], v)
            step(ins)
            pool.wait_ge(pos_landed, 16 * T)
            step(g.tensor_copy(pos_f[:, :], pos_i[:, :]))
            for t in range(T):
                step(g.tensor_scalar(ang[:, 0, t, :], inv_f[:, :], pos_f[:, t:t + 1], None, ALU.mult))
                step(g.tensor_copy(ang[:, 1, t, :], ang[:, 0, t, :]))
            step(g.tensor_scalar(red[:, 0, :, :], ang[:, 0, :, :], 1.0 / TWO_PI, 0.0, ALU.mult, ALU.add))
            step(g.tensor_scalar(red[:, 1, :, :], ang[:, 1, :, :], 1.0 / TWO_PI, 0.25, ALU.mult, ALU.add))
            step(g.tensor_scalar(red[:, :, :, :], red[:, :, :, :], MAGIC, None, ALU.add))
            step(g.tensor_scalar(red[:, :, :, :], red[:, :, :, :], -MAGIC, None, ALU.add))
            for c in (C1, C2, C3):
                step(g.tensor_scalar(turn, red[:, :, :, :], c, None, ALU.mult))
                step(g.tensor_tensor(ang[:, :, :, :], ang[:, :, :, :], turn, ALU.subtract))
            step(g.tensor_scalar(ang[:, 1, :, :], ang[:, 1, :, :], np.pi / 2, None, ALU.add))
            step(g.tensor_scalar(ang[:, :, :, :], ang[:, :, :, :], 3.1415925, -3.1415925, ALU.min, ALU.max))
            pool.sem_inc(ang_ready, 1)
            pool.wait_ge(trig_ready, 2)
            step(g.tensor_copy(cos_[:, :, 1, :], cos_[:, :, 0, :]))
            step(g.tensor_scalar(sin_[:, :, 0, :], sin_[:, :, 1, :], -1.0, None, ALU.mult))
            pool.sem_inc(rope_tab, 1)

            pool.wait_ge(gla_g_landed, 16)
            pool.wait_ge(silu_ready, 4)
            pool.wait_ge(evac_a, 14)
            for t in range(T):
                v = ys[:, t, SBH * DH:].rearrange("p (h e) -> p h e", h=GH)
                g.tensor_tensor(v, v, gla_g[:, :].unsqueeze(1).to_broadcast([P, GH, GV]), ALU.mult).then_inc(gg_ready, 1)
            pool.wait_ge(lev_copied, 17)
            v = att.rearrange("p (a q) -> p a q", q=P)
            g.affine_select(out=v, in_=v, compare_op=ALU.is_ge, fill=0.0, base=0,
                            pattern=[[0, T * GH], [1, P]], channel_multiplier=-1).then_inc(att_ready, 1)
            inverse_root(16, 24, GV, 2 + 8)
            def strictly_before(buf, signal):
                v = buf.rearrange("p (a q) -> p a q", q=P)[:, 0:3:2, :]
                g.affine_select(out=v, in_=v, compare_op=ALU.is_gt, fill=0.0, base=0,
                                pattern=[[0, 2], [1, P]], channel_multiplier=-1).then_inc(signal, 1)

            for h0 in range(0, SBH, 2):
                for h in (h0, h0 + 1):
                    pool.wait_ge(ssp_ready, h + 1)
                    strictly_before(sp_[h % 2], ssel_ready)
                for h in (h0, h0 + 1):
                    pool.wait_ge(sw_ready, h + 1)
                    strictly_before(sa[h % 2], swm_ready)

            def add_residual(c0):
                with pool.Fori(0, 2) as i:
                    for par in range(2):
                        pool.wait_ge(evac_a, i * 2 + (c0 + par + 1))
                        dst = xs[:, 0, bass.ds(i * (2 * CW) + par * CW, CW)]
                        g.tensor_tensor(dst, dst, stg[par][:, 0, :], ALU.add).then_inc(res_added, 1)

            pool.sem_inc(res_added, 1)
            add_residual(14)
            inverse_root(2, 4, D, 12)
            pool.wait_ge(kr_evac, 2)
            rs = [0]

            def rotate(xv, m1, m2, last):
                c = cos_[:, :, :, :].rearrange("p t a c -> p t (a c)")
                h2 = ROPE // 2
                g.tensor_tensor(m1, xv, c, ALU.mult)
                g.tensor_tensor(m2[:, :, 0:h2], xv[:, :, h2:], sin_[:, :, 0, :], ALU.mult)
                g.tensor_tensor(m2[:, :, h2:], xv[:, :, 0:h2], sin_[:, :, 1, :], ALU.mult).then_inc(rope_seq, 1)
                return lambda: g.tensor_tensor(xv, m1, m2, ALU.add).then_inc(last, 1)

            mm = [(rope_m1[:, 128 * i:128 * i + 128].rearrange("p (t n) -> p t n", t=T),
                   rope_m2[:, 128 * i:128 * i + 128].rearrange("p (t n) -> p t n", t=T)) for i in range(2)]
            end = rotate(kr_tok, *mm[0], kr_roped)
            pool.wait_ge(rope_seq, 1)
            end()
            inverse_root(4, 8, LAT, 16)

            def rotate_queries(p):
                pool.wait_ge(evac_a, p * 2 + (C_MLA + 1))
                pool.wait_ge(evac_d, p * 2 + (C_MLA + 1))
                ends = [rotate(q_tok[:, :, QH * h + DH:QH * h + QH], *mm[h], q_roped) for h in range(2)]
                for h in range(2):
                    pool.wait_ge(rope_seq, p * 2 + (2 + h))
                    ends[h]()

            with pool.Fori(0, PAIRS) as p:
                rotate_queries(p)
            add_residual(C_OUT1)
            inverse_root(8, 10, D, 18)

        @block.scalar
        def _(act):
            a = nc.scalar

            def ahead(b, following=PK * CW, pieces=8):
                for k in range(pieces):
                    s = 4 + k
                    w = PK * CW if k < 4 else following
                    if isinstance(w, tuple):
                        w = w[k % 4]
                    act.wait_ge(piece_used, b * 8 + (s - RING + 1))
                    act.wait_ge(raw_landed[s % RAW], b * 16 + (16 if s < 8 else 32))
                    a.activation(w_hi[:, s % RING, 0:w], raw[:, s % RAW, 0:w], ACT.Copy).then_inc(hi_ready, 1)

            def evac(par, c, dst, scale=1.0, func=ACT.Copy, part="full"):
                act.wait_ge(piece_used, pieces_through(c, part))
                a.activation(dst, ps[:, 2 * par, :][:, 0:dst.shape[-1]], func, scale=scale).then_inc(evac_a, 1)

            def prep(u0, kts, gain, scaled=True):
                for s in range(kts // 4):
                    for bank in range(2):
                        act.wait_ge(t_done, 2 * (u0 + s) + bank + 1)
                        k = 4 * s + 2 * bank
                        if not scaled:
                            ins = a.activation(a_hi[:, k:k + 2, :], ps[:, 4 + bank, :].rearrange("p (k n) -> p k n", k=2), ACT.Copy)
                        else:
                            for kk in range(2):
                                ins = a.activation(a_hi[:, k + kk, :], ps[:, 4 + bank, 256 * kk:256 * kk + 256], ACT.Copy,
                                                   scale=gain_t[:, gain + k + kk:gain + k + kk + 1])
                        ins.then_inc(t_free_a, 1)

            def squares(src, dst, signal, out_):
                a.activation(out_, src, ACT.Square, accum_out=dst).then_inc(signal, 1)

            act.dma_start(xs[:, 0, :], x_d[0]).then_inc(x_landed[0], 16)
            act.dma_start(xs[:, 1, :], x_d[1]).then_inc(x_landed[1], 16)
            for s in range(RING):
                act.wait_ge(raw_landed[s], 16)
                a.activation(w_hi[:, s, :], raw[:, s, :], ACT.Copy).then_inc(hi_ready, 1)
            act.wait_ge(gain_ready, 1)
            prep(U_PREP0, KT, 0)
            for t in range(T):
                if t:
                    act.wait_ge(sq_ready, t)
                squares(xs[:, t, :], ssum[:, t:t + 1], sq_ready, junk)
            act.wait_ge(na_landed, 16)
            a.activation(n_hi[:, :, 0:GR], na_raw, ACT.Copy).then_inc(n_hi_ready, 1)
            act.wait_ge(rstd_ready, 1)
            r0 = rstd[:, 0:1]

            def pair_transposed(c, b, u, dst_of, scale):
                for par in range(2):
                    ahead(b + par)
                    evac(par, c + par, stg[par][:, 0, :], r0)
                for par in range(2):
                    act.wait_ge(t_done, u * 2 + (2 * par + 1))
                    a.activation(dst_of(par), ps[:, 4, :].rearrange("p (h q) -> p h q", h=2), ACT.Copy, scale=scale(par)).then_inc(t_free_a, 1)

            act.wait_ge(sq_ready, 2)
            pair_transposed(0, 0, U_QK, lambda par: gqk_t[:, 4 * par:4 * par + 2, :], lambda par: SB_SCALE if par == 0 else 1.0)
            for kind in range(2):
                c = 2 + 2 * kind
                pair_transposed(c, c, U_QK + c, lambda par: qk_t[:, 8 * kind + 4 * par:8 * kind + 4 * par + 2, :],
                                lambda par: SB_SCALE if kind == 0 else 1.0)
            act.wait_ge(ang_ready, 1)
            a.activation(sin_[:, :, 1, :], ang[:, 0, :, :], ACT.Sin).then_inc(trig_ready, 1)
            a.activation(cos_[:, :, 0, :], ang[:, 1, :, :], ACT.Sin).then_inc(trig_ready, 1)
            for half_ in range(2):
                v = (sb_v, g_v)[half_]
                for par in range(2):
                    ahead(B_SBV + 4 * half_ + par)
                    evac(par, 6 + 4 * half_ + par, v[:, 0, par * CW:par * CW + CW], r0)
                for par in range(2):
                    c = 8 + 4 * half_ + par
                    ahead(c)
                    dst = ys[:, :, 1024 * half_ + CW * par:1024 * half_ + CW * par + CW]
                    evac(par, c, dst[:, 0, :], r0, ACT.Silu)
                    act.wait_ge(evac_d, c + 1)
                    a.activation(dst[:, 1, :], dst[:, 1, :], ACT.Silu).then_inc(silu_ready, 1)

            act.wait_ge(ua_ready, 1)
            a.activation(g_e2, g_e2, ACT.Exp, scale=-1.0).then_inc(ue_ready, 1)
            act.wait_ge(ue_ready, 1)
            a.activation(g_e2, g_e2, ACT.Ln, bias=1.0).then_inc(ue_ready, 1)
            for lev in range(8):
                act.wait_ge(gd_ready, 2 * lev + 2)
                a.activation(g_u, g_u, ACT.Exp).then_inc(ge_ready, 1)
            for n in range(8):
                t, h = divmod(n, GH)
                if h % 2 == 0:
                    act.wait_ge(go_done, n // 2 + 1)
                act.wait_ge(sq_ready, 2 + n)
                squares(ps[:, 4 + 2 * t + h // 2, 256 * (h % 2):256 * (h % 2) + 256], ssum[:, 16 + n:17 + n], sq_ready, g_u[:, 0:GV])
            for h0 in range(0, SBH, 2):
                for h in (h0, h0 + 1):
                    act.wait_ge(sabs_ready, h + 1)
                    a.activation(sa[h % 2], sa[h % 2], ACT.Exp, scale=-1.0).then_inc(sexp_ready, 1)
                    act.wait_ge(sexp_ready, h + 1)
                    a.activation(sa[h % 2], sa[h % 2], ACT.Ln, bias=1.0).then_inc(slog_ready, 1)
                for h in (h0, h0 + 1):
                    act.wait_ge(sarg_done, h + 1)
                    a.activation(sa[h % 2], ps[:, 6 + h % 2, 0:384], ACT.Exp).then_inc(sw_ready, 1)

            prep(U_PREPY, KT, 0, scaled=False)

            def out_projection(b0, c0, added, last):
                def pair(i, end):
                    for par in range(2):
                        ahead(i * 2 + (b0 + par), pieces=4 if end and par else 8)
                        act.wait_ge(res_added, i * 2 + (par + added))
                        evac(par, i * 2 + (c0 + par), stg[par][:, 0, :], part="out" if last else "full")
                if last:
                    pair(0, False)
                    pair(1, True)
                else:
                    with act.Fori(0, 2) as i:
                        pair(i, False)

            out_projection(B_OUT0, 14, 0, False)
            prep(U_PREP1, KT, 16)
            act.wait_ge(res_added, 5)
            act.wait_ge(evac_d, 18)
            for t in range(T):
                act.wait_ge(sq_ready, 10 + t)
                squares(xs[:, t, :], ssum[:, 2 + t:3 + t], sq_ready, junk)
            act.wait_ge(kr_landed, 16)
            act.wait_ge(ga_done, 1)
            a.activation(n_hi[:, :, :], kr_raw, ACT.Copy).then_inc(n_hi_ready, 1)
            act.wait_ge(rstd_ready, 3)
            r1 = rstd[:, 2:3]
            for par in range(2):
                ahead(B_LAT + par)
                evac(par, 18 + par, lat[:, 0, CW * par:CW * par + CW], r1)
            for n in range(4):
                kind, t = divmod(n, T)
                act.wait_ge(evac_a, 20)
                act.wait_ge(evac_d, 20)
                act.wait_ge(sq_ready, 12 + n)
                squares(lat[:, t, CW * kind:CW * kind + CW], ssum[:, 4 + n:5 + n], sq_ready, junk[:, 0:CW])
            up_w = (PK * 2 * QH, PK * 2 * QH, PK * CW, PK * CW)

            def gate_pair(i, final):
                for par in range(2):
                    ahead(i * 2 + (B_GATE + par), following=up_w if final and par else PK * CW)
                    c = i * 2 + (20 + par)
                    evac(par, c, ys[:, 0, bass.ds(i * (2 * CW) + CW * par, CW)], r1, ACT.Silu)
                    act.wait_ge(evac_d, c + 1)
                    d1 = ys[:, 1, bass.ds(i * (2 * CW) + CW * par, CW)]
                    a.activation(d1, d1, ACT.Silu).then_inc(silu_ready, 1)

            gate_pair(0, False)
            gate_pair(1, True)
            prep(U_LAT, 8, 32)
            act.wait_ge(krt_done, 1)
            a.activation(kr_t, ps[0:ROPE, 6, 0:T * P], ACT.Copy).then_inc(krt_ready, 1)
            act.wait_ge(rstd_ready, 4)

            def front(i, par, first=False, last=False):
                p = i * 2 + par
                nxt = (PK * CW,) * 4 if last else up_w
                def piece(k):
                    s = 4 * (1 - par) + k
                    act.wait_ge(piece_used, p * 4 + (8 * B_MLA + 4 + k - (RING - 1)))
                    act.wait_ge(raw_landed[s], i * 16 + (16 * (B_MLA + 1) + (16 if par else 0)))
                    a.activation(w_hi[:, k, 0:nxt[k]], raw[:, s, 0:nxt[k]], ACT.Copy).then_inc(hi_ready, 1)
                evac(0, p * 2 + C_MLA, q_tok[:, 0, :], rstd[:, 4:5], part="up")
                piece(0)
                evac(1, p * 2 + (C_MLA + 1), kv_tok[par][:, 0, :], rstd[:, 6:7], part="up")
                if not first:
                    act.wait_ge(t_done, p * 4 + (2 * (U_MLA - 1) + 1))
                    a.activation(p_t[:, 0, :], ps[:, 4, 0:384], ACT.Copy).then_inc(t_free_a, 1)
                piece(1)
                piece(2)
                act.wait_ge(t_done, p * 4 + (2 * U_MLA + 1))
                a.activation(qn_t, ps[:, 4, :], ACT.Copy).then_inc(t_free_a, 1)
                act.wait_ge(qrt_done, p + 1)
                a.activation(qr_t[0:ROPE, :], ps[0:ROPE, 7, :], ACT.Copy).then_inc(qrt_ready, 1)
                piece(3)
                act.wait_ge(nmx_ready, p + 1)
                for h in range(2):
                    for t in range(T):
                        cols = (slice(0, P), slice(P, 384))[t]
                        j = 2 * h + t
                        a.activation(s_m[h][:, cols], s_m[h][:, cols], ACT.Exp, bias=nmx[:, j:j + 1], scale=MLA_SCALE,
                                     accum_out=rsum[:, j:j + 1]).then_inc(p_ready, 1)

            front(0, 0, first=True)
            with act.Fori(0, PAIRS // 2 - 1) as i:
                front(i, 1)
                front(i + 1, 0)
            front(PAIRS // 2 - 1, 1, last=True)
            act.wait_ge(t_done, 2 * (U_MLA + 2 * PAIRS - 1) + 1)
            a.activation(p_t[:, 0, :], ps[:, 4, 0:384], ACT.Copy).then_inc(t_free_a, 1)
            prep(U_PREPZ, KT, 0, scaled=False)
            out_projection(B_OUT1, C_OUT1, 4, True)
            act.wait_ge(res_added, 9)
            act.wait_ge(evac_d, C_OUT1 + 4)
            for t in range(T):
                act.wait_ge(sq_ready, 16 + t)
                squares(xs[:, t, :], ssum[:, 8 + t:9 + t], sq_ready, junk)

        @block.vector
        def _(dve):
            v = nc.vector

            def split_lo(b, s, w):
                dve.wait_ge(hi_ready, b * 8 + (s + 1))
                v.tensor_tensor(w_lo[:, s % RING, 0:w], raw[:, s % RAW, 0:w], w_hi[:, s % RING, 0:w].bitcast(F32),
                                ALU.subtract).then_inc(lo_ready, 1)

            def ahead(b, following=PK * CW, pieces=8):
                for k in range(pieces):
                    w = PK * CW if k < 4 else following
                    split_lo(b, 4 + k, w[k % 4] if isinstance(w, tuple) else w)

            def evac(par, c, dst, scale, part="full"):
                dve.wait_ge(piece_used, pieces_through(c, part))
                v.tensor_scalar(dst, ps[:, 2 * par + 1, :][:, 0:dst.shape[-1]], scale, None, ALU.mult).then_inc(evac_d, 1)

            def prep(u0, kts, gain, scaled=True):
                for s in range(kts // 4):
                    for bank in range(2):
                        k = 4 * s + 2 * bank
                        dve.wait_ge(t_free_a, freed(u0) + 2 * s + bank + 1)
                        if not scaled:
                            ins = v.tensor_tensor(a_lo[:, k:k + 2, :], ps[:, 4 + bank, :].rearrange("p (k n) -> p k n", k=2),
                                                  a_hi[:, k:k + 2, :].bitcast(F32), ALU.subtract)
                        else:
                            for kk in range(2):
                                ins = v.scalar_tensor_tensor(
                                    out=a_lo[:, k + kk, :], in0=ps[:, 4 + bank, 256 * kk:256 * kk + 256],
                                    scalar=gain_t[:, gain + k + kk:gain + k + kk + 1],
                                    in1=a_hi[:, k + kk, :].bitcast(F32), op0=ALU.mult, op1=ALU.subtract)
                        ins.then_inc(t_free_d, 1)

            dve.wait_ge(gain_done, 1)
            v.tensor_copy(gain_t[:, :], ps[:, 6, 0:40]).then_inc(gain_ready, 1)
            for s in range(RING):
                split_lo(0, s, PK * CW)
            dve.wait_ge(gain_ready, 1)
            prep(U_PREP0, KT, 0)
            dve.wait_ge(n_hi_ready, 1)
            v.tensor_tensor(n_lo[:, :, 0:GR], na_raw, n_hi[:, :, 0:GR].bitcast(F32), ALU.subtract).then_inc(n_lo_ready, 1)
            dve.wait_ge(rstd_ready, 1)
            r0, r1 = rstd[:, 0:1], rstd[:, 1:2]

            def pair_transposed(c, u, dst_of, scale):
                for par in range(2):
                    ahead(c + par)
                    evac(par, c + par, stg[par][:, 1, :], r1)
                if c == 0:
                    dve.wait_ge(ga_done, 1)
                    v.tensor_scalar(ga_tok[:, 0, :], ps[:, 6, 0:GR], r0, None, ALU.mult).then_inc(ga_ready, 1)
                    v.tensor_scalar(ga_tok[:, 1, :], ps[:, 6, GR:2 * GR], r1, None, ALU.mult).then_inc(ga_ready, 1)
                for par in range(2):
                    dve.wait_ge(t_done, u * 2 + (2 * par + 2))
                    v.tensor_scalar(dst_of(par), ps[:, 5, :].rearrange("p (h q) -> p h q", h=2), scale(par), None,
                                    ALU.mult).then_inc(t_free_d, 1)
                if c == 0:
                    dve.wait_ge(gat_done, 1)
                    v.tensor_copy(ga_t, ps[0:GR, 7, 0:T * P]).then_inc(gat_ready, 1)
                    dve.wait_ge(bias_landed, 16)
                    for t in range(T):
                        dve.wait_ge(u_done, t + 1)
                        v.tensor_tensor(g_u[:, 512 * t:512 * t + 512], ps[:, 6 + t, :], g_bias, ALU.add).then_inc(u_ready, 1)

            pair_transposed(0, U_QK, lambda par: gqk_t[:, 4 * par + 2:4 * par + 4, :], lambda par: SB_SCALE if par == 0 else 1.0)
            for kind in range(2):
                c = 2 + 2 * kind
                pair_transposed(c, U_QK + c, lambda par: qk_t[:, 8 * kind + 4 * par + 2:8 * kind + 4 * par + 4, :],
                                lambda par: SB_SCALE if kind == 0 else 1.0)
            for half_ in range(2):
                vv = (sb_v, g_v)[half_]
                for par in range(2):
                    ahead(B_SBV + 4 * half_ + par)
                    evac(par, 6 + 4 * half_ + par, vv[:, 1, par * CW:par * CW + CW], r1)
                for par in range(2):
                    c = 8 + 4 * half_ + par
                    ahead(c)
                    evac(par, c, ys[:, 1, 1024 * half_ + CW * par:1024 * half_ + CW * par + CW], r1)

            dve.wait_ge(u_ready, 2)
            v.tensor_scalar(g_e2.bitcast(I32), g_u.bitcast(I32), ABS, None, ALU.bitwise_and).then_inc(ua_ready, 1)
            dve.wait_ge(ue_ready, 2)
            v.scalar_tensor_tensor(out=g_u, in0=g_u, scalar=0.0, in1=g_e2, op0=ALU.min, op1=ALU.subtract).then_inc(g_ready, 1)
            for bank in range(2):
                dve.wait_ge(b_done, bank + 1)
                v.tensor_copy(g_b[:, 512 * bank:512 * bank + 512], ps[:, 6 + bank, :]).then_inc(b_ready, 1)
            dve.wait_ge(t_done, 2 * U_PREPY)
            v.memset(work[:, 0:2048], 0.0).then_inc(gd_init, 1)
            dve.wait_ge(gd_init, 1)
            dve.wait_ge(t_free_a, freed(U_PREPY))
            dve.wait_ge(t_free_d, freed(U_PREPY))
            for lev in range(9):
                if lev < 8:
                    L = P >> lev

                    def halves(t_):
                        w = t_.rearrange("p (m a l) -> p m a l", a=2, l=L)
                        return w[:, :, 0, :], w[:, :, 1, :]

                    (b0, b1), (e0, e1) = halves(g_b), halves(g_u)
                    q1 = halves(even[:, 4096:5120])[1]
                    k0 = halves(even[:, 5120:6144])[0]
                    qd1, kd0 = halves(g_qd)[1], halves(g_kd)[0]
                    ref = b0[:, :, L - 1:L].to_broadcast([P, GH * T * P // (2 * L), L])
                    if lev:
                        dve.wait_ge(gq_ready, 2 * lev)
                    else:
                        dve.wait_ge(b_ready, 2)
                    v.tensor_tensor(e0, ref, b0, ALU.subtract).then_inc(gd_ready, 1)
                    if lev == 0:
                        v.tensor_copy(e1, b1).then_inc(gd_ready, 1)
                    else:
                        v.tensor_tensor(e1, b1, ref, ALU.subtract).then_inc(gd_ready, 1)
                    dve.wait_ge(ge_ready, lev + 1)
                    if lev:
                        dve.wait_ge(lev_done, 2 * lev - 1)
                    v.scalar_tensor_tensor(out=qd1, in0=e1, scalar=1.0, in1=q1, op0=ALU.min, op1=ALU.mult).then_inc(gq_ready, 1)
                    v.scalar_tensor_tensor(out=kd0, in0=e0, scalar=1.0, in1=k0, op0=ALU.min, op1=ALU.mult).then_inc(gq_ready, 1)
                for bank in range(1 if lev == 0 else 2):
                    dve.wait_ge(lev_done, 2 * lev + bank if lev else 1)
                    src = ps[:, 6 + bank, :]
                    dst = att[:, 512 * bank:512 * bank + 512]
                    if lev == 0:
                        v.tensor_copy(att_x, src).then_inc(lev_copied, 1)
                    elif lev == 1:
                        v.tensor_copy(dst, src).then_inc(lev_copied, 1)
                    else:
                        m = masks[:, lev - 2, :] if lev < 8 else ident[:, :]
                        dve.wait_ge(consts, 10)
                        dve.wait_ge(lev_copied, 2 * lev - 1 + bank)
                        v.copy_predicated(dst.rearrange("p (h q) -> p h q", h=GH),
                                          m.bitcast(I32).unsqueeze(1).to_broadcast([P, GH, P]),
                                          src.rearrange("p (h q) -> p h q", h=GH)).then_inc(lev_copied, 1)
            dve.wait_ge(rstd_ready, 2)
            dve.wait_ge(gg_ready, 2)
            for n in range(8):
                t, h = divmod(n, GH)
                y = ys[:, t, SBH * DH + GV * h:SBH * DH + GV * h + GV]
                v.scalar_tensor_tensor(out=y, in0=ps[:, 4 + 2 * t + h // 2, GV * (h % 2):GV * (h % 2) + GV],
                                       scalar=rstd[:, 16 + n:17 + n], in1=y, op0=ALU.mult, op1=ALU.mult).then_inc(gy_ready, 1)
            for h0 in range(0, SBH, 2):
                for h in (h0, h0 + 1):
                    dve.wait_ge(sz_done, h + 1)
                    v.tensor_scalar(sa[h % 2].bitcast(I32), ps[:, 6 + h % 2, 0:384].bitcast(I32), ABS, None, ALU.bitwise_and).then_inc(sabs_ready, 1)
                for h in (h0, h0 + 1):
                    dve.wait_ge(slog_ready, h + 1)
                    v.scalar_tensor_tensor(out=sp_[h % 2], in0=ps[:, 6 + h % 2, 0:384], scalar=0.0, in1=sa[h % 2],
                                           op0=ALU.max, op1=ALU.add).then_inc(ssp_ready, 1)
                for h in (h0, h0 + 1):
                    dve.wait_ge(sy_done, h + 1)
                    y = ys[:, :, DH * h:DH * h + DH]
                    v.tensor_tensor(y, y, ps[:, 4 + h % 2, 0:T * DH].rearrange("p (t e) -> p t e", t=T), ALU.mult).then_inc(sy_ready, 1)
            prep(U_PREPY, KT, 0, scaled=False)

            def out_projection(b0, c0, last):
                def pair(i, end):
                    for par in range(2):
                        ahead(i * 2 + (b0 + par), pieces=4 if end and par else 8)
                        dve.wait_ge(piece_used, pieces_through(i * 2 + (c0 + par), "out" if last else "full"))
                        dst = xs[:, 1, bass.ds(i * (2 * CW) + par * CW, CW)]
                        v.tensor_tensor(dst, dst, ps[:, 2 * par + 1, :], ALU.add).then_inc(evac_d, 1)
                if last:
                    pair(0, False)
                    pair(1, True)
                else:
                    with dve.Fori(0, 2) as i:
                        pair(i, False)

            out_projection(B_OUT0, 14, False)
            prep(U_PREP1, KT, 16)
            dve.wait_ge(n_hi_ready, 2)
            v.tensor_tensor(n_lo[:, :, :], kr_raw, n_hi[:, :, :].bitcast(F32), ALU.subtract).then_inc(n_lo_ready, 1)
            dve.wait_ge(rstd_ready, 3)
            r1 = rstd[:, 3:4]
            for par in range(2):
                ahead(B_LAT + par)
                evac(par, 18 + par, lat[:, 1, CW * par:CW * par + CW], r1)
            dve.wait_ge(kr_done, 1)
            v.tensor_scalar(kr_tok[:, 0, :], ps[:, 6, 0:ROPE], rstd[:, 2:3], None, ALU.mult).then_inc(kr_evac, 1)
            v.tensor_scalar(kr_tok[:, 1, :], ps[:, 6, ROPE:2 * ROPE], r1, None, ALU.mult).then_inc(kr_evac, 1)
            up_w = (PK * 2 * QH, PK * 2 * QH, PK * CW, PK * CW)

            def gate_pair(i, final):
                for par in range(2):
                    ahead(i * 2 + (B_GATE + par), following=up_w if final and par else PK * CW)
                    evac(par, i * 2 + (20 + par), ys[:, 1, bass.ds(i * (2 * CW) + CW * par, CW)], r1)

            gate_pair(0, False)
            gate_pair(1, True)
            prep(U_LAT, 8, 32)
            dve.wait_ge(rstd_ready, 4)

            def weighted(i, par):
                dve.wait_ge(my_done, i * 4 + (2 * par + 2))
                for h in range(2):
                    for t in range(T):
                        y = ys[:, t, bass.ds(i * (4 * DH) + (2 * par + h) * DH, DH)]
                        v.scalar_tensor_tensor(out=y, in0=ps[:, 6, (2 * h + t) * DH:(2 * h + t + 1) * DH],
                                               scalar=rinv[:, 2 * h + t:2 * h + t + 1], in1=y,
                                               op0=ALU.mult, op1=ALU.mult).then_inc(my_ready, 1)

            def before(i, par):
                return (i, 0) if par else (i - 1, 1)

            def front(i, par, first=False, last=False):
                p = i * 2 + par
                nxt = (PK * CW,) * 4 if last else up_w

                def piece(k):
                    dve.wait_ge(hi_ready, p * 4 + (8 * B_MLA + 5 + k))
                    v.tensor_tensor(w_lo[:, k, 0:nxt[k]], raw[:, 4 * (1 - par) + k, 0:nxt[k]],
                                    w_hi[:, k, 0:nxt[k]].bitcast(F32), ALU.subtract).then_inc(lo_ready, 1)

                evac(0, p * 2 + C_MLA, q_tok[:, 1, :], rstd[:, 5:6], part="up")
                piece(0)
                evac(1, p * 2 + (C_MLA + 1), kv_tok[par][:, 1, :], rstd[:, 7:8], part="up")
                if not first:
                    dve.wait_ge(p_ready, p * 4)
                    v.reciprocal(rinv[:, :], rsum[:, :]).then_inc(rinv_ready, 1)
                    dve.wait_ge(t_done, p * 4 + (2 * (U_MLA - 1) + 2))
                    v.tensor_copy(p_t[:, 1, :], ps[:, 5, 0:384]).then_inc(t_free_d, 1)
                piece(1)
                piece(2)
                if not first:
                    dve.wait_ge(rinv_ready, p)
                    weighted(*before(i, par))
                dve.wait_ge(t_done, p * 4 + (2 * U_MLA + 2))
                v.tensor_copy(kn_t, ps[:, 5, :]).then_inc(t_free_d, 1)
                piece(3)
                for h in range(2):
                    dve.wait_ge(sc_done, p * 2 + (h + 1))
                    v.memset(idle[:, h:h + 1], 0.0)
                    for t in range(T):
                        cols = (slice(0, P), slice(P, 384))[t]
                        v.tensor_tensor_reduce(s_m[h][:, cols], ps[:, 6 + h, cols], causal[:, P if t == 0 else 0:2 * P],
                                               1.0, -3.0e38, ALU.add, ALU.max, mx[:, 2 * h + t:2 * h + t + 1]).then_inc(sc_max, 1)
                dve.wait_ge(sc_max, p * 4 + 4)
                v.tensor_scalar(nmx[:, :], mx[:, :], -MLA_SCALE, None, ALU.mult).then_inc(nmx_ready, 1)

            front(0, 0, first=True)
            with dve.Fori(0, PAIRS // 2 - 1) as i:
                front(i, 1)
                front(i + 1, 0)
            front(PAIRS // 2 - 1, 1, last=True)
            dve.wait_ge(p_ready, 4 * PAIRS)
            v.reciprocal(rinv[:, :], rsum[:, :]).then_inc(rinv_ready, 1)
            dve.wait_ge(t_done, 2 * (U_MLA + 2 * PAIRS - 1) + 2)
            v.tensor_copy(p_t[:, 1, :], ps[:, 5, 0:384]).then_inc(t_free_d, 1)
            dve.wait_ge(rinv_ready, PAIRS)
            weighted(PAIRS // 2 - 1, 1)
            prep(U_PREPZ, KT, 0, scaled=False)
            out_projection(B_OUT1, C_OUT1, True)
            dve.wait_ge(rstd_ready, 5)
            dve.wait_ge(fin_landed, 16)
            for t in range(T):
                v.scalar_tensor_tensor(out=xs[:, t, :], in0=xs[:, t, :], scalar=rstd[:, 8 + t:9 + t], in1=fin_g,
                                       op0=ALU.mult, op1=ALU.mult).then_inc(fin_ready, 1)

        @block.tensor
        def _(pe):
            m = nc.tensor

            def project(n0, c, par, wait=True, tiles=NP, k0=0, s0=0, n=CW):
                if wait:
                    pe.wait_ge(evac_a, c - 1)
                    pe.wait_ge(evac_d, c - 1)
                for j in range(tiles):
                    s = (s0 + j) % RING
                    pe.wait_ge(lo_ready, n0 + (j + 1))
                    for kk in range(PK):
                        k = k0 + PK * j + kk
                        hi, lo = w_hi[:, s, kk * n:kk * n + n], w_lo[:, s, kk * n:kk * n + n]
                        first, last = j == 0 and kk == 0, j == tiles - 1 and kk == PK - 1
                        for t in range(T):
                            acc = ps[:, 2 * par + t, 0:n]
                            tok = slice(t * P, t * P + P)
                            m.matmul(acc, a_hi[:, k, tok], hi, start=first, stop=False)
                            m.matmul(acc, a_hi[:, k, tok], lo, start=False, stop=False)
                            ins = m.matmul(acc, a_lo[:, k, tok], hi, start=False, stop=last)
                    ins.then_inc(piece_used, 1)

            def narrow(n, signal):
                for t in range(T):
                    for k in range(KT):
                        acc = ps[:, 6, t * n:t * n + n]
                        tok = slice(t * P, t * P + P)
                        m.matmul(acc, a_hi[:, k, tok], n_hi[:, k, 0:n], start=k == 0, stop=False)
                        m.matmul(acc, a_hi[:, k, tok], n_lo[:, k, 0:n], start=False, stop=False)
                        ins = m.matmul(acc, a_lo[:, k, tok], n_hi[:, k, 0:n], start=False, stop=k == KT - 1)
                ins.then_inc(signal, 1)

            def step_free(u):
                pe.wait_ge(t_free_a, freed(u))
                pe.wait_ge(t_free_d, freed(u))

            def transpose_operand(u0, kts, src):
                for s in range(kts // 4):
                    step_free(u0 + s)
                    for bank in range(2):
                        for kk in range(2):
                            k = 4 * s + 2 * bank + kk
                            for t in range(T):
                                ins = m.transpose(ps[:, 4 + bank, 256 * kk + P * t:256 * kk + P * t + P],
                                                  src[:, t, P * k:P * k + P], ident[:, :])
                        ins.then_inc(t_done, 1)

            pe.wait_ge(consts, 1)
            pe.wait_ge(gains_landed, 64)
            m.transpose(ps[:, 6, 0:40], gain_rows, ident[0:40, 0:40]).then_inc(gain_done, 1)
            for t in range(T):
                pe.wait_ge(x_landed[t], 16)
            transpose_operand(U_PREP0, KT, xs)
            step_free(U_QK)

            def heads_transposed(c, par, u):
                pe.wait_ge(evac_a, c + 1)
                pe.wait_ge(evac_d, c + 1)
                step_free(u)
                for bank in range(2):
                    for kk in range(2):
                        for t in range(T):
                            blk = 2 * bank + kk
                            ins = m.transpose(ps[:, 4 + bank, 256 * kk + P * t:256 * kk + P * t + P],
                                              stg[par][:, t, P * blk:P * blk + P], ident[:, :])
                    ins.then_inc(t_done, 1)

            for q in range(3):
                for par in range(2):
                    c = 2 * q + par
                    project(NP * c, c, par, wait=q > 0)
                if q == 0:
                    pe.wait_ge(n_lo_ready, 1)
                    pe.wait_ge(gain_ready, 1)
                    narrow(GR, ga_done)
                for par in range(2):
                    heads_transposed(2 * q + par, par, U_QK + 2 * q + par)
                if q == 0:
                    pe.wait_ge(ga_ready, 2)
                    for t in range(T):
                        ins = m.transpose(ps[0:GR, 7, P * t:P * t + P], ga_tok[:, t, :], ident[:, :])
                    ins.then_inc(gat_done, 1)
                    pe.wait_ge(gat_ready, 1)
                    pe.wait_ge(alpha_landed, 16)
                    for t in range(T):
                        m.matmul(ps[:, 6 + t, :], ga_t[:, P * t:P * t + P], g_alpha, start=True, stop=True).then_inc(u_done, 1)
            with pe.Fori(0, 4) as i:
                for par in range(2):
                    project(i * (2 * NP) + NP * (6 + par), i * 2 + (6 + par), par)

            pe.wait_ge(g_ready, 1)
            for h in range(GH):
                for t in range(T):
                    ins = m.matmul(ps[:, 6 + h // 2, 256 * (h % 2) + P * t:256 * (h % 2) + P * t + P],
                                   g_u[:, 512 * t + DH * h:512 * t + DH * h + DH], tri16[:, :], start=True, stop=True)
                if h % 2:
                    ins.then_inc(b_done, 1)
            for lev in range(9):
                if lev == 0:
                    pe.wait_ge(b_ready, 2)
                else:
                    pe.wait_ge(lev_copied, 2 * lev - 1)
                if lev < 8:
                    pe.wait_ge(gq_ready, 2 * lev + 2)
                kd, qd = (g_kd, g_qd) if lev < 8 else (even[:, 5120:6144], even[:, 4096:5120])
                for t in range(1 if lev == 0 else 2):
                    for h in range(GH):
                        kt, qt = 256 * h + P * t, 256 * h + P * t
                        if lev == 0:
                            qt += P
                        ins = m.matmul(ps[:, 6 + t, P * h:P * h + P], kd[:, kt:kt + P], qd[:, qt:qt + P], start=True, stop=True)
                    ins.then_inc(lev_done, 1)
            pe.wait_ge(lev_copied, 17)
            pe.wait_ge(att_ready, 1)
            step_free(U_PREPY)
            for t in range(T):
                for h in range(GH):
                    o = ps[:, 4 + 2 * t + h // 2, GV * (h % 2):GV * (h % 2) + GV]
                    if t:
                        m.matmul(o, att_x[:, P * h:P * h + P], g_v[:, 0, GV * h:GV * h + GV], start=True, stop=False)
                    ins = m.matmul(o, att[:, 512 * t + P * h:512 * t + P * h + P], g_v[:, t, GV * h:GV * h + GV],
                                   start=t == 0, stop=True)
                    if h % 2:
                        ins.then_inc(go_done, 1)

            pe.wait_ge(gy_ready, 8)
            pe.wait_ge(consts, 3)
            for h0 in range(0, SBH, 2):
                for h in (h0, h0 + 1):
                    qh, kh = qk_t[:, h, :], qk_t[:, SBH + h, :]
                    m.matmul(ps[:, 6 + h % 2, 0:256], kh[:, 0:P], qh, start=True, stop=True)
                    m.matmul(ps[:, 6 + h % 2, 256:384], kh[:, P:2 * P], qh[:, P:2 * P], start=False, stop=True,
                             skip_group_check=True).then_inc(sz_done, 1)
                for h in (h0, h0 + 1):
                    pe.wait_ge(ssel_ready, h + 1)
                    z, s = ps[:, 6 + h % 2, :], sp_[h % 2]
                    m.matmul(z[:, 0:256], neg_tri[:, :], s[:, 0:256], start=False, stop=False, skip_group_check=True)
                    m.matmul(z[:, P:256], neg_one[:, :], s[:, 256:384], start=False, stop=False, skip_group_check=True)
                    m.matmul(z[:, 256:384], neg_tri[:, :], s[:, 256:384], start=False, stop=True,
                             skip_group_check=True).then_inc(sarg_done, 1)
                for h in (h0, h0 + 1):
                    pe.wait_ge(swm_ready, h + 1)
                    if h >= 2:
                        pe.wait_ge(sy_ready, h - 1)
                    w, o = sa[h % 2], ps[:, 4 + h % 2, :]
                    hc = slice(DH * h, DH * h + DH)
                    m.matmul(o[:, 0:DH], w[:, 0:P], sb_v[:, 0, hc], start=True, stop=True)
                    m.matmul(o[:, DH:2 * DH], w[:, P:256], sb_v[:, 0, hc], start=True, stop=False)
                    m.matmul(o[:, DH:2 * DH], w[:, 256:384], sb_v[:, 1, hc], start=False, stop=True).then_inc(sy_done, 1)
            pe.wait_ge(sy_ready, SBH)
            transpose_operand(U_PREPY, KT, ys)
            step_free(U_PREP1)
            with pe.Fori(0, 2) as i:
                for par in range(2):
                    project(i * (2 * NP) + NP * (B_OUT0 + par), i * 2 + (14 + par), par)

            pe.wait_ge(res_added, 5)
            pe.wait_ge(evac_d, 18)
            transpose_operand(U_PREP1, KT, xs)
            step_free(U_LAT)
            for par in range(2):
                project(NP * (B_LAT + par), 18 + par, par)
            pe.wait_ge(n_lo_ready, 2)
            narrow(ROPE, kr_done)
            with pe.Fori(0, 2) as i:
                for par in range(2):
                    project(i * (2 * NP) + NP * (B_GATE + par), i * 2 + (20 + par), par)
            transpose_operand(U_LAT, 8, lat)
            pe.wait_ge(kr_roped, 1)
            pe.wait_ge(kr_evac, 2)
            for t in range(T):
                ins = m.transpose(ps[0:ROPE, 6, P * t:P * t + P], kr_tok[:, t, :], ident[:, :])
            ins.then_inc(krt_done, 1)
            step_free(U_MLA)
            pe.wait_ge(krt_ready, 1)

            def mix(i, par):
                p = i * 2 + par
                pe.wait_ge(p_ready, p * 4 + 4)
                pe.wait_ge(t_free_a, p * 2 + (freed(U_MLA) + 1))
                pe.wait_ge(t_free_d, p * 2 + (freed(U_MLA) + 1))
                for h in range(2):
                    for c in range(3):
                        ins = m.transpose(ps[:, 4 + h, P * c:P * c + P], s_m[h][:, ((0, 1, 2)[c]) * P:((0, 1, 2)[c]) * P + P], ident[:, :])
                    ins.then_inc(t_done, 1)
                for h in range(2):
                    if h == 0:
                        pe.wait_ge(t_free_a, p * 2 + (freed(U_MLA) + 2))
                    else:
                        pe.wait_ge(t_free_d, p * 2 + (freed(U_MLA) + 2))
                    o = ps[:, 6, 2 * DH * h:2 * DH * h + 2 * DH]
                    vh = slice(2 * DH * h + DH, 2 * DH * h + 2 * DH)
                    m.matmul(o[:, 0:DH], p_t[:, h, 0:P], kv_tok[par][:, 0, vh], start=True, stop=True)
                    m.matmul(o[:, DH:2 * DH], p_t[:, h, P:2 * P], kv_tok[par][:, 0, vh], start=True, stop=False)
                    m.matmul(o[:, DH:2 * DH], p_t[:, h, 2 * P:3 * P], kv_tok[par][:, 1, vh], start=False, stop=True).then_inc(my_done, 1)

            def front(i, par):
                p = i * 2 + par
                for kind in range(2):
                    project(p * 4 + (NP * B_MLA + 2 * kind), p * 2 + (C_MLA + kind), kind, tiles=2, k0=4 * kind, s0=2 * kind,
                            n=2 * QH if kind == 0 else CW)

            def scores(i, par):
                p = i * 2 + par
                pe.wait_ge(q_roped, p * 2 + 2)
                pe.wait_ge(evac_a, p * 2 + (C_MLA + 2))
                pe.wait_ge(evac_d, p * 2 + (C_MLA + 2))
                pe.wait_ge(t_free_a, p * 2 + freed(U_MLA))
                pe.wait_ge(t_free_d, p * 2 + freed(U_MLA))
                for h in range(2):
                    for t in range(T):
                        ins = m.transpose(ps[:, 4, 256 * h + P * t:256 * h + P * t + P], q_tok[:, t, QH * h:QH * h + DH], ident[:, :])
                ins.then_inc(t_done, 1)
                for h in range(2):
                    for t in range(T):
                        ins = m.transpose(ps[:, 5, 256 * h + P * t:256 * h + P * t + P], kv_tok[par][:, t, 2 * DH * h:2 * DH * h + DH], ident[:, :])
                ins.then_inc(t_done, 1)
                for h in range(2):
                    for t in range(T):
                        ins = m.transpose(ps[0:ROPE, 7, 256 * h + P * t:256 * h + P * t + P], q_tok[:, t, QH * h + DH:QH * h + QH], ident[:, :])
                ins.then_inc(qrt_done, 1)
                pe.wait_ge(t_free_a, p * 2 + (freed(U_MLA) + 1))
                pe.wait_ge(t_free_d, p * 2 + (freed(U_MLA) + 1))
                pe.wait_ge(qrt_ready, p + 1)
                pe.wait_ge(my_ready, p * 4)
                for h in range(2):
                    for t in range(T):
                        o = ps[:, 6 + h, 0:P] if t == 0 else ps[:, 6 + h, P:384]
                        kc = slice(256 * h, 256 * h + P * (t + 1))
                        m.matmul(o, qn_t[:, 256 * h + P * t:256 * h + P * t + P], kn_t[:, kc], start=True, stop=False)
                        ins = m.matmul(o, qr_t[0:ROPE, 256 * h + P * t:256 * h + P * t + P], kr_t[:, 0:P * (t + 1)],
                                       start=False, stop=True)
                    ins.then_inc(sc_done, 1)

            front(0, 0)
            scores(0, 0)
            with pe.Fori(0, PAIRS // 2 - 1) as i:
                for j in range(2):
                    front(i + j, 1 - j)
                    mix(i, j)
                    scores(i + j, 1 - j)
            front(PAIRS // 2 - 1, 1)
            mix(PAIRS // 2 - 1, 0)
            scores(PAIRS // 2 - 1, 1)
            mix(PAIRS // 2 - 1, 1)
            pe.wait_ge(my_ready, 4 * PAIRS)
            transpose_operand(U_PREPZ, KT, ys)
            step_free(U_PREPZ + 4)
            with pe.Fori(0, 2) as i:
                for par in range(2):
                    project(i * (2 * NP) + NP * (B_OUT1 + par), i * 2 + (C_OUT1 + par), par)


_INS = ["x", "positions", "ln_even", "w_in_even", "gla_alpha_up", "gla_alpha_bias", "gla_norm", "w_out_even",
        "ln_odd", "w_in_odd", "q_norm", "w_q_up", "kv_norm", "w_kv_up", "w_out_odd", "final_norm"]


def kernel(**inputs):
    import concourse.bacc as bacc
    from concourse.bass_utils import run_bass_kernel_spmd

    nc = bacc.Bacc("TRN2", target_bir_lowering=False, num_devices=1)
    arrays, args = {}, []
    for name in _INS:
        arr = np.ascontiguousarray(inputs[name])
        arrays[f"in_{name}"] = arr
        args.append(nc.dram_tensor(f"in_{name}", arr.shape, mybir.dt.from_np(arr.dtype), kind="ExternalInput").ap())
    shape = arrays["in_x"].shape
    args.append(nc.dram_tensor("out_0", shape, F32, kind="ExternalOutput").ap())
    build(nc, *args)
    r = run_bass_kernel_spmd(nc, [arrays], core_ids=[0])
    return r.results[0]["out_0"]
```

```python
from contextlib import ExitStack

import numpy as np

import concourse.bass as bass
from concourse import mybir
from concourse.alu_op_type import AluOpType as ALU

ACT = mybir.ActivationFunctionType
F32 = mybir.dt.float32
F32R = mybir.dt.float32r
I32 = mybir.dt.int32

P = 128
D = 2048
T = 2
KT = D // P
CW = 512
PK = 2
NP = KT // PK
RAW = 8
RING = 4
SBH, GH, MH = 8, 4, 16
DH = 128
GV = 256
GR = 16
ROPE = 64
QH = DH + ROPE
LAT = 512
PAIRS = MH // 2
EPS = 1e-6
SB_SCALE = float(DH) ** -0.5
MLA_SCALE = float(QH) ** -0.5
NEG = -1e30
ABS = 0x7FFFFFFF
THETA = 10000.0
TWO_PI = 2 * np.pi
C1 = 6.28125
C2 = float(np.float32(TWO_PI - C1))
C3 = float(np.float32(TWO_PI - C1 - C2))
MAGIC = 12582912.0
INV_FREQ = [float(v) for v in (np.float32(THETA) ** (-np.arange(ROPE // 2, dtype=np.float32) / np.float32(ROPE // 2)))]

SB_Q, SB_V, G_QK, G_V, G_A = 0, 2048, 4096, 5120, 7168
O_KR, O_GATE = 2 * LAT, 2 * LAT + ROPE

B_GA, B_GQK, B_SBQK, B_MIX, B_OUT0 = 0, 1, 3, 7, 15
B_LAT, B_KR, B_GATE, B_MLA, B_OUT1, B_END = 19, 21, 22, 26, 30, 34
C_GQK, C_SBQK, C_MIX, C_OUT0, C_LAT, C_GATE, C_MLA = 0, 2, 6, 14, 18, 20, 24
C_OUT1 = C_MLA + 2 * PAIRS
U_PREP0, U_QK, U_PREPY, U_PREP1, U_LAT, U_MLA = 0, 4, 10, 14, 18, 20
U_PREPZ = U_MLA + PAIRS
FULL = PK * CW
UP = (PK * 2 * QH, PK * 2 * QH, PK * CW, PK * CW)


def freed(u):
    n = 0
    for first, last, each in ((U_PREP0, U_QK, 2), (U_QK, U_PREPY, 1), (U_PREPY, U_MLA, 2), (U_MLA, U_PREPZ, 1), (U_PREPZ, 999, 2)):
        n += each * max(0, min(u, last) - first)
    return n


def pieces_through(c, part="even"):
    if part == "up":
        return c * 2 + (NP * B_MLA - 2 * C_MLA + 2)
    b0 = {"even": B_GQK - C_GQK, "gate": B_GATE - C_GATE, "out": B_OUT1 - C_OUT1}[part]
    return c * NP + (NP * b0 + NP)


def levels_done(lev):
    return 2 * lev + 1


def build(nc, x, positions, ln_even, w_in_even, gla_alpha_up, gla_alpha_bias, gla_norm, w_out_even,
          ln_odd, w_in_odd, q_norm, w_q_up, kv_norm, w_kv_up, w_out_odd, final_norm, out):
    x_d = x[0].rearrange("(t p) d -> t p d", p=P)
    out_d = out[0].rearrange("(t p) d -> t p d", p=P)

    def by_k(w):
        return w[0].rearrange("(k p) n -> p k n", p=P)

    we_d, wo0_d, wi1_d, wo1_d = by_k(w_in_even), by_k(w_out_even), by_k(w_in_odd), by_k(w_out_odd)
    wq_d, wkv_d = by_k(w_q_up), by_k(w_kv_up)

    with ExitStack() as ctx:
        def sb(name, shape, dt=F32):
            return ctx.enter_context(nc.sbuf_tensor(name, shape, dt))

        def sem(name):
            return ctx.enter_context(nc.semaphore(name))

        ps = ctx.enter_context(nc.psum_tensor("ps", [P, 8, CW], F32))

        raw = sb("raw", [P, RAW, PK * CW])
        w_hi = sb("w_hi", [P, RING, PK * CW], F32R)
        w_lo = sb("w_lo", [P, RING, PK * CW], F32R)
        a_hi = sb("a_hi", [P, KT, T * P], F32R)
        a_lo = sb("a_lo", [P, KT, T * P], F32R)
        xs = sb("xs", [P, T, D])
        ys = sb("ys", [P, T, D])
        even = sb("even", [P, 10240])
        work = sb("work", [P, 2048 + 3584])

        qk_t = even[:, 0:4096].rearrange("p (h q) -> p h q", h=2 * SBH)
        gqk_t = even[:, 4096:6144].rearrange("p (h q) -> p h q", h=2 * GH)
        vals = even[:, 6144:10240].rearrange("p (t n) -> p t n", t=T)
        lat = even[:, 0:2048].rearrange("p (t n) -> p t n", t=T)
        fin_g = even[:, 3072:5120]
        q_tok = even[:, 5120:5888].rearrange("p (t n) -> p t n", t=T)
        qn_t = even[:, 5888:6400]
        kn_t = even[:, 6400:6912]
        qr_t = even[:, 6912:7424]
        kv_tok = [even[:, 7424 + 1024 * i:8448 + 1024 * i].rearrange("p (t n) -> p t n", t=T) for i in range(2)]
        p_t = even[:, 9472:10240].rearrange("p (h q) -> p h q", h=2)
        stg = [work[:, 1024 * i:1024 * i + 1024].rearrange("p (t n) -> p t n", t=T) for i in range(2)]
        junk = work[:, 0:2048]
        g_b = work[:, 2048:3072]
        g_u = work[:, 3072:4096]
        att = work[:, 4096:5120]
        att_x = work[:, 5120:5632]
        g_bias = work[:, 4096:4608]
        g_alpha = work[0:GR, 4608:5120]
        att_junk = work[:, 2048:2304]
        g_e2 = g_b
        sa = [work[:, 2048 + 768 * i:2432 + 768 * i] for i in range(2)]
        sp_ = [work[:, 2432 + 768 * i:2816 + 768 * i] for i in range(2)]
        k_head = [work[:, 3584 + 256 * i:3840 + 256 * i] for i in range(2)]
        s_m = [work[:, 2048 + 384 * i:2432 + 384 * i] for i in range(2)]
        rope_m1 = work[:, 3072:3328]
        rope_m2 = work[:, 3328:3584]
        kr_t = work[0:ROPE, 3584:3840]
        kr_tok = work[:, 3840:3968].rearrange("p (t n) -> p t n", t=T)

        ident = sb("ident", [P, P])
        tri16 = sb("tri16", [P, P])
        neg_tri = sb("neg_tri", [P, P])
        neg_one = sb("neg_one", [P, P])
        idle_p = sb("idle_p", [P, 4])
        masks = sb("masks", [P, 7, P])
        causal = sb("causal", [P, 2 * P])
        gla_g = sb("gla_g", [P, GV])
        gain_rows = work[0:40, 0:P]
        gain_t = sb("gain_t", [P, 40])
        pos_i = sb("pos_i", [P, T], I32)
        pos_f = sb("pos_f", [P, T])
        ang, red, turn = (work[:, 5120 + 128 * i:5248 + 128 * i].rearrange("p (a t c) -> p a t c", a=2, t=T) for i in range(3))
        inv_f = work[:, 5504:5504 + ROPE // 2]
        cos_ = sb("cos_", [P, T, 2, ROPE // 2])
        sin_ = sb("sin_", [P, T, 2, ROPE // 2])
        half = sb("half", [P, 8])
        ssum = sb("ssum", [P, 24])
        rstd = sb("rstd", [P, 24])
        ga_tok = sb("ga_tok", [P, T, GR])
        ga_t = work[0:GR, 2048:2048 + T * P]
        idle = sb("idle", [P, 2])
        mx = sb("mx", [P, 4])
        nmx = sb("nmx", [P, 4])
        rsum = sb("rsum", [P, 4])
        rinv = sb("rinv", [P, 4])

        x_landed = [sem(f"x_landed{n}") for n in range(2 * T)]
        gains_landed, bias_landed, alpha_landed, gla_g_landed = (sem(n) for n in ("gains_landed", "bias_landed", "alpha_landed", "gla_g_landed"))
        pos_landed, fin_landed = sem("pos_landed"), sem("fin_landed")
        raw_landed = [sem(f"raw_landed{s}") for s in range(RAW)]
        hi_ready, lo_ready, piece_used = sem("hi_ready"), sem("lo_ready"), sem("piece_used")
        evac_a, evac_d = sem("evac_a"), sem("evac_d")
        t_done, t_free_a, t_free_d = sem("t_done"), sem("t_free_a"), sem("t_free_d")
        consts, pool_seq = sem("consts"), sem("pool_seq")
        gain_done, gain_ready = sem("gain_done"), sem("gain_ready")
        sq_ready, ms_ready, rstd_ready = sem("sq_ready"), sem("ms_ready"), sem("rstd_ready")
        silu_ready = sem("silu_ready")
        res_added = sem("res_added")
        ga_ready, gat_done, gat_ready, u_done, u_ready = (sem(n) for n in ("ga_ready", "gat_done", "gat_ready", "u_done", "u_ready"))
        ua_ready, ue_ready, g_ready, b_done, b_ready = (sem(n) for n in ("ua_ready", "ue_ready", "g_ready", "b_done", "b_ready"))
        gd_ready, ge_ready, gq_ready, lev_done, lev_copied = (sem(n) for n in ("gd_ready", "ge_ready", "gq_ready", "lev_done", "lev_copied"))
        att_ready, go_done, go_sq, gy_ready, gg_ready = (sem(n) for n in ("att_ready", "go_done", "go_sq", "gy_ready", "gg_ready"))
        sk_ready, sz_done, sabs_ready, sexp_ready, slog_ready, ssp_ready, ssel_ready = (sem(n) for n in ("sk_ready", "sz_done", "sabs_ready", "sexp_ready", "slog_ready", "ssp_ready", "ssel_ready"))
        sarg_done, sw_ready, swm_ready, sy_done, sy_ready = (sem(n) for n in ("sarg_done", "sw_ready", "swm_ready", "sy_done", "sy_ready"))
        ang_ready, trig_ready, rope_tab = sem("ang_ready"), sem("trig_ready"), sem("rope_tab")
        kr_evac, kr_roped, krt_done, krt_ready = (sem(n) for n in ("kr_evac", "kr_roped", "krt_done", "krt_ready"))
        rope_seq, q_roped, qkt_done, qt_ready, kt_ready = (sem(n) for n in ("rope_seq", "q_roped", "qkt_done", "qt_ready", "kt_ready"))
        sc_done, sc_max, nmx_ready, p_ready, rinv_ready, my_done, my_ready = (
            sem(n) for n in ("sc_done", "sc_max", "nmx_ready", "p_ready", "rinv_ready", "my_done", "my_ready"))
        fin_seq, fin_ready, out_written = sem("fin_seq"), sem("fin_ready"), sem("out_written")

        def halves(v, L):
            w = v.rearrange("p (m a l) -> p m a l", a=2, l=L)
            return w[:, :, 0, :], w[:, :, 1, :]

        block = ctx.enter_context(nc.Block())

        @block.sync
        def _(sp):
            def block_of(w, col, b, n=CW, free=True):
                for j in range(NP):
                    if free:
                        sp.wait_ge(lo_ready, b * NP + (j + 1))
                    dst = raw[:, j, 0:PK * n].rearrange("p (k n) -> p k n", k=PK)
                    sp.dma_start(dst, w[:, PK * j:PK * j + PK, bass.ds(col, n)]).then_inc(raw_landed[j], 16)

            block_of(we_d, G_A, None, GR, free=False)
            sp.dma_start(gain_rows[0:16, :], ln_even[0].rearrange("(k p) -> k p", p=P)).then_inc(gains_landed, 16)
            sp.dma_start(gain_rows[16:32, :], ln_odd[0].rearrange("(k p) -> k p", p=P)).then_inc(gains_landed, 16)
            sp.dma_start(gain_rows[32:36, :], q_norm[0].rearrange("(k p) -> k p", p=P)).then_inc(gains_landed, 16)
            sp.dma_start(gain_rows[36:40, :], kv_norm[0].rearrange("(k p) -> k p", p=P)).then_inc(gains_landed, 16)
            block_of(we_d, G_QK, B_GQK - 1)
            sp.dma_start(g_bias, gla_alpha_bias.to_broadcast([P, GH * DH])).then_inc(bias_landed, 16)
            sp.dma_start(g_alpha, gla_alpha_up[0]).then_inc(alpha_landed, 16)
            sp.dma_start(gla_g[:, :], gla_norm.to_broadcast([P, GV])).then_inc(gla_g_landed, 16)
            for t in range(T):
                sp.dma_start(pos_i[:, t:t + 1], positions[0, P * t:P * t + P].rearrange("(p a) -> p a", a=1)).then_inc(pos_landed, 16)
            block_of(we_d, G_QK + CW, B_GQK)
            with sp.Fori(0, 4) as i:
                block_of(we_d, i * CW + SB_Q, i + (B_SBQK - 1))
            for kind, col in enumerate((SB_V, G_V)):
                with sp.Fori(0, 2) as i:
                    for e in range(2):
                        block_of(we_d, i * CW + (col + 1024 * e), i * 2 + (B_MIX - 1 + 4 * kind + e))
            with sp.Fori(0, 4) as i:
                block_of(wo0_d, i * CW, i + (B_OUT0 - 1))
            sp.wait_ge(t_done, 2 * U_PREP1)
            sp.dma_start(fin_g, final_norm.rearrange("(a d) -> a d", a=1).to_broadcast([P, D])).then_inc(fin_landed, 16)
            with sp.Fori(0, 2) as i:
                block_of(wi1_d, i * CW, i + (B_LAT - 1))
            block_of(wi1_d, O_KR, B_KR - 1, ROPE)
            with sp.Fori(0, 4) as i:
                block_of(wi1_d, i * CW + O_GATE, i + (B_GATE - 1))
            with sp.Fori(0, PAIRS // 2) as i:
                for e in range(2):
                    for j in range(4):
                        slot = 4 * e + j
                        sp.wait_ge(lo_ready, i * NP + (NP * (B_MLA - 1) + slot + 1))
                        w, n = (wq_d, 2 * QH) if j < 2 else (wkv_d, CW)
                        k = PK * (j % 2)
                        dst = raw[:, slot, 0:PK * n].rearrange("p (k n) -> p k n", k=PK)
                        sp.dma_start(dst, w[:, k:k + PK, bass.ds(i * (2 * n) + e * n, n)]).then_inc(raw_landed[slot], 16)
            with sp.Fori(0, 4) as i:
                block_of(wo1_d, i * CW, i + (B_OUT1 - 1))
            for n in range(2 * T):
                t, hf = n % T, n // T
                sp.wait_ge(fin_ready, n + 1)
                sp.dma_start(out_d[t][:, 1024 * hf:1024 * hf + 1024], xs[:, t, 1024 * hf:1024 * hf + 1024]).then_inc(out_written, 16)
            sp.wait_ge(out_written, 16 * 2 * T)

        @block.gpsimd
        def _(pool):
            g = nc.gpsimd
            seq = [0]

            def step(ins):
                seq[0] += 1
                ins.then_inc(pool_seq, 1)
                pool.wait_ge(pool_seq, seq[0])

            step(g.memset(ident[:, :], 0.0))
            g.affine_select(out=ident[:, :], in_=ident[:, :], compare_op=ALU.not_equal, fill=1.0,
                            base=0, pattern=[[-1, P]], channel_multiplier=1).then_inc(consts, 1)
            g.memset(tri16[:, :], 1.0 / 16.0).then_inc(pool_seq, 1)
            g.memset(neg_tri[:, :], -1.0).then_inc(pool_seq, 1)
            g.memset(neg_one[:, :], -1.0).then_inc(pool_seq, 1)
            g.memset(idle_p[:, :], 0.0).then_inc(pool_seq, 1)
            g.memset(masks[:, :, :], 1.0).then_inc(pool_seq, 1)
            g.memset(causal[:, :], 0.0).then_inc(pool_seq, 1)
            g.memset(half[:, :], -0.5).then_inc(pool_seq, 1)
            seq[0] += 7
            pool.wait_ge(pool_seq, seq[0])
            g.affine_select(out=tri16[:, :], in_=tri16[:, :], compare_op=ALU.is_ge, fill=0.0,
                            base=0, pattern=[[1, P]], channel_multiplier=-1).then_inc(consts, 1)

            ms = [0]

            def inverse_root(a, b, width, count):
                pool.wait_ge(sq_ready, count)
                ms[0] += 1
                g.tensor_scalar(ssum[:, a:b], ssum[:, a:b], 1.0 / width, EPS, ALU.mult, ALU.add).then_inc(ms_ready, 1)
                pool.wait_ge(ms_ready, ms[0])
                g.tensor_tensor(rstd[:, a:b], ssum[:, a:b], half[:, 0:b - a], ALU.pow).then_inc(rstd_ready, 1)

            inverse_root(0, 2, D, 2)
            for m in range(7):
                s = P >> m
                v = masks[:, m, :].rearrange("p (b s) -> p b s", s=s)
                if m:
                    step(g.affine_select(out=v, in_=v, compare_op=ALU.is_ge, fill=0.0, base=0,
                                         pattern=[[-s, P // s], [0, s]], channel_multiplier=1))
                    step(g.affine_select(out=v, in_=v, compare_op=ALU.is_ge, fill=0.0, base=s - 1,
                                         pattern=[[s, P // s], [0, s]], channel_multiplier=-1))
                g.affine_select(out=masks[:, m, :], in_=masks[:, m, :], compare_op=ALU.not_equal, fill=0.0,
                                base=0, pattern=[[-1, P]], channel_multiplier=1).then_inc(consts, 1)
            g.affine_select(out=neg_tri[:, :], in_=neg_tri[:, :], compare_op=ALU.is_ge, fill=0.0,
                            base=0, pattern=[[-1, P]], channel_multiplier=1).then_inc(consts, 1)
            g.affine_select(out=causal[:, P:2 * P], in_=causal[:, P:2 * P], compare_op=ALU.is_ge, fill=NEG,
                            base=0, pattern=[[-1, P]], channel_multiplier=1).then_inc(consts, 1)

            for lev in range(8):
                L = P >> lev
                if lev == 0:
                    pool.wait_ge(b_ready, 2)
                else:
                    pool.wait_ge(lev_done, levels_done(lev))
                (b0, b1), (e0, e1) = halves(g_b, L), halves(g_u, L)
                ref = b0[:, :, L - 1:L].to_broadcast([P, GH * T * P // (2 * L), L])
                g.tensor_tensor(e0, ref, b0, ALU.subtract).then_inc(gd_ready, 1)
                if lev == 0:
                    g.tensor_copy(e1, b1).then_inc(gd_ready, 1)
                else:
                    g.tensor_tensor(e1, b1, ref, ALU.subtract).then_inc(gd_ready, 1)
            pool.wait_ge(lev_copied, levels_done(8))
            v = att.rearrange("p (a q) -> p a q", q=P)
            g.affine_select(out=v, in_=v, compare_op=ALU.is_ge, fill=0.0, base=0,
                            pattern=[[0, T * GH], [1, P]], channel_multiplier=-1).then_inc(att_ready, 1)

            def strictly_before(buf, signal):
                v = buf.rearrange("p (a q) -> p a q", q=P)[:, 0:3:2, :]
                g.affine_select(out=v, in_=v, compare_op=ALU.is_gt, fill=0.0, base=0,
                                pattern=[[0, 2], [1, P]], channel_multiplier=-1).then_inc(signal, 1)

            pool.wait_ge(t_free_a, freed(U_PREPY))
            pool.wait_ge(t_free_d, freed(U_PREPY))
            with pool.Fori(0, SBH // 2) as i:
                for par in range(2):
                    g.tensor_copy(k_head[par], even[:, bass.ds(i * 512 + (2048 + 256 * par), 256)]).then_inc(sk_ready, 1)
                for par in range(2):
                    pool.wait_ge(ssp_ready, i * 2 + (par + 1))
                    g.tensor_tensor(idle_p[:, par:par + 1], idle_p[:, par:par + 1], idle_p[:, par:par + 1], ALU.add)
                    strictly_before(sp_[par], ssel_ready)
                for par in range(2):
                    pool.wait_ge(sw_ready, i * 2 + (par + 1))
                    g.tensor_tensor(idle_p[:, 2 + par:3 + par], idle_p[:, 2 + par:3 + par], idle_p[:, 2 + par:3 + par], ALU.add)
                    strictly_before(sa[par], swm_ready)

            pool.wait_ge(gla_g_landed, 16)
            pool.wait_ge(silu_ready, 4)
            pool.wait_ge(evac_a, 14)
            for t in range(T):
                v = ys[:, t, SBH * DH:].rearrange("p (h e) -> p h e", h=GH)
                g.tensor_tensor(v, v, gla_g[:, :].unsqueeze(1).to_broadcast([P, GH, GV]), ALU.mult).then_inc(gg_ready, 1)
            inverse_root(16, 24, GV, 2 + 8)

            for j, v in enumerate(INV_FREQ):
                ins = g.memset(inv_f[:, j:j + 1], v)
            step(ins)
            pool.wait_ge(pos_landed, 16 * T)
            step(g.tensor_copy(pos_f[:, :], pos_i[:, :]))
            for t in range(T):
                step(g.tensor_scalar(ang[:, 0, t, :], inv_f, pos_f[:, t:t + 1], None, ALU.mult))
                step(g.tensor_copy(ang[:, 1, t, :], ang[:, 0, t, :]))
            step(g.tensor_scalar(red[:, 0, :, :], ang[:, 0, :, :], 1.0 / TWO_PI, 0.0, ALU.mult, ALU.add))
            step(g.tensor_scalar(red[:, 1, :, :], ang[:, 1, :, :], 1.0 / TWO_PI, 0.25, ALU.mult, ALU.add))
            step(g.tensor_scalar(red[:, :, :, :], red[:, :, :, :], MAGIC, None, ALU.add))
            step(g.tensor_scalar(red[:, :, :, :], red[:, :, :, :], -MAGIC, None, ALU.add))
            for c in (C1, C2, C3):
                step(g.tensor_scalar(turn, red[:, :, :, :], c, None, ALU.mult))
                step(g.tensor_tensor(ang[:, :, :, :], ang[:, :, :, :], turn, ALU.subtract))
            step(g.tensor_scalar(ang[:, 1, :, :], ang[:, 1, :, :], np.pi / 2, None, ALU.add))
            seq[0] += 1
            g.tensor_scalar(ang[:, :, :, :], ang[:, :, :, :], 3.1415925, -3.1415925, ALU.min, ALU.max).then_inc(pool_seq, 1)
            pool.wait_ge(pool_seq, seq[0])
            pool.sem_inc(ang_ready, 1)

            def add_residual(c0):
                with pool.Fori(0, 2) as i:
                    for par in range(2):
                        pool.wait_ge(evac_a, i * 2 + (c0 + par + 1))
                        dst = xs[:, 0, bass.ds(i * (2 * CW) + par * CW, CW)]
                        g.tensor_tensor(dst, dst, stg[par][:, 0, :], ALU.add).then_inc(res_added, 1)

            pool.sem_inc(res_added, 2)
            add_residual(C_OUT0)
            pool.wait_ge(trig_ready, 2)
            step(g.tensor_copy(cos_[:, :, 1, :], cos_[:, :, 0, :]))
            step(g.tensor_scalar(sin_[:, :, 0, :], sin_[:, :, 1, :], -1.0, None, ALU.mult))
            inverse_root(2, 4, D, 12)

            def rotate(xv, m1, m2, last):
                c = cos_[:, :, :, :].rearrange("p t a c -> p t (a c)")
                h2 = ROPE // 2
                g.tensor_tensor(m1, xv, c, ALU.mult)
                g.tensor_tensor(m2[:, :, 0:h2], xv[:, :, h2:], sin_[:, :, 0, :], ALU.mult)
                g.tensor_tensor(m2[:, :, h2:], xv[:, :, 0:h2], sin_[:, :, 1, :], ALU.mult).then_inc(rope_seq, 1)
                return lambda: g.tensor_tensor(xv, m1, m2, ALU.add).then_inc(last, 1)

            mm = [(rope_m1[:, 128 * i:128 * i + 128].rearrange("p (t n) -> p t n", t=T),
                   rope_m2[:, 128 * i:128 * i + 128].rearrange("p (t n) -> p t n", t=T)) for i in range(2)]
            pool.wait_ge(kr_evac, 2)
            end = rotate(kr_tok, *mm[0], kr_roped)
            pool.wait_ge(rope_seq, 1)
            end()
            inverse_root(4, 8, LAT, 16)
            with pool.Fori(0, PAIRS) as p:
                pool.wait_ge(evac_a, p * 2 + (C_MLA + 1))
                pool.wait_ge(evac_d, p * 2 + (C_MLA + 1))
                ends = [rotate(q_tok[:, :, QH * h + DH:QH * h + QH], *mm[h], q_roped) for h in range(2)]
                for h in range(2):
                    pool.wait_ge(rope_seq, p * 2 + (2 + h))
                    ends[h]()
            add_residual(C_OUT1)
            inverse_root(8, 10, D, 18)

        @block.scalar
        def _(act):
            a = nc.scalar

            def piece(b, s, w=FULL):
                act.wait_ge(piece_used, b * NP + (s - RING + 1))
                act.wait_ge(raw_landed[s % RAW], b * 16 + (16 if s < RAW else 32))
                a.activation(w_hi[:, s % RING, 0:w], raw[:, s % RAW, 0:w], ACT.Copy).then_inc(hi_ready, 1)

            def ahead(b, this=FULL, following=FULL, pieces=8):
                for k in range(pieces):
                    w = this if k < 4 else following
                    piece(b, 4 + k, w[k % 4] if isinstance(w, tuple) else w)

            def evac(par, c, dst, scale=1.0, func=ACT.Copy, part="even"):
                act.wait_ge(piece_used, pieces_through(c, part))
                a.activation(dst, ps[:, 2 * par, :][:, 0:dst.shape[-1]], func, scale=scale).then_inc(evac_a, 1)

            def prep(u0, kts, gain=None):
                for s in range(kts // 4):
                    for bank in range(2):
                        act.wait_ge(t_done, 2 * (u0 + s) + bank + 1)
                        k = 4 * s + 2 * bank
                        if gain is None:
                            ins = a.activation(a_hi[:, k:k + 2, :], ps[:, 4 + bank, :].rearrange("p (k n) -> p k n", k=2), ACT.Copy)
                        else:
                            for kk in range(2):
                                ins = a.activation(a_hi[:, k + kk, :], ps[:, 4 + bank, 256 * kk:256 * kk + 256], ACT.Copy,
                                                   scale=gain_t[:, gain + k + kk:gain + k + kk + 1])
                        ins.then_inc(t_free_a, 1)

            sq = [0]

            def squares(src, dst, out_):
                if sq[0]:
                    act.wait_ge(sq_ready, sq[0])
                a.activation(out_, src, ACT.Square, accum_out=dst).then_inc(sq_ready, 1)
                sq[0] += 1

            for hf in range(2):
                for t in range(T):
                    act.dma_start(xs[:, t, 1024 * hf:1024 * hf + 1024], x_d[t][:, 1024 * hf:1024 * hf + 1024]).then_inc(x_landed[2 * hf + t], 16)
            a.preload_act_table_set("natural_log_exp_and_others")
            for s in range(RING):
                act.wait_ge(raw_landed[s], 16)
                a.activation(w_hi[:, s, 0:PK * GR], raw[:, s, 0:PK * GR], ACT.Copy).then_inc(hi_ready, 1)
            act.wait_ge(gain_ready, 1)
            prep(U_PREP0, KT, 0)
            ahead(B_GA, this=PK * GR)
            for t in range(T):
                squares(xs[:, t, :], ssum[:, t:t + 1], junk)
            act.wait_ge(rstd_ready, 1)
            r0 = rstd[:, 0:1]

            def level(lev):
                act.wait_ge(gd_ready, 2 * lev + 2)
                a.activation(g_u, g_u, ACT.Exp).then_inc(ge_ready, 1)

            for c in range(C_MIX):
                b, par = B_GQK + c, c % 2
                piece(b, 4)
                if c >= C_SBQK:
                    level(2 * (c - C_SBQK))
                piece(b, 5)
                piece(b, 6)
                piece(b, 7)
                if c >= C_SBQK:
                    level(2 * (c - C_SBQK) + 1)
                for s in range(8, 12):
                    piece(b, s)
                evac(par, c, stg[par][:, 0, :], r0)
                if c == 0:
                    act.wait_ge(ua_ready, 1)
                    a.activation(g_e2, g_e2, ACT.Exp, scale=-1.0).then_inc(ue_ready, 1)
                    act.wait_ge(ue_ready, 1)
                    a.activation(g_e2, g_e2, ACT.Ln, bias=1.0).then_inc(ue_ready, 1)
                if par:
                    for e in range(2):
                        u = U_QK + c - 1 + e
                        act.wait_ge(t_done, 2 * u + 1)
                        dst = gqk_t[:, 4 * e:4 * e + 2, :] if c == 1 else qk_t[:, 4 * (c - 3 + e):4 * (c - 3 + e) + 2, :]
                        scale = SB_SCALE if (c == 3 or c == 1 and e == 0) else 1.0
                        a.activation(dst, ps[:, 4, :].rearrange("p (h q) -> p h q", h=2), ACT.Copy, scale=scale).then_inc(t_free_a, 1)

            with act.Fori(0, SBH // 2) as i:
                ahead(i * 2 + B_MIX)
                evac(0, i * 2 + C_MIX, vals[:, 0, bass.ds(i * CW, CW)], r0)
                a.preload_act_table_set("natural_log_exp_and_others")
                for par in range(2):
                    act.wait_ge(sabs_ready, i * 2 + (par + 1))
                    a.activation(sa[par], sa[par], ACT.Exp, scale=-1.0).then_inc(sexp_ready, 1)
                for par in range(2):
                    act.wait_ge(sexp_ready, i * 2 + (par + 1))
                    a.activation(sa[par], sa[par], ACT.Ln, bias=1.0).then_inc(slog_ready, 1)
                b = i * 2 + (B_MIX + 1)
                for s in (4, 5, 6):
                    piece(b, s)
                for par in range(2):
                    act.wait_ge(sarg_done, i * 2 + (par + 1))
                    a.activation(sa[par], ps[:, 6 + par, 0:384], ACT.Exp).then_inc(sw_ready, 1)
                for s in range(7, 12):
                    piece(b, s)
                evac(1, i * 2 + (C_MIX + 1), ys[:, 0, bass.ds(i * CW, CW)], r0, ACT.Silu)
                act.wait_ge(evac_d, i * 2 + (C_MIX + 2))
                gate = ys[:, 1, bass.ds(i * CW, CW)]
                a.activation(gate, gate, ACT.Silu).then_inc(silu_ready, 1)
            for n in range(8):
                t, h = divmod(n, GH)
                if h % 2 == 0:
                    act.wait_ge(go_done, n // 2 + 1)
                squares(ps[:, 4 + 2 * t + h // 2, 256 * (h % 2):256 * (h % 2) + 256], ssum[:, 16 + n:17 + n], att_junk)
            prep(U_PREPY, KT)

            def out_pair(b, c, i, added, end=False, part="even"):
                for par in range(2):
                    ahead(i * 2 + (b + par), pieces=4 if end and par else 8)
                    act.wait_ge(res_added, i * 2 + (par + 1 + added))
                    evac(par, i * 2 + (c + par), stg[par][:, 0, :], part=part)

            act.wait_ge(ang_ready, 1)
            a.activation(sin_[:, :, 1, :], ang[:, 0, :, :], ACT.Sin).then_inc(trig_ready, 1)
            a.activation(cos_[:, :, 0, :], ang[:, 1, :, :], ACT.Sin).then_inc(trig_ready, 1)
            with act.Fori(0, 2) as i:
                out_pair(B_OUT0, C_OUT0, i, 0)
            prep(U_PREP1, KT, 16)
            act.wait_ge(res_added, 6)
            act.wait_ge(evac_d, C_LAT)
            for k in range(4):
                piece(B_LAT, 4 + k)
            for t in range(T):
                squares(xs[:, t, :], ssum[:, 2 + t:3 + t], junk)
            for k in range(4):
                piece(B_LAT, 8 + k)
            act.wait_ge(rstd_ready, 3)
            r1 = rstd[:, 2:3]
            evac(0, C_LAT, lat[:, 0, 0:CW], r1)
            ahead(B_LAT + 1, following=PK * ROPE)
            evac(1, C_LAT + 1, lat[:, 0, CW:2 * CW], r1)
            ahead(B_KR, this=PK * ROPE)
            for n in range(4):
                kind, t = divmod(n, T)
                if n == 0:
                    act.wait_ge(evac_a, C_GATE)
                    act.wait_ge(evac_d, C_GATE)
                squares(lat[:, t, CW * kind:CW * kind + CW], ssum[:, 4 + n:5 + n], junk[:, 0:CW])

            def gate_pair(i, final):
                for par in range(2):
                    ahead(i * 2 + (B_GATE + par), following=UP if final and par else FULL)
                    c = i * 2 + (C_GATE + par)
                    cols = bass.ds(i * (2 * CW) + CW * par, CW)
                    evac(par, c, ys[:, 0, cols], r1, ACT.Silu, part="gate")
                    act.wait_ge(evac_d, c + 1)
                    a.activation(ys[:, 1, cols], ys[:, 1, cols], ACT.Silu).then_inc(silu_ready, 1)

            gate_pair(0, False)
            gate_pair(1, True)
            prep(U_LAT, 8, 32)
            act.wait_ge(krt_done, 1)
            a.activation(kr_t, ps[0:ROPE, 6, 0:T * P], ACT.Copy).then_inc(krt_ready, 1)
            act.wait_ge(rstd_ready, 4)

            def pair_of(i, par, first=False, last=False):
                p = i * 2 + par
                nxt = (FULL,) * 4 if last else UP

                def up_piece(k):
                    act.wait_ge(piece_used, p * 4 + (NP * B_MLA + 4 + k - (RING - 1)))
                    s = 4 * (1 - par) + k
                    act.wait_ge(raw_landed[s], i * 16 + (16 * (B_MLA + 1) + (16 if par else 0)))
                    a.activation(w_hi[:, k, 0:nxt[k]], raw[:, s, 0:nxt[k]], ACT.Copy).then_inc(hi_ready, 1)

                evac(0, p * 2 + C_MLA, q_tok[:, 0, :], rstd[:, 4:5], part="up")
                up_piece(0)
                evac(1, p * 2 + (C_MLA + 1), kv_tok[par][:, 0, :], rstd[:, 6:7], part="up")
                if not first:
                    weights_out(p)
                act.wait_ge(qkt_done, p * 3 + 1)
                a.activation(qn_t, ps[:, 0, :], ACT.Copy).then_inc(qt_ready, 1)
                act.wait_ge(qkt_done, p * 3 + 2)
                a.activation(qr_t[0:ROPE, :], ps[0:ROPE, 1, :], ACT.Copy).then_inc(qt_ready, 1)
                up_piece(1)
                up_piece(2)
                act.wait_ge(nmx_ready, p + 1)
                for h in range(2):
                    for t in range(T):
                        cols = (slice(0, P), slice(P, 384))[t]
                        j = 2 * h + t
                        a.activation(s_m[h][:, cols], s_m[h][:, cols], ACT.Exp, bias=nmx[:, j:j + 1], scale=MLA_SCALE,
                                     accum_out=rsum[:, j:j + 1]).then_inc(p_ready, 1)
                up_piece(3)

            def weights_out(p):
                act.wait_ge(t_done, p * 2 + (2 * (U_MLA - 1) + 1))
                a.activation(p_t[:, 0, :], ps[:, 4, 0:384], ACT.Copy).then_inc(t_free_a, 1)

            pair_of(0, 0, first=True)
            with act.Fori(0, PAIRS // 2 - 1) as i:
                pair_of(i, 1)
                pair_of(i + 1, 0)
            pair_of(PAIRS // 2 - 1, 1, last=True)
            weights_out(PAIRS)
            prep(U_PREPZ, KT)
            out_pair(B_OUT1, C_OUT1, 0, 4, part="out")
            out_pair(B_OUT1, C_OUT1, 1, 4, end=True, part="out")
            act.wait_ge(res_added, 10)
            act.wait_ge(evac_d, C_OUT1 + 4)
            for t in range(T):
                squares(xs[:, t, :], ssum[:, 8 + t:9 + t], junk)

        @block.vector
        def _(dve):
            v = nc.vector

            def piece(b, s, w=FULL):
                dve.wait_ge(hi_ready, b * NP + (s + 1))
                v.tensor_tensor(w_lo[:, s % RING, 0:w], raw[:, s % RAW, 0:w], w_hi[:, s % RING, 0:w].bitcast(F32),
                                ALU.subtract).then_inc(lo_ready, 1)

            def ahead(b, this=FULL, following=FULL, pieces=8):
                for k in range(pieces):
                    w = this if k < 4 else following
                    piece(b, 4 + k, w[k % 4] if isinstance(w, tuple) else w)

            def evac(par, c, dst, scale, part="even"):
                dve.wait_ge(piece_used, pieces_through(c, part))
                v.tensor_scalar(dst, ps[:, 2 * par + 1, :][:, 0:dst.shape[-1]], scale, None, ALU.mult).then_inc(evac_d, 1)

            def prep(u0, kts, gain=None):
                for s in range(kts // 4):
                    for bank in range(2):
                        k = 4 * s + 2 * bank
                        dve.wait_ge(t_free_a, freed(u0) + 2 * s + bank + 1)
                        if gain is None:
                            ins = v.tensor_tensor(a_lo[:, k:k + 2, :], ps[:, 4 + bank, :].rearrange("p (k n) -> p k n", k=2),
                                                  a_hi[:, k:k + 2, :].bitcast(F32), ALU.subtract)
                        else:
                            for kk in range(2):
                                ins = v.scalar_tensor_tensor(
                                    out=a_lo[:, k + kk, :], in0=ps[:, 4 + bank, 256 * kk:256 * kk + 256],
                                    scalar=gain_t[:, gain + k + kk:gain + k + kk + 1],
                                    in1=a_hi[:, k + kk, :].bitcast(F32), op0=ALU.mult, op1=ALU.subtract)
                        ins.then_inc(t_free_d, 1)

            dve.wait_ge(gain_done, 1)
            v.tensor_copy(gain_t[:, :], ps[:, 6, 0:40]).then_inc(gain_ready, 1)
            for s in range(RING):
                piece(0, s, PK * GR)
            dve.wait_ge(gain_ready, 1)
            prep(U_PREP0, KT, 0)
            ahead(B_GA, this=PK * GR)
            r0, r1 = rstd[:, 0:1], rstd[:, 1:2]

            def decayed(lev):
                L = P >> lev
                e0, e1 = halves(g_u, L)
                q1, k0 = halves(even[:, 4096:5120], L)[1], halves(even[:, 5120:6144], L)[0]
                dve.wait_ge(ge_ready, lev + 1)
                v.scalar_tensor_tensor(out=e1, in0=e1, scalar=1.0, in1=q1, op0=ALU.min, op1=ALU.mult).then_inc(gq_ready, 1)
                v.scalar_tensor_tensor(out=e0, in0=e0, scalar=1.0, in1=k0, op0=ALU.min, op1=ALU.mult).then_inc(gq_ready, 1)

            def copied(lev):
                if lev == 0:
                    for n, (bank, dst) in enumerate(((6, att_x), (7, att[:, 0:512]), (5, att[:, 512:1024]))):
                        dve.wait_ge(lev_done, n + 1)
                        v.tensor_copy(dst, ps[:, bank, :]).then_inc(lev_copied, 1)
                    return
                dve.wait_ge(consts, 9)
                for bank in range(2):
                    dve.wait_ge(lev_done, levels_done(lev) + bank + 1)
                    dve.wait_ge(lev_copied, levels_done(lev) + bank)
                    v.copy_predicated(att[:, 512 * bank:512 * bank + 512].rearrange("p (h q) -> p h q", h=GH),
                                      masks[:, lev - 1, :].bitcast(I32).unsqueeze(1).to_broadcast([P, GH, P]),
                                      ps[:, 6 + bank, :].rearrange("p (h q) -> p h q", h=GH)).then_inc(lev_copied, 1)

            for c in range(C_MIX):
                b, par = B_GQK + c, c % 2
                mixed = c >= C_SBQK
                lev = 2 * (c - C_SBQK)
                piece(b, 4)
                if c == C_SBQK:
                    dve.wait_ge(t_free_a, freed(U_QK + 2))
                    dve.wait_ge(t_free_d, freed(U_QK + 2))
                if c == 0:
                    dve.wait_ge(rstd_ready, 1)
                    dve.wait_ge(piece_used, NP)
                    v.tensor_scalar(ga_tok[:, 0, :], ps[:, 6, 0:GR], r0, None, ALU.mult).then_inc(ga_ready, 1)
                    v.tensor_scalar(ga_tok[:, 1, :], ps[:, 7, 0:GR], r1, None, ALU.mult).then_inc(ga_ready, 1)
                if mixed:
                    decayed(lev)
                piece(b, 5)
                piece(b, 6)
                if c == 0:
                    dve.wait_ge(gat_done, 1)
                    v.tensor_copy(ga_t, ps[0:GR, 7, 0:T * P]).then_inc(gat_ready, 1)
                if c == 1:
                    for bank in range(2):
                        dve.wait_ge(b_done, bank + 1)
                        v.tensor_copy(g_b[:, 512 * bank:512 * bank + 512], ps[:, 6 + bank, :]).then_inc(b_ready, 1)
                if mixed:
                    copied(lev)
                piece(b, 7)
                piece(b, 8)
                if mixed:
                    decayed(lev + 1)
                for s in range(9, 12):
                    piece(b, s)
                evac(par, c, stg[par][:, 1, :], r1)
                if c == 0:
                    dve.wait_ge(bias_landed, 16)
                    for t in range(T):
                        dve.wait_ge(u_done, t + 1)
                        v.tensor_tensor(g_u[:, 512 * t:512 * t + 512], ps[:, 6 + t, :], g_bias, ALU.add).then_inc(u_ready, 1)
                    dve.wait_ge(u_ready, 2)
                    v.tensor_scalar(g_e2.bitcast(I32), g_u.bitcast(I32), ABS, None, ALU.bitwise_and).then_inc(ua_ready, 1)
                    dve.wait_ge(ue_ready, 2)
                    v.scalar_tensor_tensor(out=g_u, in0=g_u, scalar=0.0, in1=g_e2, op0=ALU.min, op1=ALU.subtract).then_inc(g_ready, 1)
                if mixed:
                    copied(lev + 1)
                if par:
                    for e in range(2):
                        u = U_QK + c - 1 + e
                        dve.wait_ge(t_done, 2 * u + 2)
                        dst = gqk_t[:, 4 * e + 2:4 * e + 4, :] if c == 1 else qk_t[:, 4 * (c - 3 + e) + 2:4 * (c - 3 + e) + 4, :]
                        scale = SB_SCALE if (c == 3 or c == 1 and e == 0) else 1.0
                        v.tensor_scalar(dst, ps[:, 5, :].rearrange("p (h q) -> p h q", h=2), scale, None, ALU.mult).then_inc(t_free_d, 1)

            dve.sem_inc(sy_ready, 2)
            dve.wait_ge(att_ready, 1)
            with dve.Fori(0, SBH // 2) as i:
                ahead(i * 2 + B_MIX)
                evac(0, i * 2 + C_MIX, vals[:, 1, bass.ds(i * CW, CW)], r1)
                for par in range(2):
                    dve.wait_ge(sz_done, i * 2 + (par + 1))
                    v.tensor_scalar(sa[par].bitcast(I32), ps[:, 6 + par, 0:384].bitcast(I32), ABS, None, ALU.bitwise_and).then_inc(sabs_ready, 1)
                for par in range(2):
                    dve.wait_ge(slog_ready, i * 2 + (par + 1))
                    v.scalar_tensor_tensor(out=sp_[par], in0=ps[:, 6 + par, 0:384], scalar=0.0, in1=sa[par],
                                           op0=ALU.max, op1=ALU.add).then_inc(ssp_ready, 1)
                ahead(i * 2 + (B_MIX + 1))
                evac(1, i * 2 + (C_MIX + 1), ys[:, 1, bass.ds(i * CW, CW)], r1)
                if True:
                    dve.wait_ge(silu_ready, i + 1)
                    dve.wait_ge(evac_a, i * 2 + (C_MIX + 2))
                for par in range(2):
                    dve.wait_ge(sy_done, i * 2 + (par + 1))
                    y = ys[:, :, bass.ds(i * (2 * DH) + par * DH, DH)]
                    v.tensor_tensor(y, y, ps[:, 4 + par, 0:T * DH].rearrange("p (t e) -> p t e", t=T), ALU.mult).then_inc(sy_ready, 1)
            dve.wait_ge(rstd_ready, 2)
            dve.wait_ge(gg_ready, 2)
            for n in range(8):
                t, h = divmod(n, GH)
                y = ys[:, t, SBH * DH + GV * h:SBH * DH + GV * h + GV]
                v.scalar_tensor_tensor(out=y, in0=ps[:, 4 + 2 * t + h // 2, GV * (h % 2):GV * (h % 2) + GV],
                                       scalar=rstd[:, 16 + n:17 + n], in1=y, op0=ALU.mult, op1=ALU.mult).then_inc(gy_ready, 1)
            prep(U_PREPY, KT)

            def out_pair(b, c, i, end=False, part="even"):
                for par in range(2):
                    ahead(i * 2 + (b + par), pieces=4 if end and par else 8)
                    dve.wait_ge(piece_used, pieces_through(i * 2 + (c + par), part))
                    dst = xs[:, 1, bass.ds(i * (2 * CW) + par * CW, CW)]
                    v.tensor_tensor(dst, dst, ps[:, 2 * par + 1, :], ALU.add).then_inc(evac_d, 1)

            with dve.Fori(0, 2) as i:
                out_pair(B_OUT0, C_OUT0, i)
            prep(U_PREP1, KT, 16)
            r1 = rstd[:, 3:4]
            ahead(B_LAT)
            dve.wait_ge(rstd_ready, 3)
            evac(0, C_LAT, lat[:, 1, 0:CW], r1)
            ahead(B_LAT + 1, following=PK * ROPE)
            evac(1, C_LAT + 1, lat[:, 1, CW:2 * CW], r1)
            ahead(B_KR, this=PK * ROPE)
            dve.wait_ge(piece_used, NP * (B_KR + 1))
            for t in range(T):
                v.tensor_scalar(kr_tok[:, t, :], ps[:, 6 + t, 0:ROPE], rstd[:, 2 + t:3 + t], None, ALU.mult).then_inc(kr_evac, 1)

            def gate_pair(i, final):
                for par in range(2):
                    ahead(i * 2 + (B_GATE + par), following=UP if final and par else FULL)
                    evac(par, i * 2 + (C_GATE + par), ys[:, 1, bass.ds(i * (2 * CW) + CW * par, CW)], r1, part="gate")

            gate_pair(0, False)
            gate_pair(1, True)
            prep(U_LAT, 8, 32)
            dve.wait_ge(rstd_ready, 4)

            def weighted(i, par):
                dve.wait_ge(my_done, i * 4 + (2 * par + 2))
                for h in range(2):
                    for t in range(T):
                        y = ys[:, t, bass.ds(i * (4 * DH) + (2 * par + h) * DH, DH)]
                        v.scalar_tensor_tensor(out=y, in0=ps[:, 6, (2 * h + t) * DH:(2 * h + t + 1) * DH],
                                               scalar=rinv[:, 2 * h + t:2 * h + t + 1], in1=y,
                                               op0=ALU.mult, op1=ALU.mult).then_inc(my_ready, 1)

            def weights_out(p):
                dve.wait_ge(p_ready, p * 4)
                v.reciprocal(rinv[:, :], rsum[:, :]).then_inc(rinv_ready, 1)
                dve.wait_ge(t_done, p * 2 + (2 * (U_MLA - 1) + 2))
                v.tensor_copy(p_t[:, 1, :], ps[:, 5, 0:384]).then_inc(t_free_d, 1)

            def pair_of(i, par, first=False, last=False):
                p = i * 2 + par
                nxt = (FULL,) * 4 if last else UP

                def up_piece(k):
                    dve.wait_ge(hi_ready, p * 4 + (NP * B_MLA + 5 + k))
                    v.tensor_tensor(w_lo[:, k, 0:nxt[k]], raw[:, 4 * (1 - par) + k, 0:nxt[k]],
                                    w_hi[:, k, 0:nxt[k]].bitcast(F32), ALU.subtract).then_inc(lo_ready, 1)

                evac(0, p * 2 + C_MLA, q_tok[:, 1, :], rstd[:, 5:6], part="up")
                up_piece(0)
                evac(1, p * 2 + (C_MLA + 1), kv_tok[par][:, 1, :], rstd[:, 7:8], part="up")
                if not first:
                    weights_out(p)
                dve.wait_ge(qkt_done, p * 3 + 3)
                v.tensor_copy(kn_t, ps[:, 2, :]).then_inc(kt_ready, 1)
                up_piece(1)
                if not first:
                    dve.wait_ge(rinv_ready, p)
                    weighted(*((i, 0) if par else (i - 1, 1)))
                up_piece(2)
                for h in range(2):
                    dve.wait_ge(sc_done, p * 2 + (h + 1))
                    v.memset(idle[:, h:h + 1], 0.0)
                    for t in range(T):
                        cols = (slice(0, P), slice(P, 384))[t]
                        v.tensor_tensor_reduce(s_m[h][:, cols], ps[:, 6 + h, cols], causal[:, P if t == 0 else 0:2 * P],
                                               1.0, -3.0e38, ALU.add, ALU.max, mx[:, 2 * h + t:2 * h + t + 1]).then_inc(sc_max, 1)
                dve.wait_ge(sc_max, p * 4 + 4)
                v.tensor_scalar(nmx[:, :], mx[:, :], -MLA_SCALE, None, ALU.mult).then_inc(nmx_ready, 1)
                up_piece(3)

            dve.wait_ge(consts, 11)
            pair_of(0, 0, first=True)
            with dve.Fori(0, PAIRS // 2 - 1) as i:
                pair_of(i, 1)
                pair_of(i + 1, 0)
            pair_of(PAIRS // 2 - 1, 1, last=True)
            weights_out(PAIRS)
            dve.wait_ge(rinv_ready, PAIRS)
            weighted(PAIRS // 2 - 1, 1)
            prep(U_PREPZ, KT)
            out_pair(B_OUT1, C_OUT1, 0, part="out")
            out_pair(B_OUT1, C_OUT1, 1, end=True, part="out")
            dve.wait_ge(rstd_ready, 5)
            dve.wait_ge(fin_landed, 16)
            for n in range(2 * T):
                t, hf = n % T, n // T
                y = xs[:, t, 1024 * hf:1024 * hf + 1024]
                v.scalar_tensor_tensor(out=y, in0=y, scalar=rstd[:, 8 + t:9 + t], in1=fin_g[:, 1024 * hf:1024 * hf + 1024],
                                       op0=ALU.mult, op1=ALU.mult).then_inc(fin_ready, 1)

        @block.tensor
        def _(pe):
            m = nc.tensor

            def project(n0, c, par, wait=True, tiles=NP, k0=0, s0=0, n=CW, before=None):
                if wait:
                    pe.wait_ge(evac_a, c - 1)
                    pe.wait_ge(evac_d, c - 1)
                for j in range(tiles):
                    if before:
                        before(j)
                    s = (s0 + j) % RING
                    pe.wait_ge(lo_ready, n0 + (j + 1))
                    for kk in range(PK):
                        k = k0 + PK * j + kk
                        hi, lo = w_hi[:, s, kk * n:kk * n + n], w_lo[:, s, kk * n:kk * n + n]
                        first, last = j == 0 and kk == 0, j == tiles - 1 and kk == PK - 1
                        for t in range(T):
                            acc = ps[:, 2 * par + t, 0:n]
                            tok = slice(t * P, t * P + P)
                            m.matmul(acc, a_hi[:, k, tok], hi, start=first, stop=False)
                            m.matmul(acc, a_hi[:, k, tok], lo, start=False, stop=False)
                            ins = m.matmul(acc, a_lo[:, k, tok], hi, start=False, stop=last)
                    ins.then_inc(piece_used, 1)

            def at_half(fn):
                return lambda j: fn() if j == NP // 2 else None

            def step_free(u):
                pe.wait_ge(t_free_a, freed(u))
                pe.wait_ge(t_free_d, freed(u))

            def transpose_step(u, s, src):
                step_free(u)
                for bank in range(2):
                    for kk in range(2):
                        k = 4 * s + 2 * bank + kk
                        for t in range(T):
                            ins = m.transpose(ps[:, 4 + bank, 256 * kk + P * t:256 * kk + P * t + P],
                                              src[:, t, P * k:P * k + P], ident[:, :])
                    ins.then_inc(t_done, 1)

            def prepared(u0, src, ready=None):
                def before(j):
                    if j % 2:
                        return
                    for s in ((0, 1) if j == 0 else (j // 2 + 1,)):
                        if s < KT // 4:
                            if ready:
                                ready(s)
                            transpose_step(u0 + s, s, src)
                    pe.wait_ge(t_free_d, freed(u0) + j + 2)
                return before

            pe.wait_ge(consts, 1)
            pe.wait_ge(gains_landed, 64)
            m.transpose(ps[:, 6, 0:40], gain_rows, ident[0:40, 0:40]).then_inc(gain_done, 1)
            pe.wait_ge(gain_ready, 1)

            def x_ready(s):
                for t in range(T):
                    pe.wait_ge(x_landed[2 * (s // 2) + t], 16)

            project(0, None, 3, wait=False, n=GR, before=prepared(U_PREP0, xs, x_ready))

            def heads_transposed(c, par, u):
                pe.wait_ge(evac_a, c + 1)
                pe.wait_ge(evac_d, c + 1)
                step_free(u)
                for bank in range(2):
                    for kk in range(2):
                        for t in range(T):
                            blk = 2 * bank + kk
                            ins = m.transpose(ps[:, 4 + bank, 256 * kk + P * t:256 * kk + P * t + P],
                                              stg[par][:, t, P * blk:P * blk + P], ident[:, :])
                    ins.then_inc(t_done, 1)

            def gates_transposed():
                pe.wait_ge(ga_ready, 2)
                for t in range(T):
                    ins = m.transpose(ps[0:GR, 7, P * t:P * t + P], ga_tok[:, t, :], ident[:, :])
                ins.then_inc(gat_done, 1)

            def gates_up():
                pe.wait_ge(gat_ready, 1)
                pe.wait_ge(alpha_landed, 16)
                for t in range(T):
                    m.matmul(ps[:, 6 + t, :], ga_t[:, P * t:P * t + P], g_alpha, start=True, stop=True).then_inc(u_done, 1)

            def gates_summed():
                pe.wait_ge(g_ready, 1)
                pe.wait_ge(consts, 2)
                for h in range(GH):
                    for t in range(T):
                        ins = m.matmul(ps[:, 6 + h // 2, 256 * (h % 2) + P * t:256 * (h % 2) + P * t + P],
                                       g_u[:, 512 * t + DH * h:512 * t + DH * h + DH], tri16[:, :], start=True, stop=True)
                    if h % 2:
                        ins.then_inc(b_done, 1)

            def level(lev):
                pe.wait_ge(gq_ready, 2 * lev + 2)
                if lev == 0:
                    step_free(U_QK + 2)
                    for h in range(GH):
                        ins = m.matmul(ps[:, 6, P * h:P * h + P], g_u[:, 256 * h:256 * h + P], g_u[:, 256 * h + P:256 * h + 256],
                                       start=True, stop=True)
                    ins.then_inc(lev_done, 1)
                    for t in range(T):
                        for h in range(GH):
                            o = 256 * h + P * t
                            ins = m.matmul(ps[:, 7 - 2 * t, P * h:P * h + P], even[:, 5120 + o:5120 + o + P],
                                           even[:, 4096 + o:4096 + o + P], start=True, stop=True)
                        ins.then_inc(lev_done, 1)
                    return
                pe.wait_ge(lev_copied, levels_done(lev))
                for t in range(T):
                    for h in range(GH):
                        o = 256 * h + P * t
                        ins = m.matmul(ps[:, 6 + t, P * h:P * h + P], g_u[:, o:o + P], g_u[:, o:o + P], start=True, stop=True)
                    ins.then_inc(lev_done, 1)

            for c in range(C_MIX):
                par = c % 2
                lev = 2 * (c - C_SBQK)
                middle = (gates_transposed, gates_summed)[c] if c < C_SBQK else (lambda: level(lev))
                project(NP * (B_GQK + c), c, par, wait=c >= 2, before=at_half(middle))
                if c == 0:
                    gates_up()
                if c >= C_SBQK:
                    level(lev + 1)
                if par:
                    for e in range(2):
                        heads_transposed(c - 1 + e, e, U_QK + c - 1 + e)

            pe.wait_ge(consts, 11)
            pe.wait_ge(lev_copied, levels_done(8))
            with pe.Fori(0, SBH // 2) as i:
                project(i * (2 * NP) + NP * B_MIX, i * 2 + C_MIX, 0)
                for par in range(2):
                    pe.wait_ge(sk_ready, i * 2 + (par + 1))
                    qh, z = i * 512 + 256 * par, ps[:, 6 + par, :]
                    m.matmul(z[:, 0:256], k_head[par][:, 0:P], even[:, bass.ds(qh, 256)], start=True, stop=True)
                    m.matmul(z[:, 256:384], k_head[par][:, P:2 * P], even[:, bass.ds(qh + P, P)], start=False, stop=True,
                             skip_group_check=True).then_inc(sz_done, 1)

                def later_keys():
                    for par in range(2):
                        pe.wait_ge(ssel_ready, i * 2 + (par + 1))
                        z, s = ps[:, 6 + par, :], sp_[par]
                        m.matmul(z[:, 0:256], neg_tri[:, :], s[:, 0:256], start=False, stop=False, skip_group_check=True)
                        m.matmul(z[:, P:256], neg_one[:, :], s[:, 256:384], start=False, stop=False, skip_group_check=True)
                        m.matmul(z[:, 256:384], neg_tri[:, :], s[:, 256:384], start=False, stop=True,
                                 skip_group_check=True).then_inc(sarg_done, 1)

                project(i * (2 * NP) + NP * (B_MIX + 1), i * 2 + (C_MIX + 1), 1, before=at_half(later_keys))
                for par in range(2):
                    pe.wait_ge(swm_ready, i * 2 + (par + 1))
                    pe.wait_ge(sy_ready, i * 2 + (par + 1))
                    pe.wait_ge(evac_d, i * 2 + (C_MIX + 1))
                    w, o = sa[par], ps[:, 4 + par, :]
                    hc = bass.ds(i * (2 * DH) + DH * par, DH)
                    m.matmul(o[:, 0:DH], w[:, 0:P], vals[:, 0, hc], start=True, stop=True)
                    m.matmul(o[:, DH:2 * DH], w[:, P:256], vals[:, 0, hc], start=True, stop=False)
                    m.matmul(o[:, DH:2 * DH], w[:, 256:384], vals[:, 1, hc], start=False, stop=True).then_inc(sy_done, 1)

            pe.wait_ge(att_ready, 1)
            pe.wait_ge(sy_ready, SBH + 2)
            for t in range(T):
                for h in range(GH):
                    o = ps[:, 4 + 2 * t + h // 2, GV * (h % 2):GV * (h % 2) + GV]
                    vc = slice(SBH * DH + GV * h, SBH * DH + GV * h + GV)
                    if t:
                        m.matmul(o, att_x[:, P * h:P * h + P], vals[:, 0, vc], start=True, stop=False)
                    ins = m.matmul(o, att[:, 512 * t + P * h:512 * t + P * h + P], vals[:, t, vc],
                                   start=t == 0, stop=True)
                    if h % 2:
                        ins.then_inc(go_done, 1)
            pe.wait_ge(gy_ready, 8)

            def out_projection(b, c, u, src):
                for par in range(2):
                    project(NP * (b + par), c + par, par, before=prepared(u, src) if par == 0 else None)
                for par in range(2):
                    project(NP * (b + 2 + par), c + 2 + par, par)

            out_projection(B_OUT0, C_OUT0, U_PREPY, ys)

            def x1_ready(s):
                pe.wait_ge(res_added, s + 3)
                pe.wait_ge(evac_d, C_OUT0 + s + 1)

            for par in range(2):
                project(NP * (B_LAT + par), C_LAT + par, par, before=prepared(U_PREP1, xs, x1_ready) if par == 0 else None)
            project(NP * B_KR, None, 3, wait=False, n=ROPE)
            with pe.Fori(0, 2) as i:
                for par in range(2):
                    project(i * (2 * NP) + NP * (B_GATE + par), i * 2 + (C_GATE + par), par)
            for s in range(2):
                transpose_step(U_LAT + s, s, lat)
            pe.wait_ge(kr_roped, 1)
            for t in range(T):
                ins = m.transpose(ps[0:ROPE, 6, P * t:P * t + P], kr_tok[:, t, :], ident[:, :])
            ins.then_inc(krt_done, 1)
            step_free(U_MLA)

            def projections(i, par):
                p = i * 2 + par
                for kind in range(2):
                    project(p * 4 + (NP * B_MLA + 2 * kind), p * 2 + (C_MLA + kind), kind, tiles=2, k0=4 * kind, s0=2 * kind,
                            n=2 * QH if kind == 0 else CW)

            def weights_transposed(i, par):
                p = i * 2 + par
                pe.wait_ge(p_ready, p * 4 + 4)
                pe.wait_ge(t_free_a, p + freed(U_MLA))
                pe.wait_ge(t_free_d, p + freed(U_MLA))
                for h in range(2):
                    for c in range(3):
                        ins = m.transpose(ps[:, 4 + h, P * c:P * c + P], s_m[h][:, P * c:P * c + P], ident[:, :])
                    ins.then_inc(t_done, 1)

            def operands_transposed(i, par):
                p = i * 2 + par
                pe.wait_ge(q_roped, p * 2 + 2)
                for bank, wide in ((0, DH), (1, ROPE)):
                    for h in range(2):
                        for t in range(T):
                            q0 = QH * h + (0 if bank == 0 else DH)
                            ins = m.transpose(ps[0:wide, bank, 256 * h + P * t:256 * h + P * t + P], q_tok[:, t, q0:q0 + wide], ident[:, :])
                    ins.then_inc(qkt_done, 1)
                pe.wait_ge(evac_a, p * 2 + (C_MLA + 2))
                pe.wait_ge(evac_d, p * 2 + (C_MLA + 2))
                for h in range(2):
                    for t in range(T):
                        ins = m.transpose(ps[:, 2, 256 * h + P * t:256 * h + P * t + P], kv_tok[par][:, t, 2 * DH * h:2 * DH * h + DH], ident[:, :])
                ins.then_inc(qkt_done, 1)

            def values_mixed(i, par):
                p = i * 2 + par
                for h in range(2):
                    if h == 0:
                        pe.wait_ge(t_free_a, p + (freed(U_MLA) + 1))
                    else:
                        pe.wait_ge(t_free_d, p + (freed(U_MLA) + 1))
                    o = ps[:, 6, 2 * DH * h:2 * DH * h + 2 * DH]
                    vh = slice(2 * DH * h + DH, 2 * DH * h + 2 * DH)
                    m.matmul(o[:, 0:DH], p_t[:, h, 0:P], kv_tok[par][:, 0, vh], start=True, stop=True)
                    m.matmul(o[:, DH:2 * DH], p_t[:, h, P:2 * P], kv_tok[par][:, 0, vh], start=True, stop=False)
                    m.matmul(o[:, DH:2 * DH], p_t[:, h, 2 * P:3 * P], kv_tok[par][:, 1, vh], start=False, stop=True).then_inc(my_done, 1)

            def scores(i, par, first=False):
                p = i * 2 + par
                pe.wait_ge(qt_ready, p * 2 + 2)
                pe.wait_ge(kt_ready, p + 1)
                for h in range(2):
                    if h == 0 and not first:
                        pe.wait_ge(my_ready, p * 4)
                    for t in range(T):
                        o = ps[:, 6 + h, 0:P] if t == 0 else ps[:, 6 + h, P:384]
                        kc = slice(256 * h, 256 * h + P * (t + 1))
                        m.matmul(o, qn_t[:, 256 * h + P * t:256 * h + P * t + P], kn_t[:, kc], start=True, stop=False)
                        ins = m.matmul(o, qr_t[0:ROPE, 256 * h + P * t:256 * h + P * t + P], kr_t[:, 0:P * (t + 1)],
                                       start=False, stop=True)
                    ins.then_inc(sc_done, 1)

            projections(0, 0)
            operands_transposed(0, 0)
            pe.wait_ge(krt_ready, 1)
            scores(0, 0, first=True)

            def turn_of(i, par, j):
                projections(i, par)
                weights_transposed(j, 1 - par)
                operands_transposed(i, par)
                values_mixed(j, 1 - par)
                scores(i, par)

            with pe.Fori(0, PAIRS // 2 - 1) as i:
                turn_of(i, 1, i)
                turn_of(i + 1, 0, i)
            turn_of(PAIRS // 2 - 1, 1, PAIRS // 2 - 1)
            weights_transposed(PAIRS // 2 - 1, 1)
            values_mixed(PAIRS // 2 - 1, 1)
            pe.wait_ge(my_ready, 4 * PAIRS)
            out_projection(B_OUT1, C_OUT1, U_PREPZ, ys)


_INS = ["x", "positions", "ln_even", "w_in_even", "gla_alpha_up", "gla_alpha_bias", "gla_norm", "w_out_even",
        "ln_odd", "w_in_odd", "q_norm", "w_q_up", "kv_norm", "w_kv_up", "w_out_odd", "final_norm"]


def kernel(**inputs):
    import concourse.bacc as bacc
    from concourse.bass_utils import run_bass_kernel_spmd

    nc = bacc.Bacc("TRN2", target_bir_lowering=False, num_devices=1)
    arrays, args = {}, []
    for name in _INS:
        arr = np.ascontiguousarray(inputs[name])
        arrays[f"in_{name}"] = arr
        args.append(nc.dram_tensor(f"in_{name}", arr.shape, mybir.dt.from_np(arr.dtype), kind="ExternalInput").ap())
    shape = arrays["in_x"].shape
    args.append(nc.dram_tensor("out_0", shape, F32, kind="ExternalOutput").ap())
    build(nc, *args)
    r = run_bass_kernel_spmd(nc, [arrays], core_ids=[0])
    return r.results[0]["out_0"]
```

```python
from contextlib import ExitStack

import numpy as np

import concourse.bass as bass
from concourse import mybir
from concourse.alu_op_type import AluOpType as ALU

ACT = mybir.ActivationFunctionType
F32 = mybir.dt.float32
F32R = mybir.dt.float32r
I32 = mybir.dt.int32

P = 128
D = 2048
T = 2
KT = D // P
CW = 512
PK = 2
NP = KT // PK
RAW = 8
RING = 4
SBH, GH, MH = 8, 4, 16
DH = 128
GV = 256
GR = 16
ROPE = 64
QH = DH + ROPE
LAT = 512
PAIRS = MH // 2
EPS = 1e-6
SB_SCALE = float(DH) ** -0.5
MLA_SCALE = float(QH) ** -0.5
NEG = -1e30
ABS = 0x7FFFFFFF
THETA = 10000.0
TWO_PI = 2 * np.pi
C1 = 6.28125
C2 = float(np.float32(TWO_PI - C1))
C3 = float(np.float32(TWO_PI - C1 - C2))
MAGIC = 12582912.0
INV_FREQ = [float(v) for v in (np.float32(THETA) ** (-np.arange(ROPE // 2, dtype=np.float32) / np.float32(ROPE // 2)))]

SB_Q, SB_V, G_QK, G_V, G_A = 0, 2048, 4096, 5120, 7168
O_KR, O_GATE = 2 * LAT, 2 * LAT + ROPE


B_GQK, B_SBQK, B_MIX, B_OUT0, B_LAT, B_GATE, B_MLA, B_OUT1 = 0, 2, 6, 14, 18, 20, 24, 28
C_GQK, C_SBQK, C_MIX, C_OUT0, C_LAT, C_GATE, C_MLA = 0, 2, 6, 14, 18, 20, 24
C_OUT1 = C_MLA + 2 * PAIRS
QUERIES = (C_GQK, C_SBQK, C_SBQK + 1)
U_PREP0, U_QK, U_PREPY, U_PREP1, U_LAT, U_MLA = 0, 4, 10, 14, 18, 20
U_LAST = U_MLA + PAIRS + 2
STEPS_Z = (U_LAST - 3, U_LAST - 2, U_LAST - 1, U_LAST + 1)
FULL = PK * CW
UP = (PK * 2 * QH, PK * 2 * QH, PK * CW, PK * CW)


def freed(u):
    n = 0
    for first, last, each in ((U_PREP0, U_QK, 2), (U_QK, U_PREPY, 1), (U_PREPY, U_MLA, 2), (U_MLA, U_LAST - 3, 1),
                              (U_LAST - 3, U_LAST, 2), (U_LAST, U_LAST + 1, 1), (U_LAST + 1, 999, 2)):
        n += each * max(0, min(u, last) - first)
    return n


def pieces_through(c, part="even"):
    if part == "up":
        return c * 2 + (NP * B_MLA - 2 * C_MLA + 2)
    b0 = {"even": B_GQK - C_GQK, "gate": B_GATE - C_GATE, "out": B_OUT1 - C_OUT1}[part]
    return c * NP + (NP * b0 + NP)


def steps_from(u):
    return tuple(range(u, u + KT // 4))


def among(prep, extra=None):
    return {0: [lambda: prep(0)], 1: [lambda: prep(1)], 2: [lambda: prep(2)], 4: [lambda: prep(3)], **(extra or {})}


def levels_done(lev):
    return 2 * lev + 1


def build(nc, x, positions, ln_even, w_in_even, gla_alpha_up, gla_alpha_bias, gla_norm, w_out_even,
          ln_odd, w_in_odd, q_norm, w_q_up, kv_norm, w_kv_up, w_out_odd, final_norm, out):
    x_d = x[0].rearrange("(t p) d -> t p d", p=P)
    out_d = out[0].rearrange("(t p) d -> t p d", p=P)

    def by_k(w):
        return w[0].rearrange("(k p) n -> p k n", p=P)

    we_d, wo0_d, wi1_d, wo1_d = by_k(w_in_even), by_k(w_out_even), by_k(w_in_odd), by_k(w_out_odd)
    wq_d, wkv_d = by_k(w_q_up), by_k(w_kv_up)

    with ExitStack() as ctx:
        def sb(name, shape, dt=F32):
            return ctx.enter_context(nc.sbuf_tensor(name, shape, dt))

        def sem(name):
            return ctx.enter_context(nc.semaphore(name))

        ps = ctx.enter_context(nc.psum_tensor("ps", [P, 8, CW], F32))

        raw = sb("raw", [P, RAW, PK * CW])
        w_hi = sb("w_hi", [P, RING, PK * CW], F32R)
        w_lo = sb("w_lo", [P, RING, PK * CW], F32R)
        narrow_hi = sb("narrow_hi", [P, KT * ROPE], F32R)
        narrow_lo = sb("narrow_lo", [P, KT * ROPE], F32R)
        a_hi = sb("a_hi", [P, KT, T * P], F32R)
        a_lo = sb("a_lo", [P, KT, T * P], F32R)
        xs = sb("xs", [P, T, D])
        ys = sb("ys", [P, T, D])
        even = sb("even", [P, 10240])
        work = sb("work", [P, 2048 + 3584])

        qk_t = even[:, 0:4096].rearrange("p (h q) -> p h q", h=2 * SBH)
        gqk_t = even[:, 4096:6144].rearrange("p (h q) -> p h q", h=2 * GH)
        vals = even[:, 6144:10240].rearrange("p (t n) -> p t n", t=T)
        kr_raw = even[:, 5120:6144]
        kr_hi, kr_lo = narrow_hi[:, :], narrow_lo[:, :]
        lat = even[:, 0:2048].rearrange("p (t n) -> p t n", t=T)
        fin_g = even[:, 0:2048]
        q_tok = even[:, 5120:5888].rearrange("p (t n) -> p t n", t=T)
        qn_t = even[:, 5888:6400]
        kn_t = even[:, 6400:6912]
        qr_t = even[:, 6912:7424]
        kv_tok = [even[:, 7424 + 1024 * i:8448 + 1024 * i].rearrange("p (t n) -> p t n", t=T) for i in range(2)]
        p_t = even[:, 9472:10240].rearrange("p (h q) -> p h q", h=2)
        stg = [work[:, 1024 * i:1024 * i + 1024].rearrange("p (t n) -> p t n", t=T) for i in range(2)]
        junk = work[:, 0:2048]
        sq_junk = work[:, 4096:4608]
        ga_raw = work[:, 3072:3072 + KT * GR]
        ga_hi, ga_lo = narrow_hi[:, 0:KT * GR], narrow_lo[:, 0:KT * GR]
        g_b = work[:, 2048:3072]
        g_u = work[:, 3072:4096]
        att = work[:, 4096:5120]
        att_x = work[:, 5120:5632]
        g_bias = work[:, 4096:4608]
        g_alpha = work[0:GR, 4608:5120]
        att_junk = work[:, 2048:2304]
        g_e2 = g_b
        sa = [work[:, 2048 + 768 * i:2432 + 768 * i] for i in range(2)]
        sp_ = [work[:, 2432 + 768 * i:2816 + 768 * i] for i in range(2)]
        k_head = [work[:, 3584 + 256 * i:3840 + 256 * i] for i in range(2)]
        s_m = [work[:, 2048 + 384 * i:2432 + 384 * i] for i in range(2)]
        rope_m1 = work[:, 3072:3328]
        rope_m2 = work[:, 3328:3584]
        kr_t = work[0:ROPE, 3584:3840]
        kr_tok = work[:, 3840:3968].rearrange("p (t n) -> p t n", t=T)

        ident = sb("ident", [P, P])
        tri16 = sb("tri16", [P, P])
        neg_tri = sb("neg_tri", [P, P])
        neg_one = sb("neg_one", [P, P])
        idle_p = sb("idle_p", [P, 4])
        masks = sb("masks", [P, 7, P])
        causal = sb("causal", [P, 2 * P])
        gla_g = sb("gla_g", [P, GV])
        gain_rows = work[0:40, 0:P]
        gain_t = sb("gain_t", [P, 40])
        pos_i = sb("pos_i", [P, T], I32)
        pos_f = sb("pos_f", [P, T])
        ang, red, turn = (work[:, 5120 + 128 * i:5248 + 128 * i].rearrange("p (a t c) -> p a t c", a=2, t=T) for i in range(3))
        inv_f = work[:, 5504:5504 + ROPE // 2]
        cos_ = sb("cos_", [P, T, 2, ROPE // 2])
        sin_ = sb("sin_", [P, T, 2, ROPE // 2])
        half = sb("half", [P, 8])
        ssum = sb("ssum", [P, 40])
        rstd = sb("rstd", [P, 24])
        ga_t = work[0:GR, 2048:2048 + T * P]
        idle = sb("idle", [P, 2])
        mx = sb("mx", [P, 4])
        nmx = sb("nmx", [P, 4])
        rsum = sb("rsum", [P, 4])
        rinv = sb("rinv", [P, 4])

        x_landed = [sem(f"x_landed{n}") for n in range(4 * T)]
        gains_landed, bias_landed, alpha_landed, gla_g_landed = (sem(n) for n in ("gains_landed", "bias_landed", "alpha_landed", "gla_g_landed"))
        pos_landed, fin_landed = sem("pos_landed"), sem("fin_landed")
        raw_landed = [sem(f"raw_landed{s}") for s in range(RAW)]
        hi_ready, lo_ready, piece_used = sem("hi_ready"), sem("lo_ready"), sem("piece_used")
        evac_a, evac_d = sem("evac_a"), sem("evac_d")
        t_done, t_free_a, t_free_d = sem("t_done"), sem("t_free_a"), sem("t_free_d")
        consts, pool_seq = sem("consts"), sem("pool_seq")
        gain_done, gain_ready = sem("gain_done"), sem("gain_ready")
        sq_ready, ms_ready, rstd_ready = sem("sq_ready"), sem("ms_ready"), sem("rstd_ready")
        silu_ready = sem("silu_ready")
        res_added = sem("res_added")
        ga_landed, ga_ready, gat_done, gat_ready, u_done, u_ready = (sem(n) for n in ("ga_landed", "ga_ready", "gat_done", "gat_ready", "u_done", "u_ready"))
        ua_ready, ue_ready, g_ready, b_done, b_ready = (sem(n) for n in ("ua_ready", "ue_ready", "g_ready", "b_done", "b_ready"))
        gd_ready, ge_ready, gq_ready, lev_done, lev_copied = (sem(n) for n in ("gd_ready", "ge_ready", "gq_ready", "lev_done", "lev_copied"))
        att_ready, go_done, gy_ready, gg_ready = (sem(n) for n in ("att_ready", "go_done", "gy_ready", "gg_ready"))
        sk_ready, sz_done, sabs_ready, sexp_ready, slog_ready, ssp_ready, ssel_ready = (sem(n) for n in ("sk_ready", "sz_done", "sabs_ready", "sexp_ready", "slog_ready", "ssp_ready", "ssel_ready"))
        sarg_done, sw_ready, swm_ready, sy_done, sy_ready = (sem(n) for n in ("sarg_done", "sw_ready", "swm_ready", "sy_done", "sy_ready"))
        ang_ready, trig_ready = sem("ang_ready"), sem("trig_ready")
        kr_landed, krw_ready, kr_done, kr_out, kr_back, kr_evac, kr_roped, krt_done, krt_ready = (
            sem(n) for n in ("kr_landed", "krw_ready", "kr_done", "kr_out", "kr_back", "kr_evac", "kr_roped", "krt_done", "krt_ready"))
        rope_seq, q_roped, qkt_done, qt_ready, kt_ready = (sem(n) for n in ("rope_seq", "q_roped", "qkt_done", "qt_ready", "kt_ready"))
        sc_done, sc_max, nmx_ready, p_ready, rinv_ready, my_done, my_ready = (
            sem(n) for n in ("sc_done", "sc_max", "nmx_ready", "p_ready", "rinv_ready", "my_done", "my_ready"))
        res_gained, last_gained, fin_a, fin_d, out_written = (sem(n) for n in ("res_gained", "last_gained", "fin_a", "fin_d", "out_written"))

        def final_pieces(t):
            return xs[:, t, 2 * CW:3 * CW], xs[:, t, 0:2 * CW], stg[1][:, t, :]

        def halves(v, L):
            w = v.rearrange("p (m a l) -> p m a l", a=2, l=L)
            return w[:, :, 0, :], w[:, :, 1, :]

        block = ctx.enter_context(nc.Block())

        @block.sync
        def _(sp):
            def block_of(w, col, b, n=CW):
                for j in range(NP):
                    sp.wait_ge(lo_ready, b * NP + (j + 1))
                    dst = raw[:, j, 0:PK * n].rearrange("p (k n) -> p k n", k=PK)
                    sp.dma_start(dst, w[:, PK * j:PK * j + PK, bass.ds(col, n)]).then_inc(raw_landed[j], 16)

            sp.dma_start(gain_rows[0:16, :], ln_even[0].rearrange("(k p) -> k p", p=P)).then_inc(gains_landed, 16)
            sp.dma_start(gain_rows[16:32, :], ln_odd[0].rearrange("(k p) -> k p", p=P)).then_inc(gains_landed, 16)
            sp.dma_start(gain_rows[32:36, :], q_norm[0].rearrange("(k p) -> k p", p=P)).then_inc(gains_landed, 16)
            sp.dma_start(gain_rows[36:40, :], kv_norm[0].rearrange("(k p) -> k p", p=P)).then_inc(gains_landed, 16)
            for j in range(NP):
                sp.dma_start(raw[:, j, :].rearrange("p (k n) -> p k n", k=PK), we_d[:, PK * j:PK * j + PK, G_QK:G_QK + CW]).then_inc(raw_landed[j], 16)
                if j == 0:
                    sp.dma_start(ga_raw.rearrange("p (k n) -> p k n", k=KT), we_d[:, :, G_A:G_A + GR]).then_inc(ga_landed, 16)
                if j < KT // 4 - 1:
                    cols = slice(CW * (j + 1), CW * (j + 2))
                    for t in range(T):
                        sp.dma_start(xs[:, t, cols], x_d[t][:, cols]).then_inc(x_landed[T * (j + 1) + t], 16)
            for t in range(T):
                sp.dma_start(pos_i[:, t:t + 1], positions[0, P * t:P * t + P].rearrange("(p a) -> p a", a=1)).then_inc(pos_landed, 16)
            sp.dma_start(g_bias, gla_alpha_bias.to_broadcast([P, GH * DH])).then_inc(bias_landed, 16)
            sp.dma_start(g_alpha, gla_alpha_up[0]).then_inc(alpha_landed, 16)
            sp.dma_start(gla_g[:, :], gla_norm.to_broadcast([P, GV])).then_inc(gla_g_landed, 16)
            block_of(we_d, G_QK + CW, B_GQK)
            with sp.Fori(0, 4) as i:
                block_of(we_d, i * CW + SB_Q, i + (B_SBQK - 1))
            for kind, col in enumerate((SB_V, G_V)):
                with sp.Fori(0, 2) as i:
                    for e in range(2):
                        block_of(we_d, i * CW + (col + 1024 * e), i * 2 + (B_MIX - 1 + 4 * kind + e))
            with sp.Fori(0, 4) as i:
                block_of(wo0_d, i * CW, i + (B_OUT0 - 1))
            sp.wait_ge(gy_ready, 8)
            sp.dma_start(kr_raw.rearrange("p (k n) -> p k n", k=KT), wi1_d[:, :, O_KR:O_KR + ROPE]).then_inc(kr_landed, 16)
            with sp.Fori(0, 2) as i:
                block_of(wi1_d, i * CW, i + (B_LAT - 1))
            with sp.Fori(0, 4) as i:
                block_of(wi1_d, i * CW + O_GATE, i + (B_GATE - 1))
            with sp.Fori(0, PAIRS // 2) as i:
                for e in range(2):
                    for j in range(4):
                        slot = 4 * e + j
                        sp.wait_ge(lo_ready, i * NP + (NP * (B_MLA - 1) + slot + 1))
                        w, n = (wq_d, 2 * QH) if j < 2 else (wkv_d, CW)
                        k = PK * (j % 2)
                        dst = raw[:, slot, 0:PK * n].rearrange("p (k n) -> p k n", k=PK)
                        sp.dma_start(dst, w[:, k:k + PK, bass.ds(i * (2 * n) + e * n, n)]).then_inc(raw_landed[slot], 16)
            sp.wait_ge(sq_ready, 22)
            sp.wait_ge(t_done, 2 * (U_LAT + 2))
            sp.dma_start(fin_g, final_norm.rearrange("(a d) -> a d", a=1).to_broadcast([P, D])).then_inc(fin_landed, 16)
            with sp.Fori(0, 4) as i:
                block_of(wo1_d, i * CW, i + (B_OUT1 - 1))
            for n, cols in enumerate((slice(2 * CW, 3 * CW), slice(0, 2 * CW), slice(3 * CW, 4 * CW))):
                for t in range(T):
                    sp.wait_ge(fin_d if t else fin_a, n + 1)
                    sp.dma_start(out_d[t][:, cols], final_pieces(t)[n]).then_inc(out_written, 16)
            sp.wait_ge(out_written, 16 * 3 * T)

        @block.gpsimd
        def _(pool):
            g = nc.gpsimd
            seq = [0]

            def step(ins):
                seq[0] += 1
                ins.then_inc(pool_seq, 1)
                pool.wait_ge(pool_seq, seq[0])

            step(g.memset(ident[:, :], 0.0))
            g.affine_select(out=ident[:, :], in_=ident[:, :], compare_op=ALU.not_equal, fill=1.0,
                            base=0, pattern=[[-1, P]], channel_multiplier=1).then_inc(consts, 1)
            g.memset(tri16[:, :], 1.0 / 16.0).then_inc(pool_seq, 1)
            g.memset(neg_tri[:, :], -1.0).then_inc(pool_seq, 1)
            g.memset(neg_one[:, :], -1.0).then_inc(pool_seq, 1)
            g.memset(idle_p[:, :], 0.0).then_inc(pool_seq, 1)
            g.memset(masks[:, :, :], 1.0).then_inc(pool_seq, 1)
            g.memset(causal[:, :], 0.0).then_inc(pool_seq, 1)
            g.memset(half[:, :], -0.5).then_inc(pool_seq, 1)
            seq[0] += 7
            pool.wait_ge(pool_seq, seq[0])
            g.affine_select(out=tri16[:, :], in_=tri16[:, :], compare_op=ALU.is_ge, fill=0.0,
                            base=0, pattern=[[1, P]], channel_multiplier=-1).then_inc(consts, 1)

            ms = [0]

            def inverse_root(a, b, width, count):
                if count:
                    pool.wait_ge(sq_ready, count)
                ms[0] += 1
                g.tensor_scalar(ssum[:, a:b], ssum[:, a:b], 1.0 / width, EPS, ALU.mult, ALU.add).then_inc(ms_ready, 1)
                pool.wait_ge(ms_ready, ms[0])
                g.tensor_tensor(rstd[:, a:b], ssum[:, a:b], half[:, 0:b - a], ALU.pow).then_inc(rstd_ready, 1)

            for m in range(7):
                s = P >> m
                v = masks[:, m, :].rearrange("p (b s) -> p b s", s=s)
                if m:
                    step(g.affine_select(out=v, in_=v, compare_op=ALU.is_ge, fill=0.0, base=0,
                                         pattern=[[-s, P // s], [0, s]], channel_multiplier=1))
                    step(g.affine_select(out=v, in_=v, compare_op=ALU.is_ge, fill=0.0, base=s - 1,
                                         pattern=[[s, P // s], [0, s]], channel_multiplier=-1))
                g.affine_select(out=masks[:, m, :], in_=masks[:, m, :], compare_op=ALU.not_equal, fill=0.0,
                                base=0, pattern=[[-1, P]], channel_multiplier=1).then_inc(consts, 1)
            g.affine_select(out=neg_tri[:, :], in_=neg_tri[:, :], compare_op=ALU.is_ge, fill=0.0,
                            base=0, pattern=[[-1, P]], channel_multiplier=1).then_inc(consts, 1)
            g.affine_select(out=causal[:, P:2 * P], in_=causal[:, P:2 * P], compare_op=ALU.is_ge, fill=NEG,
                            base=0, pattern=[[-1, P]], channel_multiplier=1).then_inc(consts, 1)

            for j, v in enumerate(INV_FREQ):
                ins = g.memset(inv_f[:, j:j + 1], v)
            step(ins)
            pool.wait_ge(pos_landed, 16 * T)
            step(g.tensor_copy(pos_f[:, :], pos_i[:, :]))
            for t in range(T):
                step(g.tensor_scalar(ang[:, 0, t, :], inv_f, pos_f[:, t:t + 1], None, ALU.mult))
                step(g.tensor_copy(ang[:, 1, t, :], ang[:, 0, t, :]))
            step(g.tensor_scalar(red[:, 0, :, :], ang[:, 0, :, :], 1.0 / TWO_PI, 0.0, ALU.mult, ALU.add))
            step(g.tensor_scalar(red[:, 1, :, :], ang[:, 1, :, :], 1.0 / TWO_PI, 0.25, ALU.mult, ALU.add))
            step(g.tensor_scalar(red[:, :, :, :], red[:, :, :, :], MAGIC, None, ALU.add))
            step(g.tensor_scalar(red[:, :, :, :], red[:, :, :, :], -MAGIC, None, ALU.add))
            for c in (C1, C2, C3):
                step(g.tensor_scalar(turn, red[:, :, :, :], c, None, ALU.mult))
                step(g.tensor_tensor(ang[:, :, :, :], ang[:, :, :, :], turn, ALU.subtract))
            step(g.tensor_scalar(ang[:, 1, :, :], ang[:, 1, :, :], np.pi / 2, None, ALU.add))
            seq[0] += 1
            g.tensor_scalar(ang[:, :, :, :], ang[:, :, :, :], 3.1415925, -3.1415925, ALU.min, ALU.max).then_inc(pool_seq, 1)
            pool.wait_ge(pool_seq, seq[0])
            pool.sem_inc(ang_ready, 1)

            inverse_root(0, 2, D, 2)
            pool.wait_ge(trig_ready, 2)
            step(g.tensor_copy(cos_[:, :, 1, :], cos_[:, :, 0, :]))
            step(g.tensor_scalar(sin_[:, :, 0, :], sin_[:, :, 1, :], -1.0, None, ALU.mult))

            for lev in range(8):
                L = P >> lev
                if lev == 0:
                    pool.wait_ge(b_ready, 2)
                else:
                    pool.wait_ge(lev_done, levels_done(lev))
                (b0, b1), (e0, e1) = halves(g_b, L), halves(g_u, L)
                ref = b0[:, :, L - 1:L].to_broadcast([P, GH * T * P // (2 * L), L])
                g.tensor_tensor(e0, ref, b0, ALU.subtract).then_inc(gd_ready, 1)
                if lev == 0:
                    g.tensor_copy(e1, b1).then_inc(gd_ready, 1)
                else:
                    g.tensor_tensor(e1, b1, ref, ALU.subtract).then_inc(gd_ready, 1)
            pool.wait_ge(lev_copied, levels_done(8))
            v = att.rearrange("p (a q) -> p a q", q=P)
            g.affine_select(out=v, in_=v, compare_op=ALU.is_ge, fill=0.0, base=0,
                            pattern=[[0, T * GH], [1, P]], channel_multiplier=-1).then_inc(att_ready, 1)

            def strictly_before(buf, signal):
                v = buf.rearrange("p (a q) -> p a q", q=P)[:, 0:3:2, :]
                g.affine_select(out=v, in_=v, compare_op=ALU.is_gt, fill=0.0, base=0,
                                pattern=[[0, 2], [1, P]], channel_multiplier=-1).then_inc(signal, 1)

            pool.wait_ge(t_free_a, freed(U_PREPY))
            pool.wait_ge(t_free_d, freed(U_PREPY))
            with pool.Fori(0, SBH // 2) as i:
                for par in range(2):
                    g.tensor_copy(k_head[par], even[:, bass.ds(i * 512 + (2048 + 256 * par), 256)]).then_inc(sk_ready, 1)
                for par in range(2):
                    pool.wait_ge(ssp_ready, i * 2 + (par + 1))
                    g.tensor_tensor(idle_p[:, par:par + 1], idle_p[:, par:par + 1], idle_p[:, par:par + 1], ALU.add)
                    strictly_before(sp_[par], ssel_ready)
                for par in range(2):
                    pool.wait_ge(sw_ready, i * 2 + (par + 1))
                    g.tensor_tensor(idle_p[:, 2 + par:3 + par], idle_p[:, 2 + par:3 + par], idle_p[:, 2 + par:3 + par], ALU.add)
                    strictly_before(sa[par], swm_ready)

            pool.wait_ge(gla_g_landed, 16)
            for n in range(2):
                pool.wait_ge(silu_ready, 4 + n)
                pool.wait_ge(evac_a, C_MIX + 6 + 2 * n)
                for t in range(T):
                    v = ys[:, t, SBH * DH + CW * n:SBH * DH + CW * n + CW].rearrange("p (h e) -> p h e", h=2)
                    g.tensor_tensor(v, v, gla_g[:, :].unsqueeze(1).to_broadcast([P, 2, GV]), ALU.mult).then_inc(gg_ready, 1)
            inverse_root(16, 24, GV, 2 + 8)

            def add_residual(c0, n):
                pool.wait_ge(evac_a, c0 + n + 1)
                dst = xs[:, 0, CW * n:CW * n + CW]
                g.tensor_tensor(dst, dst, stg[n % 2][:, 0, :], ALU.add).then_inc(res_added, 1)

            def stream_sums(a0, dst):
                pool.wait_ge(sq_ready, 18 if a0 == 24 else 30)
                v = ssum[:, a0:a0 + 8].rearrange("p (t s) -> p t s", t=T)
                step(g.tensor_tensor(v[:, :, 0:2], v[:, :, 0:2], v[:, :, 2:4], ALU.add))
                step(g.tensor_tensor(ssum[:, dst:dst + 2], v[:, :, 0], v[:, :, 1], ALU.add))

            pool.sem_inc(res_added, 2)
            for n in range(4):
                add_residual(C_OUT0, n)
            stream_sums(24, 2)
            inverse_root(2, 4, D, None)

            def rotate(xv, m1, m2, last):
                c = cos_[:, :, :, :].rearrange("p t a c -> p t (a c)")
                h2 = ROPE // 2
                g.tensor_tensor(m1, xv, c, ALU.mult)
                g.tensor_tensor(m2[:, :, 0:h2], xv[:, :, h2:], sin_[:, :, 0, :], ALU.mult)
                g.tensor_tensor(m2[:, :, h2:], xv[:, :, 0:h2], sin_[:, :, 1, :], ALU.mult).then_inc(rope_seq, 1)
                return lambda: g.tensor_tensor(xv, m1, m2, ALU.add).then_inc(last, 1)

            mm = [(rope_m1[:, 128 * i:128 * i + 128].rearrange("p (t n) -> p t n", t=T),
                   rope_m2[:, 128 * i:128 * i + 128].rearrange("p (t n) -> p t n", t=T)) for i in range(2)]
            pool.wait_ge(kr_evac, 2)
            end = rotate(kr_tok, *mm[0], kr_roped)
            pool.wait_ge(rope_seq, 1)
            end()
            inverse_root(4, 8, LAT, 22)
            with pool.Fori(0, PAIRS) as p:
                pool.wait_ge(evac_a, p * 2 + (C_MLA + 1))
                pool.wait_ge(evac_d, p * 2 + (C_MLA + 1))
                ends = [rotate(q_tok[:, :, QH * h + DH:QH * h + QH], *mm[h], q_roped) for h in range(2)]
                for h in range(2):
                    pool.wait_ge(rope_seq, p * 2 + (2 + h))
                    ends[h]()
            pool.wait_ge(fin_landed, 16)
            for n in range(3):
                add_residual(C_OUT1, n)
                pool.wait_ge(sq_ready, 22 + 2 * n + 2)
                for t in range(T):
                    y = xs[:, t, CW * n:CW * n + CW]
                    g.tensor_tensor(y, y, fin_g[:, CW * n:CW * n + CW], ALU.mult).then_inc(res_gained, 1)
            stream_sums(32, 8)
            inverse_root(8, 10, D, None)

        @block.scalar
        def _(act):
            a = nc.scalar

            def piece(b, s, w=FULL):
                act.wait_ge(piece_used, b * NP + (s - RING + 1))
                act.wait_ge(raw_landed[s % RAW], b * 16 + (16 if s < RAW else 32))
                a.activation(w_hi[:, s % RING, 0:w], raw[:, s % RAW, 0:w], ACT.Copy).then_inc(hi_ready, 1)

            def ahead(b, this=FULL, following=FULL, pieces=8, between=None):
                for k in range(pieces):
                    for fn in (between or {}).get(k, []):
                        fn()
                    w = this if k < 4 else following
                    piece(b, 4 + k, w[k % 4] if isinstance(w, tuple) else w)

            def evac(par, c, dst, scale=1.0, func=ACT.Copy, part="even"):
                act.wait_ge(piece_used, pieces_through(c, part))
                a.activation(dst, ps[:, 2 * par, :][:, 0:dst.shape[-1]], func, scale=scale).then_inc(evac_a, 1)

            def prep(us, gain=None):
                def step(s):
                    for bank in range(2):
                        act.wait_ge(t_done, 2 * us[s] + bank + 1)
                        k = 4 * s + 2 * bank
                        if gain is None:
                            ins = a.activation(a_hi[:, k:k + 2, :], ps[:, 4 + bank, :].rearrange("p (k n) -> p k n", k=2), ACT.Copy)
                        else:
                            for kk in range(2):
                                ins = a.activation(a_hi[:, k + kk, :], ps[:, 4 + bank, 256 * kk:256 * kk + 256], ACT.Copy,
                                                   scale=gain_t[:, gain + k + kk:gain + k + kk + 1])
                        ins.then_inc(t_free_a, 1)
                return step

            sq = [0]

            def squares(src, dst, out_):
                if sq[0]:
                    act.wait_ge(sq_ready, sq[0])
                a.activation(out_, src, ACT.Square, accum_out=dst).then_inc(sq_ready, 1)
                sq[0] += 1

            for t in range(T):
                act.dma_start(xs[:, t, 0:CW], x_d[t][:, 0:CW]).then_inc(x_landed[t], 16)
            a.preload_act_table_set("natural_log_exp_and_others")
            x_prep = prep(steps_from(U_PREP0), 0)
            for s in range(RING):
                act.wait_ge(raw_landed[s], 16)
                a.activation(w_hi[:, s, :], raw[:, s, :], ACT.Copy).then_inc(hi_ready, 1)
                if s == 0:
                    act.wait_ge(gain_ready, 1)
                    x_prep(0)
                    act.wait_ge(ga_landed, 16)
                    a.activation(ga_hi, ga_raw, ACT.Copy).then_inc(ga_ready, 1)
                if s == 2:
                    x_prep(1)
            r0 = rstd[:, 0:1]

            def level(lev):
                act.wait_ge(gd_ready, 2 * lev + 2)
                a.activation(g_u, g_u, ACT.Exp).then_inc(ge_ready, 1)

            def heads_out(c):
                act.wait_ge(t_done, 2 * (U_QK + c) + 1)
                e = c % 2
                dst = gqk_t[:, 4 * e:4 * e + 2, :] if c < C_SBQK else qk_t[:, 4 * (c - C_SBQK):4 * (c - C_SBQK) + 2, :]
                scale = SB_SCALE if c in QUERIES else 1.0
                a.activation(dst, ps[:, 4, :].rearrange("p (h q) -> p h q", h=2), ACT.Copy, scale=scale).then_inc(t_free_a, 1)

            def x_squares():
                for n in range(4 * T):
                    act.wait_ge(x_landed[n], 16)
                for t in range(T):
                    squares(xs[:, t, :], ssum[:, t:t + 1], junk)

            def gates_log():
                act.wait_ge(ua_ready, 1)
                a.activation(g_e2, g_e2, ACT.Exp, scale=-1.0).then_inc(ue_ready, 1)
                act.wait_ge(ue_ready, 1)
                a.activation(g_e2, g_e2, ACT.Ln, bias=1.0).then_inc(ue_ready, 1)

            for c in range(C_MIX):
                b, par, lev = B_GQK + c, c % 2, 2 * (c - C_SBQK)
                if c == 0:
                    ahead(b, between=among(x_prep, {0: [], 1: [], 6: [x_squares]}))
                elif c == 1:
                    ahead(b, between={2: [gates_log]})
                else:
                    ahead(b, between={1: [] if par else [lambda: heads_out(c - 1)], 2: [lambda: level(lev)], 4: [lambda: level(lev + 1)]})
                if c == 0:
                    act.wait_ge(rstd_ready, 1)
                evac(par, c, stg[par][:, 0, :], r0)
                if c == 0:
                    act.wait_ge(ang_ready, 1)
                    a.activation(sin_[:, :, 1, :], ang[:, 0, :, :], ACT.Sin).then_inc(trig_ready, 1)
                    a.activation(cos_[:, :, 0, :], ang[:, 1, :, :], ACT.Sin).then_inc(trig_ready, 1)
                    a.preload_act_table_set("natural_log_exp_and_others")
                if par:
                    heads_out(c - 1)
            def two_heads(i, between=None):
                ahead(i * 2 + B_MIX, between=between)
                evac(0, i * 2 + C_MIX, vals[:, 0, bass.ds(i * CW, CW)], r0)
                a.preload_act_table_set("natural_log_exp_and_others")
                for par in range(2):
                    act.wait_ge(sabs_ready, i * 2 + (par + 1))
                    a.activation(sa[par], sa[par], ACT.Exp, scale=-1.0).then_inc(sexp_ready, 1)
                for par in range(2):
                    act.wait_ge(sexp_ready, i * 2 + (par + 1))
                    a.activation(sa[par], sa[par], ACT.Ln, bias=1.0).then_inc(slog_ready, 1)
                b = i * 2 + (B_MIX + 1)
                for s in (4, 5, 6):
                    piece(b, s)
                for par in range(2):
                    act.wait_ge(sarg_done, i * 2 + (par + 1))
                    a.activation(sa[par], ps[:, 6 + par, 0:384], ACT.Exp).then_inc(sw_ready, 1)
                for s in range(7, 12):
                    piece(b, s)
                evac(1, i * 2 + (C_MIX + 1), ys[:, 0, bass.ds(i * CW, CW)], r0, ACT.Silu)
                act.wait_ge(evac_d, i * 2 + (C_MIX + 2))
                gate = ys[:, 1, bass.ds(i * CW, CW)]
                a.activation(gate, gate, ACT.Silu).then_inc(silu_ready, 1)

            two_heads(0, {1: [lambda: heads_out(C_MIX - 1)]})
            with act.Fori(1, SBH // 2) as i:
                two_heads(i)

            def head_squares(t):
                for h in range(GH):
                    if h % 2 == 0:
                        act.wait_ge(go_done, 2 * (1 - t) + h // 2 + 1)
                    squares(ps[:, 2 + 4 * t + h // 2, GV * (h % 2):GV * (h % 2) + GV], ssum[:, 16 + GH * t + h:17 + GH * t + h],
                            att_junk)

            def outputs(b, c, added, plans, part="even", end=False):
                for n, plan in enumerate(plans):
                    last = end and n == 3
                    ahead(b + n, pieces=4 if last else 8, between=plan)
                    if last:
                        return
                    act.wait_ge(res_added, n + 1 + added)
                    evac(n % 2, c + n, stg[n % 2][:, 0, :], part=part)

            def stream_squares(n, c, added, a0):
                def fn():
                    act.wait_ge(res_added, n + 3 + added)
                    act.wait_ge(evac_d, c + n + 1)
                    for t in range(T):
                        squares(xs[:, t, CW * n:CW * n + CW], ssum[:, a0 + 4 * t + n:a0 + 4 * t + n + 1], sq_junk)
                return fn

            head_squares(1)
            y_prep, x1_prep = prep(steps_from(U_PREPY)), prep(steps_from(U_PREP1), 16)
            outputs(B_OUT0, C_OUT0, 0, (
                {**among(y_prep), 0: [lambda: y_prep(0), lambda: head_squares(0)]},
                {5: [stream_squares(0, C_OUT0, 0, 24)]},
                {5: [stream_squares(1, C_OUT0, 0, 24)]},
                {2: [lambda: x1_prep(0)], 4: [lambda: x1_prep(1)], 5: [stream_squares(2, C_OUT0, 0, 24)], 6: [lambda: x1_prep(2)]}))
            ahead(B_LAT, between={2: [lambda: x1_prep(3)], 3: [stream_squares(3, C_OUT0, 0, 24)]})
            act.wait_ge(rstd_ready, 3)
            r1 = rstd[:, 2:3]
            evac(0, C_LAT, lat[:, 0, 0:CW], r1)

            def kr_weights():
                act.wait_ge(kr_landed, 16)
                a.activation(kr_hi, kr_raw, ACT.Copy).then_inc(krw_ready, 1)

            ahead(B_LAT + 1, between={4: [kr_weights]})
            evac(1, C_LAT + 1, lat[:, 0, CW:2 * CW], r1)

            def latent_squares():
                act.wait_ge(evac_a, C_GATE)
                act.wait_ge(evac_d, C_GATE)
                for n in range(4):
                    kind, t = divmod(n, T)
                    squares(lat[:, t, CW * kind:CW * kind + CW], ssum[:, 4 + n:5 + n], sq_junk)

            def kr_taken():
                act.wait_ge(kr_done, 1)
                a.activation(kr_t, ps[0:ROPE, 7, 0:T * P], ACT.Copy).then_inc(kr_out, 1)

            def kr_turned():
                act.wait_ge(krt_done, 1)
                a.activation(kr_t, ps[0:ROPE, 6, 0:T * P], ACT.Copy).then_inc(krt_ready, 1)

            lat_prep = prep((U_LAT, U_LAT + 1), 32)
            plans = ({1: [latent_squares], 4: [kr_taken]}, {}, {2: [kr_turned]}, {2: [lambda: lat_prep(0)], 4: [lambda: lat_prep(1)]})
            for n, between in enumerate(plans):
                ahead(B_GATE + n, following=UP if n == 3 else FULL, between=between)
                cols = slice(CW * n, CW * n + CW)
                evac(n % 2, C_GATE + n, ys[:, 0, cols], r1, ACT.Silu, part="gate")
                act.wait_ge(evac_d, C_GATE + n + 1)
                a.activation(ys[:, 1, cols], ys[:, 1, cols], ACT.Silu).then_inc(silu_ready, 1)
            act.wait_ge(rstd_ready, 4)

            z_prep = prep(STEPS_Z)

            def pair_of(i, par, first=False, last=False):
                p = i * 2 + par
                nxt = (FULL,) * 4 if last else UP

                def up_piece(k):
                    act.wait_ge(piece_used, p * 4 + (NP * B_MLA + 4 + k - (RING - 1)))
                    s = 4 * (1 - par) + k
                    act.wait_ge(raw_landed[s], i * 16 + (16 * (B_MLA + 1) + (16 if par else 0)))
                    a.activation(w_hi[:, k, 0:nxt[k]], raw[:, s, 0:nxt[k]], ACT.Copy).then_inc(hi_ready, 1)

                evac(0, p * 2 + C_MLA, q_tok[:, 0, :], rstd[:, 4:5], part="up")
                up_piece(0)
                evac(1, p * 2 + (C_MLA + 1), kv_tok[par][:, 0, :], rstd[:, 6:7], part="up")
                if not first:
                    weights_out(p)
                act.wait_ge(qkt_done, p * 3 + 1)
                a.activation(qn_t, ps[:, 0, :], ACT.Copy).then_inc(qt_ready, 1)
                act.wait_ge(qkt_done, p * 3 + 2)
                a.activation(qr_t[0:ROPE, :], ps[0:ROPE, 1, :], ACT.Copy).then_inc(qt_ready, 1)
                up_piece(1)
                if last:
                    z_prep(0)
                up_piece(2)
                act.wait_ge(nmx_ready, p + 1)
                for h in range(2):
                    for t in range(T):
                        cols = (slice(0, P), slice(P, 384))[t]
                        j = 2 * h + t
                        a.activation(s_m[h][:, cols], s_m[h][:, cols], ACT.Exp, bias=nmx[:, j:j + 1], scale=MLA_SCALE,
                                     accum_out=rsum[:, j:j + 1]).then_inc(p_ready, 1)
                if last:
                    z_prep(1)
                up_piece(3)

            def weights_out(p):
                act.wait_ge(t_done, 2 * U_LAST + 1 if p is None else p * 2 + (2 * (U_MLA - 1) + 1))
                a.activation(p_t[:, 0, :], ps[:, 4, 0:384], ACT.Copy).then_inc(t_free_a, 1)

            pair_of(0, 0, first=True)
            with act.Fori(0, PAIRS // 2 - 1) as i:
                pair_of(i, 1)
                pair_of(i + 1, 0)
            pair_of(PAIRS // 2 - 1, 1, last=True)
            outputs(B_OUT1, C_OUT1, 4, (
                {2: [lambda: z_prep(2)], 3: [lambda: weights_out(None)], 5: [lambda: z_prep(3)]},
                {5: [stream_squares(0, C_OUT1, 4, 32)]},
                {5: [stream_squares(1, C_OUT1, 4, 32)]},
                {3: [stream_squares(2, C_OUT1, 4, 32)]}), part="out", end=True)
            for t in range(T):
                act.wait_ge(evac_d, C_OUT1 + 4 + t)
                squares(xs[:, t, 3 * CW:], ssum[:, 35 + 4 * t:36 + 4 * t], sq_junk)
            act.wait_ge(rstd_ready, 5)
            for n, out_part in enumerate(final_pieces(0)):
                if n == 2:
                    act.wait_ge(last_gained, 1)
                act.wait_ge(res_gained, 2 * 3)
                a.activation(out_part, out_part, ACT.Copy, scale=rstd[:, 8:9]).then_inc(fin_a, 1)

        @block.vector
        def _(dve):
            v = nc.vector

            def piece(b, s, w=FULL):
                dve.wait_ge(hi_ready, b * NP + (s + 1))
                v.tensor_tensor(w_lo[:, s % RING, 0:w], raw[:, s % RAW, 0:w], w_hi[:, s % RING, 0:w].bitcast(F32),
                                ALU.subtract).then_inc(lo_ready, 1)

            def ahead(b, this=FULL, following=FULL, pieces=8, between=None):
                for k in range(pieces):
                    for fn in (between or {}).get(k, []):
                        fn()
                    w = this if k < 4 else following
                    piece(b, 4 + k, w[k % 4] if isinstance(w, tuple) else w)

            def evac(par, c, dst, scale, part="even"):
                dve.wait_ge(piece_used, pieces_through(c, part))
                v.tensor_scalar(dst, ps[:, 2 * par + 1, :][:, 0:dst.shape[-1]], scale, None, ALU.mult).then_inc(evac_d, 1)

            def prep(us, gain=None):
                def step(s):
                    for bank in range(2):
                        k = 4 * s + 2 * bank
                        dve.wait_ge(t_free_a, freed(us[s]) + bank + 1)
                        if gain is None:
                            ins = v.tensor_tensor(a_lo[:, k:k + 2, :], ps[:, 4 + bank, :].rearrange("p (k n) -> p k n", k=2),
                                                  a_hi[:, k:k + 2, :].bitcast(F32), ALU.subtract)
                        else:
                            for kk in range(2):
                                ins = v.scalar_tensor_tensor(
                                    out=a_lo[:, k + kk, :], in0=ps[:, 4 + bank, 256 * kk:256 * kk + 256],
                                    scalar=gain_t[:, gain + k + kk:gain + k + kk + 1],
                                    in1=a_hi[:, k + kk, :].bitcast(F32), op0=ALU.mult, op1=ALU.subtract)
                        ins.then_inc(t_free_d, 1)
                return step

            dve.wait_ge(gain_done, 1)
            v.tensor_copy(gain_t[:, :], ps[:, 6, 0:40]).then_inc(gain_ready, 1)
            x_prep = prep(steps_from(U_PREP0), 0)
            for s in range(RING):
                piece(0, s)
                if s == 0:
                    dve.wait_ge(gain_ready, 1)
                    x_prep(0)
                    dve.wait_ge(ga_ready, 1)
                    v.tensor_tensor(ga_lo, ga_raw, ga_hi.bitcast(F32), ALU.subtract).then_inc(ga_ready, 1)
                if s == 2:
                    x_prep(1)
            r0, r1 = rstd[:, 0:1], rstd[:, 1:2]

            def decayed(lev):
                L = P >> lev
                if lev == 0:
                    dve.wait_ge(t_free_a, freed(U_QK + 2))
                    dve.wait_ge(t_free_d, freed(U_QK + 2))
                e0, e1 = halves(g_u, L)
                q1, k0 = halves(even[:, 4096:5120], L)[1], halves(even[:, 5120:6144], L)[0]
                dve.wait_ge(ge_ready, lev + 1)
                v.scalar_tensor_tensor(out=e1, in0=e1, scalar=1.0, in1=q1, op0=ALU.min, op1=ALU.mult).then_inc(gq_ready, 1)
                v.scalar_tensor_tensor(out=e0, in0=e0, scalar=1.0, in1=k0, op0=ALU.min, op1=ALU.mult).then_inc(gq_ready, 1)

            def copied(lev):
                if lev == 0:
                    for n, (bank, dst) in enumerate(((6, att_x), (7, att[:, 0:512]), (5, att[:, 512:1024]))):
                        dve.wait_ge(lev_done, n + 1)
                        v.tensor_copy(dst, ps[:, bank, :]).then_inc(lev_copied, 1)
                    return
                dve.wait_ge(consts, 9)
                for bank in range(2):
                    dve.wait_ge(lev_done, levels_done(lev) + bank + 1)
                    dve.wait_ge(lev_copied, levels_done(lev) + bank)
                    v.copy_predicated(att[:, 512 * bank:512 * bank + 512].rearrange("p (h q) -> p h q", h=GH),
                                      masks[:, lev - 1, :].bitcast(I32).unsqueeze(1).to_broadcast([P, GH, P]),
                                      ps[:, 6 + bank, :].rearrange("p (h q) -> p h q", h=GH)).then_inc(lev_copied, 1)

            def heads_out(c):
                dve.wait_ge(t_done, 2 * (U_QK + c) + 2)
                e = c % 2
                dst = gqk_t[:, 4 * e + 2:4 * e + 4, :] if c < C_SBQK else qk_t[:, 4 * (c - C_SBQK) + 2:4 * (c - C_SBQK) + 4, :]
                scale = SB_SCALE if c in QUERIES else 1.0
                v.tensor_scalar(dst, ps[:, 5, :].rearrange("p (h q) -> p h q", h=2), scale, None, ALU.mult).then_inc(t_free_d, 1)

            def gates_taken():
                dve.wait_ge(gat_done, 1)
                v.tensor_copy(ga_t, ps[0:GR, 6, 0:T * P]).then_inc(gat_ready, 1)

            def gates_biased():
                dve.wait_ge(bias_landed, 16)
                for t in range(T):
                    dve.wait_ge(u_done, t + 1)
                    v.scalar_tensor_tensor(out=g_u[:, 512 * t:512 * t + 512], in0=ps[:, 6 + t, :], scalar=rstd[:, t:t + 1],
                                           in1=g_bias, op0=ALU.mult, op1=ALU.add).then_inc(u_ready, 1)
                dve.wait_ge(u_ready, 2)
                v.tensor_scalar(g_e2.bitcast(I32), g_u.bitcast(I32), ABS, None, ALU.bitwise_and).then_inc(ua_ready, 1)

            def log_gates():
                dve.wait_ge(ue_ready, 2)
                v.scalar_tensor_tensor(out=g_u, in0=g_u, scalar=0.0, in1=g_e2, op0=ALU.min, op1=ALU.subtract).then_inc(g_ready, 1)

            def sums_taken():
                for bank in range(2):
                    dve.wait_ge(b_done, bank + 1)
                    v.tensor_copy(g_b[:, 512 * bank:512 * bank + 512], ps[:, 6 + bank, :]).then_inc(b_ready, 1)

            for c in range(C_MIX):
                b, par = B_GQK + c, c % 2
                lev = 2 * (c - C_SBQK)
                if c == 0:
                    ahead(b, between=among(x_prep, {0: [], 1: []}))
                    dve.wait_ge(rstd_ready, 1)
                elif c == 1:
                    ahead(b, between={0: [gates_taken], 1: [gates_biased], 3: [log_gates], 6: [sums_taken]})
                else:
                    ahead(b, between={1: [] if par else [lambda: heads_out(c - 1)], 2: [lambda: decayed(lev)], 3: [lambda: copied(lev)], 5: [lambda: decayed(lev + 1)]})
                evac(par, c, stg[par][:, 1, :], r1)
                if c >= C_SBQK:
                    copied(lev + 1)
                if par:
                    heads_out(c - 1)
            dve.sem_inc(sy_ready, 2)
            dve.sem_inc(silu_ready, 1)

            def two_heads(i, between=None):
                ahead(i * 2 + B_MIX, between=between)
                evac(0, i * 2 + C_MIX, vals[:, 1, bass.ds(i * CW, CW)], r1)
                dve.wait_ge(att_ready, 1)
                for par in range(2):
                    dve.wait_ge(sz_done, i * 2 + (par + 1))
                    v.tensor_scalar(sa[par].bitcast(I32), ps[:, 6 + par, 0:384].bitcast(I32), ABS, None, ALU.bitwise_and).then_inc(sabs_ready, 1)
                for par in range(2):
                    dve.wait_ge(slog_ready, i * 2 + (par + 1))
                    v.scalar_tensor_tensor(out=sp_[par], in0=ps[:, 6 + par, 0:384], scalar=0.0, in1=sa[par],
                                           op0=ALU.max, op1=ALU.add).then_inc(ssp_ready, 1)
                ahead(i * 2 + (B_MIX + 1))
                evac(1, i * 2 + (C_MIX + 1), ys[:, 1, bass.ds(i * CW, CW)], r1)
                dve.wait_ge(silu_ready, 2)
                dve.wait_ge(evac_a, C_MIX + 2)
                dve.wait_ge(silu_ready, i + 1)
                dve.wait_ge(evac_a, i * 2 + C_MIX)
                for par in range(2):
                    dve.wait_ge(sy_done, i * 2 + (par + 1))
                    y = ys[:, :, bass.ds(i * (2 * DH) + par * DH, DH)]
                    v.tensor_tensor(y, y, ps[:, 4 + par, 0:T * DH].rearrange("p (t e) -> p t e", t=T), ALU.mult).then_inc(sy_ready, 1)

            two_heads(0, {1: [lambda: heads_out(C_MIX - 1)]})
            with dve.Fori(1, SBH // 2) as i:
                two_heads(i)

            def heads_gated():
                dve.wait_ge(rstd_ready, 2)
                dve.wait_ge(gg_ready, 4)
                for n in range(2 * GH):
                    t, h = 1 - n // GH, n % GH
                    y = ys[:, t, SBH * DH + GV * h:SBH * DH + GV * h + GV]
                    v.scalar_tensor_tensor(out=y, in0=ps[:, 2 + 4 * t + h // 2, GV * (h % 2):GV * (h % 2) + GV],
                                           scalar=rstd[:, 16 + GH * t + h:17 + GH * t + h], in1=y,
                                           op0=ALU.mult, op1=ALU.mult).then_inc(gy_ready, 1)

            def outputs(b, c, plans, part="even", end=False):
                for n, plan in enumerate(plans):
                    last = end and n == 3
                    ahead(b + n, pieces=4 if last else 8, between=plan)
                    dve.wait_ge(piece_used, pieces_through(c + n, part))
                    for t in range(T) if last else (1,):
                        dst = xs[:, t, CW * n:CW * n + CW]
                        v.tensor_tensor(dst, dst, ps[:, 2 * (n % 2) + t, :], ALU.add).then_inc(evac_d, 1)

            y_prep, x1_prep = prep(steps_from(U_PREPY)), prep(steps_from(U_PREP1), 16)
            outputs(B_OUT0, C_OUT0, (
                {**among(y_prep), 0: [lambda: y_prep(0), heads_gated, lambda: y_prep(1)], 1: []},
                {}, {},
                {2: [lambda: x1_prep(0)], 4: [lambda: x1_prep(1)], 6: [lambda: x1_prep(2)]}))
            r1 = rstd[:, 3:4]
            ahead(B_LAT, between={2: [lambda: x1_prep(3)]})
            dve.wait_ge(rstd_ready, 3)
            evac(0, C_LAT, lat[:, 1, 0:CW], r1)

            def kr_weights():
                dve.wait_ge(krw_ready, 1)
                v.tensor_tensor(kr_lo, kr_raw, kr_hi.bitcast(F32), ALU.subtract).then_inc(krw_ready, 1)

            ahead(B_LAT + 1, between={5: [kr_weights]})
            evac(1, C_LAT + 1, lat[:, 1, CW:2 * CW], r1)

            def kr_scaled():
                dve.wait_ge(kr_back, 1)
                for t in range(T):
                    v.tensor_scalar(kr_tok[:, t, :], ps[:, 7, 256 + ROPE * t:256 + ROPE * t + ROPE], rstd[:, 2 + t:3 + t],
                                    None, ALU.mult).then_inc(kr_evac, 1)

            lat_prep = prep((U_LAT, U_LAT + 1), 32)
            plans = ({}, {1: [kr_scaled]}, {}, {2: [lambda: lat_prep(0)], 4: [lambda: lat_prep(1)]})
            for n, between in enumerate(plans):
                ahead(B_GATE + n, following=UP if n == 3 else FULL, between=between)
                evac(n % 2, C_GATE + n, ys[:, 1, CW * n:CW * n + CW], r1, part="gate")
            dve.wait_ge(rstd_ready, 4)

            def weighted(i, par):
                dve.wait_ge(my_done, i * 4 + (2 * par + 2))
                for h in range(2):
                    for t in range(T):
                        y = ys[:, t, bass.ds(i * (4 * DH) + (2 * par + h) * DH, DH)]
                        v.scalar_tensor_tensor(out=y, in0=ps[:, 3, (2 * h + t) * DH:(2 * h + t + 1) * DH],
                                               scalar=rinv[:, 2 * h + t:2 * h + t + 1], in1=y,
                                               op0=ALU.mult, op1=ALU.mult).then_inc(my_ready, 1)

            def weights_out(p, last=False):
                dve.wait_ge(p_ready, p * 4)
                v.reciprocal(rinv[:, :], rsum[:, :]).then_inc(rinv_ready, 1)
                dve.wait_ge(t_done, 2 * U_LAST + 2 if last else p * 2 + (2 * (U_MLA - 1) + 2))
                v.tensor_copy(p_t[:, 1, :], ps[:, 5, 0:384]).then_inc(t_free_d, 1)

            z_prep = prep(STEPS_Z)

            def pair_of(i, par, first=False, last=False):
                p = i * 2 + par
                nxt = (FULL,) * 4 if last else UP

                def up_piece(k):
                    dve.wait_ge(hi_ready, p * 4 + (NP * B_MLA + 5 + k))
                    v.tensor_tensor(w_lo[:, k, 0:nxt[k]], raw[:, 4 * (1 - par) + k, 0:nxt[k]],
                                    w_hi[:, k, 0:nxt[k]].bitcast(F32), ALU.subtract).then_inc(lo_ready, 1)

                evac(0, p * 2 + C_MLA, q_tok[:, 1, :], rstd[:, 5:6], part="up")
                up_piece(0)
                evac(1, p * 2 + (C_MLA + 1), kv_tok[par][:, 1, :], rstd[:, 7:8], part="up")
                if not first:
                    weights_out(p)
                dve.wait_ge(qkt_done, p * 3 + 3)
                v.tensor_copy(kn_t, ps[:, 2, :]).then_inc(kt_ready, 1)
                if not first:
                    dve.wait_ge(rinv_ready, p)
                    weighted(*((i, 0) if par else (i - 1, 1)))
                up_piece(1)
                if last:
                    z_prep(0)
                up_piece(2)
                for h in range(2):
                    dve.wait_ge(sc_done, p * 2 + (h + 1))
                    v.memset(idle[:, h:h + 1], 0.0)
                    for t in range(T):
                        cols = (slice(0, P), slice(P, 384))[t]
                        v.tensor_tensor_reduce(s_m[h][:, cols], ps[:, 6 + h, cols], causal[:, P if t == 0 else 0:2 * P],
                                               1.0, -3.0e38, ALU.add, ALU.max, mx[:, 2 * h + t:2 * h + t + 1]).then_inc(sc_max, 1)
                dve.wait_ge(sc_max, p * 4 + 4)
                v.tensor_scalar(nmx[:, :], mx[:, :], -MLA_SCALE, None, ALU.mult).then_inc(nmx_ready, 1)
                if last:
                    z_prep(1)
                up_piece(3)

            dve.wait_ge(consts, 11)
            pair_of(0, 0, first=True)
            with dve.Fori(0, PAIRS // 2 - 1) as i:
                pair_of(i, 1)
                pair_of(i + 1, 0)
            pair_of(PAIRS // 2 - 1, 1, last=True)

            def last_weighted():
                dve.wait_ge(rinv_ready, PAIRS)
                weighted(PAIRS // 2 - 1, 1)

            outputs(B_OUT1, C_OUT1, (
                {2: [lambda: z_prep(2)], 3: [lambda: weights_out(PAIRS, last=True)], 4: [last_weighted], 5: [lambda: z_prep(3)]},
                {}, {}, {}), part="out", end=True)
            dve.wait_ge(fin_landed, 16)
            dve.wait_ge(res_added, 9)
            for t in range(T):
                dve.wait_ge(evac_d, C_OUT1 + 4 + t)
                v.tensor_tensor(stg[1][:, t, :], xs[:, t, 3 * CW:], fin_g[:, 3 * CW:], ALU.mult).then_inc(last_gained, 1)
            dve.wait_ge(rstd_ready, 5)
            dve.wait_ge(res_gained, 2 * 3)
            for n, out_part in enumerate(final_pieces(1)):
                if n == 2:
                    dve.wait_ge(last_gained, 2)
                v.tensor_scalar(out_part, out_part, rstd[:, 9:10], None, ALU.mult).then_inc(fin_d, 1)

        @block.tensor
        def _(pe):
            m = nc.tensor

            def project(n0, c, par, wait=True, tiles=NP, k0=0, s0=0, n=CW, before=None):
                if wait:
                    pe.wait_ge(evac_a, c - 1)
                    pe.wait_ge(evac_d, c - 1)
                for j in range(tiles):
                    if before:
                        before(j)
                    s = (s0 + j) % RING
                    pe.wait_ge(lo_ready, n0 + (j + 1))
                    for kk in range(PK):
                        k = k0 + PK * j + kk
                        hi, lo = w_hi[:, s, kk * n:kk * n + n], w_lo[:, s, kk * n:kk * n + n]
                        first, last = j == 0 and kk == 0, j == tiles - 1 and kk == PK - 1
                        for t in range(T):
                            acc = ps[:, 2 * par + t, 0:n]
                            tok = slice(t * P, t * P + P)
                            m.matmul(acc, a_hi[:, k, tok], hi, start=first, stop=False)
                            m.matmul(acc, a_hi[:, k, tok], lo, start=False, stop=False)
                            ins = m.matmul(acc, a_lo[:, k, tok], hi, start=False, stop=last)
                    ins.then_inc(piece_used, 1)

            def at_half(fn):
                return lambda j: fn() if j == NP // 2 else None

            def step_free(u):
                pe.wait_ge(t_free_a, freed(u))
                pe.wait_ge(t_free_d, freed(u))

            def transpose_step(u, s, src):
                step_free(u)
                for bank in range(2):
                    for kk in range(2):
                        k = 4 * s + 2 * bank + kk
                        for t in range(T):
                            ins = m.transpose(ps[:, 4 + bank, 256 * kk + P * t:256 * kk + P * t + P],
                                              src[:, t, P * k:P * k + P], ident[:, :])
                    ins.then_inc(t_done, 1)

            def prepared(us, src, ready, first=True):
                def before(j):
                    if j % 2 == 0:
                        if j == 0 and first:
                            ready(0)
                            transpose_step(us[0], 0, src)
                        pe.wait_ge(t_free_d, freed(us[j // 2]) + 2)
                    step = {1: 1, 2: 2, 4: 3}.get(j)
                    if step:
                        ready(step)
                        transpose_step(us[step], step, src)
                return before

            def x_ready(s):
                for t in range(T):
                    pe.wait_ge(x_landed[T * s + t], 16)

            def narrow(out_, hi, lo, n, ks):
                for k in ks:
                    w = slice(n * k, n * k + n)
                    m.matmul(out_, hi[:, w], a_hi[:, k, :], start=k == 0, stop=False)
                    m.matmul(out_, lo[:, w], a_hi[:, k, :], start=False, stop=False)
                    ins = m.matmul(out_, hi[:, w], a_lo[:, k, :], start=False, stop=k == KT - 1)
                return ins

            pe.wait_ge(consts, 1)
            x_ready(0)
            transpose_step(U_PREP0, 0, xs)
            pe.wait_ge(gains_landed, 64)
            m.transpose(ps[:, 6, 0:40], gain_rows, ident[0:40, 0:40]).then_inc(gain_done, 1)
            x_prepared = prepared(steps_from(U_PREP0), xs, x_ready, first=False)

            def gates_down(j):
                ks = range(PK * j, PK * j + PK)
                return narrow(ps[0:GR, 6, 0:T * P], ga_hi, ga_lo, GR, ks)

            def first_chunk(j):
                x_prepared(j)
                if j == 1:
                    pe.wait_ge(ga_ready, 2)
                    pe.wait_ge(gain_ready, 1)
                if j:
                    gates_down(j - 1)

            def heads_transposed(c, par, u):
                pe.wait_ge(evac_a, c + 1)
                pe.wait_ge(evac_d, c + 1)
                step_free(u)
                for bank in range(2):
                    for kk in range(2):
                        for t in range(T):
                            blk = 2 * bank + kk
                            ins = m.transpose(ps[:, 4 + bank, 256 * kk + P * t:256 * kk + P * t + P],
                                              stg[par][:, t, P * blk:P * blk + P], ident[:, :])
                    ins.then_inc(t_done, 1)

            def gates_up():
                pe.wait_ge(gat_ready, 1)
                pe.wait_ge(alpha_landed, 16)
                for t in range(T):
                    m.matmul(ps[:, 6 + t, :], ga_t[:, P * t:P * t + P], g_alpha, start=True, stop=True).then_inc(u_done, 1)

            def gates_summed():
                pe.wait_ge(g_ready, 1)
                pe.wait_ge(consts, 2)
                for h in range(GH):
                    for t in range(T):
                        ins = m.matmul(ps[:, 6 + h // 2, 256 * (h % 2) + P * t:256 * (h % 2) + P * t + P],
                                       g_u[:, 512 * t + DH * h:512 * t + DH * h + DH], tri16[:, :], start=True, stop=True)
                    if h % 2:
                        ins.then_inc(b_done, 1)

            def level(lev):
                pe.wait_ge(gq_ready, 2 * lev + 2)
                if lev == 0:
                    step_free(U_QK + 2)
                    for h in range(GH):
                        ins = m.matmul(ps[:, 6, P * h:P * h + P], g_u[:, 256 * h:256 * h + P], g_u[:, 256 * h + P:256 * h + 256],
                                       start=True, stop=True)
                    ins.then_inc(lev_done, 1)
                    for t in range(T):
                        for h in range(GH):
                            o = 256 * h + P * t
                            ins = m.matmul(ps[:, 7 - 2 * t, P * h:P * h + P], even[:, 5120 + o:5120 + o + P],
                                           even[:, 4096 + o:4096 + o + P], start=True, stop=True)
                        ins.then_inc(lev_done, 1)
                    return
                pe.wait_ge(lev_copied, levels_done(lev))
                for t in range(T):
                    for h in range(GH):
                        o = 256 * h + P * t
                        ins = m.matmul(ps[:, 6 + t, P * h:P * h + P], g_u[:, o:o + P], g_u[:, o:o + P], start=True, stop=True)
                    ins.then_inc(lev_done, 1)

            def second_chunk(j):
                if j == 2:
                    gates_up()
                if j == 6:
                    gates_summed()

            for c in range(C_MIX):
                par = c % 2
                lev = 2 * (c - C_SBQK)

                def third_and_later(j):
                    if j == 1 and par == 0:
                        heads_transposed(c - 1, 1, U_QK + c - 1)
                    if j == NP // 2:
                        level(lev)

                middle = (first_chunk, second_chunk)[c] if c < C_SBQK else third_and_later
                project(NP * (B_GQK + c), c, par, wait=c >= 2, before=middle)
                if c == 0:
                    gates_down(NP - 1).then_inc(gat_done, 1)
                if c >= C_SBQK:
                    level(lev + 1)
                if par:
                    heads_transposed(c - 1, 0, U_QK + c - 1)

            pe.wait_ge(consts, 11)
            def two_heads(i, before=None):
                project(i * (2 * NP) + NP * B_MIX, i * 2 + C_MIX, 0, before=before)
                pe.wait_ge(lev_copied, levels_done(8))
                for par in range(2):
                    pe.wait_ge(sk_ready, i * 2 + (par + 1))
                    qh, z = i * 512 + 256 * par, ps[:, 6 + par, :]
                    m.matmul(z[:, 0:256], k_head[par][:, 0:P], even[:, bass.ds(qh, 256)], start=True, stop=True)
                    m.matmul(z[:, 256:384], k_head[par][:, P:2 * P], even[:, bass.ds(qh + P, P)], start=False, stop=True,
                             skip_group_check=True).then_inc(sz_done, 1)

                def later_keys():
                    for par in range(2):
                        pe.wait_ge(ssel_ready, i * 2 + (par + 1))
                        z, s = ps[:, 6 + par, :], sp_[par]
                        m.matmul(z[:, 0:256], neg_tri[:, :], s[:, 0:256], start=False, stop=False, skip_group_check=True)
                        m.matmul(z[:, P:256], neg_one[:, :], s[:, 256:384], start=False, stop=False, skip_group_check=True)
                        m.matmul(z[:, 256:384], neg_tri[:, :], s[:, 256:384], start=False, stop=True,
                                 skip_group_check=True).then_inc(sarg_done, 1)

                project(i * (2 * NP) + NP * (B_MIX + 1), i * 2 + (C_MIX + 1), 1, before=at_half(later_keys))
                for par in range(2):
                    pe.wait_ge(swm_ready, i * 2 + (par + 1))
                    pe.wait_ge(sy_ready, i * 2 + (par + 1))
                    pe.wait_ge(evac_d, i * 2 + (C_MIX + 1))
                    w, o = sa[par], ps[:, 4 + par, :]
                    hc = bass.ds(i * (2 * DH) + DH * par, DH)
                    m.matmul(o[:, 0:DH], w[:, 0:P], vals[:, 0, hc], start=True, stop=True)
                    m.matmul(o[:, DH:2 * DH], w[:, P:256], vals[:, 0, hc], start=True, stop=False)
                    m.matmul(o[:, DH:2 * DH], w[:, 256:384], vals[:, 1, hc], start=False, stop=True).then_inc(sy_done, 1)

            two_heads(0, lambda j: heads_transposed(C_MIX - 1, 1, U_QK + C_MIX - 1) if j == 1 else None)
            with pe.Fori(1, SBH // 2) as i:
                two_heads(i)

            def heads_out(t):
                for h in range(GH):
                    o = ps[:, 2 + 4 * t + h // 2, GV * (h % 2):GV * (h % 2) + GV]
                    vc = slice(SBH * DH + GV * h, SBH * DH + GV * h + GV)
                    if t:
                        m.matmul(o, att_x[:, P * h:P * h + P], vals[:, 0, vc], start=True, stop=False)
                    ins = m.matmul(o, att[:, 512 * t + P * h:512 * t + P * h + P], vals[:, t, vc],
                                   start=t == 0, stop=True)
                    if h % 2:
                        ins.then_inc(go_done, 1)

            pe.wait_ge(att_ready, 1)
            pe.wait_ge(sw_ready, SBH)
            pe.wait_ge(evac_a, C_MIX + 7)
            pe.wait_ge(evac_d, C_MIX + 7)
            heads_out(1)
            pe.wait_ge(evac_a, C_MIX + 8)
            pe.wait_ge(evac_d, C_MIX + 8)

            def y_ready(s):
                if s < 2:
                    pe.wait_ge(sy_ready, SBH + 2)
                else:
                    pe.wait_ge(gy_ready, 2 * GH)

            y_ready(0)
            transpose_step(U_PREPY, 0, ys)
            heads_out(0)

            def out_projection(b, c, befores):
                for n, before in enumerate(befores):
                    project(NP * (b + n), c + n, n % 2, before=before)

            x1_steps = steps_from(U_PREP1)

            def x1_early(j):
                if j in (2, 4, 6):
                    n = j // 2 - 1
                    pe.wait_ge(res_added, n + 3)
                    pe.wait_ge(evac_d, C_OUT0 + n + 1)
                    transpose_step(x1_steps[n], n, xs)

            out_projection(B_OUT0, C_OUT0, (prepared(steps_from(U_PREPY), ys, y_ready, first=False), None, None, x1_early))

            def x1_last(j):
                if j == 2:
                    pe.wait_ge(res_added, 6)
                    pe.wait_ge(evac_d, C_OUT0 + 4)
                    transpose_step(x1_steps[3], 3, xs)
                if j % 2 == 0:
                    pe.wait_ge(t_free_d, freed(x1_steps[j // 2]) + 2)

            for par in range(2):
                project(NP * (B_LAT + par), C_LAT + par, par, before=None if par else x1_last)

            def rotary_keys(j):
                if j == 2:
                    pe.wait_ge(krw_ready, 2)
                    narrow(ps[0:ROPE, 7, 0:T * P], kr_hi, kr_lo, ROPE, range(KT)).then_inc(kr_done, 1)

            def rotary_keys_back(j):
                if j == 1:
                    pe.wait_ge(kr_out, 1)
                    for t in range(T):
                        ins = m.transpose(ps[:, 7, 256 + ROPE * t:256 + ROPE * t + ROPE], kr_t[:, P * t:P * t + P], ident[0:ROPE, 0:ROPE])
                    ins.then_inc(kr_back, 1)

            def rotary_keys_turned(j):
                if j == 2:
                    pe.wait_ge(kr_roped, 1)
                    for t in range(T):
                        ins = m.transpose(ps[0:ROPE, 6, P * t:P * t + P], kr_tok[:, t, :], ident[:, :])
                    ins.then_inc(krt_done, 1)

            def latents_transposed(j):
                if j in (2, 4):
                    transpose_step(U_LAT + j // 2 - 1, j // 2 - 1, lat)

            for n, before in enumerate((rotary_keys, rotary_keys_back, rotary_keys_turned, latents_transposed)):
                project(NP * (B_GATE + n), C_GATE + n, n % 2, before=before)
            step_free(U_MLA)

            def projections(i, par, outputs_before=True):
                p = i * 2 + par
                for kind in range(2):
                    if kind and outputs_before:
                        pe.wait_ge(my_ready, p * 4 - 4)
                    project(p * 4 + (NP * B_MLA + 2 * kind), p * 2 + (C_MLA + kind), kind, tiles=2, k0=4 * kind, s0=2 * kind,
                            n=2 * QH if kind == 0 else CW)

            def weights_transposed(i, par, before=freed(U_MLA)):
                p = i * 2 + par
                pe.wait_ge(p_ready, p * 4 + 4)
                pe.wait_ge(t_free_a, p + before)
                pe.wait_ge(t_free_d, p + before)
                for h in range(2):
                    for c in range(3):
                        ins = m.transpose(ps[:, 4 + h, P * c:P * c + P], s_m[h][:, P * c:P * c + P], ident[:, :])
                    ins.then_inc(t_done, 1)

            def operands_transposed(i, par):
                p = i * 2 + par
                pe.wait_ge(q_roped, p * 2 + 2)
                for bank, wide in ((0, DH), (1, ROPE)):
                    for h in range(2):
                        for t in range(T):
                            q0 = QH * h + (0 if bank == 0 else DH)
                            ins = m.transpose(ps[0:wide, bank, 256 * h + P * t:256 * h + P * t + P], q_tok[:, t, q0:q0 + wide], ident[:, :])
                    ins.then_inc(qkt_done, 1)
                pe.wait_ge(evac_a, p * 2 + (C_MLA + 2))
                pe.wait_ge(evac_d, p * 2 + (C_MLA + 2))
                for h in range(2):
                    for t in range(T):
                        ins = m.transpose(ps[:, 2, 256 * h + P * t:256 * h + P * t + P], kv_tok[par][:, t, 2 * DH * h:2 * DH * h + DH], ident[:, :])
                ins.then_inc(qkt_done, 1)

            def values_mixed(i, par, before=freed(U_MLA)):
                p = i * 2 + par
                for h in range(2):
                    if h == 0:
                        pe.wait_ge(t_free_a, p + (before + 1))
                    else:
                        pe.wait_ge(t_free_d, p + (before + 1))
                    o = ps[:, 3, 2 * DH * h:2 * DH * h + 2 * DH]
                    vh = slice(2 * DH * h + DH, 2 * DH * h + 2 * DH)
                    m.matmul(o[:, 0:DH], p_t[:, h, 0:P], kv_tok[par][:, 0, vh], start=True, stop=True)
                    m.matmul(o[:, DH:2 * DH], p_t[:, h, P:2 * P], kv_tok[par][:, 0, vh], start=True, stop=False)
                    m.matmul(o[:, DH:2 * DH], p_t[:, h, 2 * P:3 * P], kv_tok[par][:, 1, vh], start=False, stop=True).then_inc(my_done, 1)

            def scores(i, par):
                p = i * 2 + par
                pe.wait_ge(qt_ready, p * 2 + 2)
                pe.wait_ge(kt_ready, p + 1)
                for h in range(2):
                    for t in range(T):
                        o = ps[:, 6 + h, 0:P] if t == 0 else ps[:, 6 + h, P:384]
                        kc = slice(256 * h, 256 * h + P * (t + 1))
                        m.matmul(o, qn_t[:, 256 * h + P * t:256 * h + P * t + P], kn_t[:, kc], start=True, stop=False)
                        ins = m.matmul(o, qr_t[0:ROPE, 256 * h + P * t:256 * h + P * t + P], kr_t[:, 0:P * (t + 1)],
                                       start=False, stop=True)
                    ins.then_inc(sc_done, 1)

            projections(0, 0, outputs_before=False)
            operands_transposed(0, 0)
            pe.wait_ge(krt_ready, 1)
            scores(0, 0)

            def z_step(s):
                pe.wait_ge(my_ready, PAIRS * (s + 1))
                transpose_step(STEPS_Z[s], s, ys)

            def turn_of(i, par, j, first=False, last=False):
                projections(i, par, outputs_before=not first)
                weights_transposed(j, 1 - par)
                operands_transposed(i, par)
                values_mixed(j, 1 - par)
                if last:
                    z_step(0)
                scores(i, par)
                if last:
                    z_step(1)

            turn_of(0, 1, 0, first=True)
            with pe.Fori(0, PAIRS // 2 - 2) as i:
                turn_of(i + 1, 0, i)
                turn_of(i + 1, 1, i + 1)
            turn_of(PAIRS // 2 - 1, 0, PAIRS // 2 - 2)
            turn_of(PAIRS // 2 - 1, 1, PAIRS // 2 - 1, last=True)
            def last_pair(j):
                last = (PAIRS // 2 - 1, 1, freed(U_LAST) - (PAIRS - 1))
                if j == 2:
                    z_step(2)
                if j == 3:
                    weights_transposed(*last)
                if j == 4:
                    values_mixed(*last)
                if j == 5:
                    z_step(3)
                if j % 2 == 0:
                    pe.wait_ge(t_free_d, freed(STEPS_Z[j // 2]) + 2)

            out_projection(B_OUT1, C_OUT1, (last_pair, None, None, None))


_INS = ["x", "positions", "ln_even", "w_in_even", "gla_alpha_up", "gla_alpha_bias", "gla_norm", "w_out_even",
        "ln_odd", "w_in_odd", "q_norm", "w_q_up", "kv_norm", "w_kv_up", "w_out_odd", "final_norm"]


def kernel(**inputs):
    import concourse.bacc as bacc
    from concourse.bass_utils import run_bass_kernel_spmd

    nc = bacc.Bacc("TRN2", target_bir_lowering=False, num_devices=1)
    arrays, args = {}, []
    for name in _INS:
        arr = np.ascontiguousarray(inputs[name])
        arrays[f"in_{name}"] = arr
        args.append(nc.dram_tensor(f"in_{name}", arr.shape, mybir.dt.from_np(arr.dtype), kind="ExternalInput").ap())
    shape = arrays["in_x"].shape
    args.append(nc.dram_tensor("out_0", shape, F32, kind="ExternalOutput").ap())
    build(nc, *args)
    r = run_bass_kernel_spmd(nc, [arrays], core_ids=[0])
    return r.results[0]["out_0"]
```
